# Optimizing a Trainium2 kernel written in Bass

```python
import jax, jax.numpy as jnp
from jax import lax
import numpy as np

D_MODEL = 1024
BATCH = 1
SEQ = 256
DEPTH = 2

CHUNK = 64
N_MIXERS = 2
N_CONV_LAYERS = (DEPTH + 1) // 2
N_MLA_LAYERS = DEPTH // 2
D_FF = 2816
FFN_RES_WEIGHT = 0.5
CONV_WIDTH = 31
N_HEADS = 8
QK_NOPE = 128
QK_ROPE = 64
V_HEAD = 128
Q_LORA = 512
KV_LORA = 256
ROPE_THETA = 10000.0
Q_BLOCK = 128
RMS_EPS = 1e-6
POS_OFFSET_MAX = 65536


def rmsnorm(x, g):
    xf = x.astype(jnp.float32)
    y = xf * lax.rsqrt(jnp.mean(xf * xf, axis=-1, keepdims=True) + RMS_EPS) * g.astype(jnp.float32)
    return y.astype(x.dtype)

def swiglu_ffn(h, w1, w3, w2):
    return (jax.nn.silu(h @ w1) * (h @ w3)) @ w2

def conv_module(h, w_pw1, w_dw, g_norm, w_pw2):
    u = h @ w_pw1
    a, b = jnp.split(u, 2, axis=-1)
    u = a * jax.nn.sigmoid(b)
    u = lax.conv_general_dilated(
        u, w_dw[:, None, :].astype(u.dtype), window_strides=(1,),
        padding=[(CONV_WIDTH - 1, 0)],
        dimension_numbers=("NWC", "WIO", "NWC"),
        feature_group_count=D_MODEL)
    u = jax.nn.silu(rmsnorm(u, g_norm))
    return u @ w_pw2

def apply_rope(x, cos, sin):
    half = x.shape[-1] // 2
    xf = x.astype(jnp.float32)
    x1, x2 = xf[..., :half], xf[..., half:]
    out = jnp.concatenate([x1 * cos - x2 * sin, x2 * cos + x1 * sin], axis=-1)
    return out.astype(x.dtype)

def mla(h, positions, w_a, g_q, g_kv, w_uq, w_ukv, w_o):
    a = h @ w_a
    c_q = rmsnorm(a[..., :Q_LORA], g_q)
    c_kv = rmsnorm(a[..., Q_LORA:Q_LORA + KV_LORA], g_kv)
    k_rope = a[..., Q_LORA + KV_LORA:]
    q = jnp.einsum("bsc,chd->bshd", c_q, w_uq)
    q_nope, q_rope = q[..., :QK_NOPE], q[..., QK_NOPE:]
    kv = jnp.einsum("bsc,chd->bshd", c_kv, w_ukv)
    k_nope, v = kv[..., :QK_NOPE], kv[..., QK_NOPE:]

    inv_freq = ROPE_THETA ** (-2.0 * jnp.arange(QK_ROPE // 2, dtype=jnp.float32) / QK_ROPE)
    ang = positions.astype(jnp.float32)[..., None] * inv_freq
    cos, sin = jnp.cos(ang), jnp.sin(ang)
    q_rope = apply_rope(q_rope, cos[:, :, None, :], sin[:, :, None, :])
    k_rope = apply_rope(k_rope, cos, sin)

    seq = h.shape[1]
    scale = (QK_NOPE + QK_ROPE) ** -0.5
    chunk_id = jnp.arange(seq) // CHUNK
    outs = []
    for blk in range(seq // Q_BLOCK):
        q0, q1 = blk * Q_BLOCK, (blk + 1) * Q_BLOCK
        s = (jnp.einsum("bqhd,bkhd->bhqk", q_nope[:, q0:q1], k_nope[:, :q1],
                        preferred_element_type=jnp.float32)
             + jnp.einsum("bqhr,bkr->bhqk", q_rope[:, q0:q1], k_rope[:, :q1],
                          preferred_element_type=jnp.float32)) * scale
        mask = chunk_id[q0:q1, None] >= chunk_id[None, :q1]
        s = jnp.where(mask[None, None], s, -jnp.inf)
        p = jax.nn.softmax(s, axis=-1).astype(v.dtype)
        outs.append(jnp.einsum("bhqk,bkhd->bqhd", p, v[:, :q1]))
    o = jnp.concatenate(outs, axis=1)
    return o.reshape(o.shape[0], seq, N_HEADS * V_HEAD) @ w_o

def first_inputs(seed: int = 0) -> dict:
    key = jax.random.key(seed)
    ks = jax.random.split(key, 24)
    f32 = jnp.float32

    def w(k, shape, fan_in):
        return jax.random.normal(k, shape, f32) * (fan_in ** -0.5)

    def gain(k, shape):
        return 1.0 + 0.02 * jax.random.normal(k, shape, f32)

    x = jax.random.normal(ks[0], (BATCH, SEQ, D_MODEL), f32)
    offset = jax.random.randint(ks[1], (BATCH, 1), 0, POS_OFFSET_MAX, dtype=jnp.int32)
    positions = offset + jnp.arange(SEQ, dtype=jnp.int32)[None, :]
    return {
        "x": x,
        "positions": positions,
        "ffn_norm1": gain(ks[2], (DEPTH, D_MODEL)),
        "ffn1_w1": w(ks[3], (DEPTH, D_MODEL, D_FF), D_MODEL),
        "ffn1_w3": w(ks[4], (DEPTH, D_MODEL, D_FF), D_MODEL),
        "ffn1_w2": w(ks[5], (DEPTH, D_FF, D_MODEL), D_FF),
        "mix_norm": gain(ks[6], (DEPTH, D_MODEL)),
        "ffn_norm2": gain(ks[7], (DEPTH, D_MODEL)),
        "ffn2_w1": w(ks[8], (DEPTH, D_MODEL, D_FF), D_MODEL),
        "ffn2_w3": w(ks[9], (DEPTH, D_MODEL, D_FF), D_MODEL),
        "ffn2_w2": w(ks[10], (DEPTH, D_FF, D_MODEL), D_FF),
        "conv_w_pw1": w(ks[11], (N_CONV_LAYERS, D_MODEL, 2 * D_MODEL), D_MODEL),
        "conv_w_dw": w(ks[12], (N_CONV_LAYERS, CONV_WIDTH, D_MODEL), CONV_WIDTH),
        "conv_norm": gain(ks[13], (N_CONV_LAYERS, D_MODEL)),
        "conv_w_pw2": w(ks[14], (N_CONV_LAYERS, D_MODEL, D_MODEL), D_MODEL),
        "mla_w_a": w(ks[15], (N_MLA_LAYERS, D_MODEL, Q_LORA + KV_LORA + QK_ROPE), D_MODEL),
        "mla_q_norm": gain(ks[16], (N_MLA_LAYERS, Q_LORA)),
        "mla_kv_norm": gain(ks[17], (N_MLA_LAYERS, KV_LORA)),
        "mla_w_uq": w(ks[18], (N_MLA_LAYERS, Q_LORA, N_HEADS, QK_NOPE + QK_ROPE), Q_LORA),
        "mla_w_ukv": w(ks[19], (N_MLA_LAYERS, KV_LORA, N_HEADS, QK_NOPE + V_HEAD), KV_LORA),
        "mla_w_o": w(ks[20], (N_MLA_LAYERS, N_HEADS * V_HEAD, D_MODEL), N_HEADS * V_HEAD),
        "final_norm": gain(ks[21], (D_MODEL,)),
    }

def first_block(x, positions, ffn_norm1, ffn1_w1, ffn1_w3, ffn1_w2, mix_norm, ffn_norm2,
              ffn2_w1, ffn2_w3, ffn2_w2, conv_w_pw1, conv_w_dw, conv_norm, conv_w_pw2,
              mla_w_a, mla_q_norm, mla_kv_norm, mla_w_uq, mla_w_ukv, mla_w_o, final_norm):
    h = x
    for i in range(DEPTH):
        h = h + FFN_RES_WEIGHT * swiglu_ffn(rmsnorm(h, ffn_norm1[i]), ffn1_w1[i], ffn1_w3[i], ffn1_w2[i])
        m = rmsnorm(h, mix_norm[i])
        j = i // N_MIXERS
        if i % N_MIXERS == 0:
            h = h + conv_module(m, conv_w_pw1[j], conv_w_dw[j], conv_norm[j], conv_w_pw2[j])
        else:
            h = h + mla(m, positions, mla_w_a[j], mla_q_norm[j], mla_kv_norm[j],
                        mla_w_uq[j], mla_w_ukv[j], mla_w_o[j])
        h = h + FFN_RES_WEIGHT * swiglu_ffn(rmsnorm(h, ffn_norm2[i]), ffn2_w1[i], ffn2_w3[i], ffn2_w2[i])
    return rmsnorm(h, final_norm)


DEPTH_2 = 1

GRID_W = 64
CTX_LEN = 256
HG_HEADS = 4
HG_DK = 128
HG_DV = 128
HG_KEY = HG_HEADS * HG_DK
HG_VAL = HG_HEADS * HG_DV
HG_CHUNK = 64
ATT_HEADS = 8
ATT_KV_HEADS = 2
ATT_HEAD_DIM = 64
ATT_GROUPS = ATT_HEADS // ATT_KV_HEADS
ATT_Q = ATT_HEADS * ATT_HEAD_DIM
ATT_KV = ATT_KV_HEADS * ATT_HEAD_DIM
ROPE_AXIS_DIM = ATT_HEAD_DIM // 2
N_EXPERTS = 16
EC_CAPACITY_FACTOR = 2
EXPERT_FF = 1024
IN_SPLITS = (HG_KEY, HG_KEY, HG_KEY, HG_VAL, HG_VAL, ATT_Q, ATT_KV, ATT_KV, D_MODEL, D_MODEL)
IN_COLS = 3 * HG_KEY + 2 * HG_VAL + ATT_Q + 2 * ATT_KV + 2 * D_MODEL
N_MOD = 6
NORM_EPS = 1e-6


def rms_norm(x, g):
    xf = x.astype(jnp.float32)
    y = xf * lax.rsqrt(jnp.mean(xf * xf, axis=-1, keepdims=True) + NORM_EPS)
    return (y * g.astype(jnp.float32)).astype(x.dtype)

def modulate(h, shift, scale):
    return h * (1 + scale) + shift

def adaln_params(cond, w_mod, b_mod):
    m = jax.nn.silu(cond) @ w_mod + b_mod
    return jnp.split(m[..., None, :], N_MOD, axis=-1)

def axial_rope_tables(length):
    rows = length // GRID_W
    row = jnp.repeat(jnp.arange(rows, dtype=jnp.float32), GRID_W)
    col = jnp.tile(jnp.arange(GRID_W, dtype=jnp.float32), rows)
    inv_freq = ROPE_THETA ** (-jnp.arange(0, ROPE_AXIS_DIM, 2, dtype=jnp.float32) / ROPE_AXIS_DIM)
    ang = jnp.concatenate([row[:, None] * inv_freq, col[:, None] * inv_freq], axis=-1)
    return jnp.cos(ang), jnp.sin(ang)

def apply_axial_rope(x, cos, sin):
    b_, length, h_, d = x.shape
    half = ROPE_AXIS_DIM // 2
    xs = x.astype(jnp.float32).reshape(b_, length, h_, 2, ROPE_AXIS_DIM)
    x1, x2 = xs[..., :half], xs[..., half:]
    c = cos.reshape(length, 1, 2, half)
    s = sin.reshape(length, 1, 2, half)
    out = jnp.concatenate([x1 * c - x2 * s, x2 * c + x1 * s], axis=-1)
    return out.reshape(b_, length, h_, d).astype(x.dtype)

def heads(a, n):
    return a.reshape(a.shape[0], a.shape[1], n, -1)

def hgrn_gates(f_pre, lb):
    f_pre = heads(f_pre.astype(jnp.float32), HG_HEADS)
    lb = lb.reshape(HG_HEADS, HG_DK)
    log_f = jnp.log(lb + (1 - lb) * jax.nn.sigmoid(f_pre))
    key = (1 - lb) * jax.nn.sigmoid(-f_pre)
    return key, log_f

def hgrn_chunk_scan(q, k, v, log_f, s0):
    b_, length, h_, _ = q.shape
    dv = v.shape[-1]
    n_chunks = length // HG_CHUNK

    def chunks(a):
        return a.astype(jnp.float32).reshape(b_, n_chunks, HG_CHUNK, h_, a.shape[-1]).transpose(1, 0, 3, 2, 4)

    incl = jnp.tril(jnp.ones((HG_CHUNK, HG_CHUNK), dtype=bool))[:, :, None]

    def step(state, inp):
        qc, kc, vc, fc = inp
        cum = jnp.cumsum(fc, axis=2)
        rel = jnp.where(incl, cum[:, :, :, None, :] - cum[:, :, None, :, :], -jnp.inf)
        scores = jnp.einsum("bhtk,bhsk,bhtsk->bhts", qc, kc, jnp.exp(rel))
        o = (jnp.einsum("bhts,bhsv->bhtv", scores, vc)
             + jnp.einsum("bhtk,bhkv->bhtv", qc * jnp.exp(cum), state))
        last = cum[:, :, -1:, :]
        new_state = (jnp.exp(last[:, :, 0, :, None]) * state
                     + jnp.einsum("bhsk,bhsv->bhkv", kc * jnp.exp(last - cum), vc))
        return new_state, o

    s_fin, o = lax.scan(step, s0.astype(jnp.float32), tuple(chunks(a) for a in (q, k, v, log_f)))
    o = o.transpose(1, 0, 3, 2, 4).reshape(b_, length, h_, dv)
    return o.astype(v.dtype), s_fin

def hgrn_bidir(q, i, k_f, lf_f, k_b, lf_b, s_f0, s_b0):
    o_f, s_f = hgrn_chunk_scan(q, k_f, i, lf_f, s_f0)
    flip = lambda a: a[:, ::-1]
    o_b, s_b = hgrn_chunk_scan(flip(q), flip(k_b), flip(i), flip(lf_b), s_b0)
    return o_f + flip(o_b), s_f, s_b

def attend_blocks(q, k, v):
    b_, lq = q.shape[:2]
    nb = lq // Q_BLOCK
    qb = q.reshape(b_, nb, Q_BLOCK, ATT_KV_HEADS, ATT_GROUPS, ATT_HEAD_DIM).transpose(1, 0, 2, 3, 4, 5)
    scale = ATT_HEAD_DIM ** -0.5

    def one_block(qi):
        s = jnp.einsum("bqhgd,bkhd->bhgqk", qi, k, preferred_element_type=jnp.float32) * scale
        p = jax.nn.softmax(s, axis=-1)
        return jnp.einsum("bhgqk,bkhd->bqhgd", p.astype(v.dtype), v)

    o = lax.map(one_block, qb)
    return o.transpose(1, 0, 2, 3, 4, 5).reshape(b_, lq, ATT_Q)

def token_mix(hx, hc, w_in, lb_f, lb_b, hg_norm_g, q_norm_g, k_norm_g,
              w_branch_a, w_branch_b, w_out, cos, sin, ctx_out):
    split_at = np.cumsum(IN_SPLITS)[:-1].tolist()

    def project(h):
        return jnp.split(h @ w_in, split_at, axis=-1)

    def qk_norm(aq, ak):
        return rms_norm(heads(aq, ATT_HEADS), q_norm_g), rms_norm(heads(ak, ATT_KV_HEADS), k_norm_g)

    def merge(o_hg, g_hg, o_att, ga, gb):
        b_, length = g_hg.shape[:2]
        a = (rms_norm(o_hg, hg_norm_g.reshape(HG_HEADS, HG_DV)).reshape(b_, length, HG_VAL)
             * jax.nn.silu(g_hg)) @ w_branch_a
        bb = o_att @ w_branch_b
        return (jax.nn.sigmoid(ga) * a + jax.nn.sigmoid(gb) * bb) @ w_out

    cq, cff, cfb, ci, cg, caq, cak, cav, cga, cgb = project(hc)
    ckf, clf = hgrn_gates(cff, lb_f)
    ckb, clb = hgrn_gates(cfb, lb_b)
    zeros = jnp.zeros((hc.shape[0], HG_HEADS, HG_DK, HG_DV), jnp.float32)
    co, cs_f, cs_b = hgrn_bidir(heads(cq, HG_HEADS), heads(ci, HG_HEADS), ckf, clf, ckb, clb, zeros, zeros)
    cqa, cka = qk_norm(caq, cak)
    cva = heads(cav, ATT_KV_HEADS)

    xq, xff, xfb, xi, xg, xaq, xak, xav, xga, xgb = project(hx)
    xkf, xlf = hgrn_gates(xff, lb_f)
    xkb, xlb = hgrn_gates(xfb, lb_b)
    xo, _, _ = hgrn_bidir(heads(xq, HG_HEADS), heads(xi, HG_HEADS), xkf, xlf, xkb, xlb, cs_f, cs_b)
    xqa, xka = qk_norm(xaq, xak)
    xqa = apply_axial_rope(xqa, cos, sin)
    xka = apply_axial_rope(xka, cos, sin)
    keys = jnp.concatenate([cka, xka], axis=1)
    vals = jnp.concatenate([cva, heads(xav, ATT_KV_HEADS)], axis=1)
    y_x = merge(xo, xg, attend_blocks(xqa, keys, vals), xga, xgb)
    if not ctx_out:
        return y_x, None
    y_c = merge(co, cg, attend_blocks(cqa, cka, cva), cga, cgb)
    return y_x, y_c

def expert_choice_moe(h, w_router, w_gate, w_up, w_down):
    b_, length, _ = h.shape
    cap = EC_CAPACITY_FACTOR * length // N_EXPERTS
    aff = jax.nn.softmax((h @ w_router).astype(jnp.float32), axis=-1)
    gate, idx = lax.top_k(jnp.swapaxes(aff, 1, 2), cap)
    bidx = jnp.arange(b_)[:, None, None]
    xe = h[bidx, idx]
    hid = jax.nn.silu(jnp.einsum("becd,edf->becf", xe, w_gate)) * jnp.einsum("becd,edf->becf", xe, w_up)
    ye = jnp.einsum("becf,efd->becd", hid, w_down) * gate[..., None].astype(h.dtype)
    return jnp.zeros_like(h).at[bidx, idx].add(ye)

def second_inputs(seed: int = 0) -> dict:
    key = jax.random.key(seed)
    ks = jax.random.split(key, 24)
    n = jax.random.normal
    f32 = jnp.float32
    d = D_MODEL
    return {
        "x": n(ks[0], (BATCH, SEQ, d), f32),
        "c": n(ks[1], (BATCH, d), f32),
        "ctx": n(ks[2], (BATCH, CTX_LEN, d), f32),
        "c_ctx": n(ks[3], (d,), f32),
        "w_mod": n(ks[4], (DEPTH_2, d, N_MOD * d), f32) * (0.5 * d ** -0.5),
        "b_mod": n(ks[5], (DEPTH_2, N_MOD * d), f32) * 0.02,
        "norm1_g": 1.0 + 0.1 * n(ks[6], (DEPTH_2, d), f32),
        "norm2_g": 1.0 + 0.1 * n(ks[7], (DEPTH_2, d), f32),
        "w_in": n(ks[8], (DEPTH_2, d, IN_COLS), f32) * d ** -0.5,
        "hg_lb_logits": 0.5 * n(ks[9], (2, DEPTH_2 + 1, HG_KEY), f32),
        "hg_norm_g": 1.0 + 0.1 * n(ks[10], (DEPTH_2, HG_VAL), f32),
        "q_norm_g": 1.0 + 0.1 * n(ks[11], (DEPTH_2, ATT_HEAD_DIM), f32),
        "k_norm_g": 1.0 + 0.1 * n(ks[12], (DEPTH_2, ATT_HEAD_DIM), f32),
        "w_branch_a": n(ks[13], (DEPTH_2, HG_VAL, d), f32) * HG_VAL ** -0.5,
        "w_branch_b": n(ks[14], (DEPTH_2, ATT_Q, d), f32) * ATT_Q ** -0.5,
        "w_out": n(ks[15], (DEPTH_2, d, d), f32) * d ** -0.5,
        "w_router": n(ks[16], (DEPTH_2, d, N_EXPERTS), f32) * d ** -0.5,
        "w_exp_gate": n(ks[17], (DEPTH_2, N_EXPERTS, d, EXPERT_FF), f32) * d ** -0.5,
        "w_exp_up": n(ks[18], (DEPTH_2, N_EXPERTS, d, EXPERT_FF), f32) * d ** -0.5,
        "w_exp_down": n(ks[19], (DEPTH_2, N_EXPERTS, EXPERT_FF, d), f32) * EXPERT_FF ** -0.5,
        "final_norm_g": 1.0 + 0.1 * n(ks[20], (d,), f32),
    }

def second_block(x, c, ctx, c_ctx, w_mod, b_mod, norm1_g, norm2_g, w_in, hg_lb_logits, hg_norm_g,
              q_norm_g, k_norm_g, w_branch_a, w_branch_b, w_out, w_router, w_exp_gate, w_exp_up,
              w_exp_down, final_norm_g):
    cos, sin = axial_rope_tables(x.shape[1])
    lb_all = jnp.cumsum(jax.nn.softmax(hg_lb_logits.astype(jnp.float32), axis=1), axis=1)
    for l in range(DEPTH_2):
        last = l == DEPTH_2 - 1
        sh1, sc1, g1, sh2, sc2, g2 = adaln_params(c, w_mod[l], b_mod[l])
        csh1, csc1, cg1, csh2, csc2, cg2 = adaln_params(c_ctx, w_mod[l], b_mod[l])
        hx = modulate(rms_norm(x, norm1_g[l]), sh1, sc1)
        hc = modulate(rms_norm(ctx, norm1_g[l]), csh1, csc1)
        y_x, y_c = token_mix(hx, hc, w_in[l], lb_all[0, l], lb_all[1, l], hg_norm_g[l], q_norm_g[l],
                             k_norm_g[l], w_branch_a[l], w_branch_b[l], w_out[l], cos, sin, not last)
        x = x + g1 * y_x
        x = x + g2 * expert_choice_moe(modulate(rms_norm(x, norm2_g[l]), sh2, sc2),
                                       w_router[l], w_exp_gate[l], w_exp_up[l], w_exp_down[l])
        if not last:
            ctx = ctx + cg1 * y_c
            ctx = ctx + cg2 * expert_choice_moe(modulate(rms_norm(ctx, norm2_g[l]), csh2, csc2),
                                                w_router[l], w_exp_gate[l], w_exp_up[l], w_exp_down[l])
    return rms_norm(x, final_norm_g)


def setup_inputs(seed=0):
    out = dict(first_inputs(seed))
    for name, value in second_inputs(seed + 1).items():
        if name != "x":
            out[name + "_2"] = value
    return out


def reference(
    x, positions, ffn_norm1, ffn1_w1, ffn1_w3, ffn1_w2, mix_norm, ffn_norm2, ffn2_w1, ffn2_w3,
    ffn2_w2, conv_w_pw1, conv_w_dw, conv_norm, conv_w_pw2, mla_w_a, mla_q_norm, mla_kv_norm,
    mla_w_uq, mla_w_ukv, mla_w_o, final_norm, c_2, ctx_2, c_ctx_2, w_mod_2, b_mod_2, norm1_g_2,
    norm2_g_2, w_in_2, hg_lb_logits_2, hg_norm_g_2, q_norm_g_2, k_norm_g_2, w_branch_a_2,
    w_branch_b_2, w_out_2, w_router_2, w_exp_gate_2, w_exp_up_2, w_exp_down_2, final_norm_g_2,
):
    x = first_block(
        x, positions, ffn_norm1, ffn1_w1, ffn1_w3, ffn1_w2, mix_norm, ffn_norm2, ffn2_w1,
        ffn2_w3, ffn2_w2, conv_w_pw1, conv_w_dw, conv_norm, conv_w_pw2, mla_w_a, mla_q_norm,
        mla_kv_norm, mla_w_uq, mla_w_ukv, mla_w_o, final_norm,
    )
    return second_block(
        x, c_2, ctx_2, c_ctx_2, w_mod_2, b_mod_2, norm1_g_2, norm2_g_2, w_in_2, hg_lb_logits_2,
        hg_norm_g_2, q_norm_g_2, k_norm_g_2, w_branch_a_2, w_branch_b_2, w_out_2, w_router_2,
        w_exp_gate_2, w_exp_up_2, w_exp_down_2, final_norm_g_2,
    )


_drawn_inputs = setup_inputs


def setup_inputs(seed=0):
    import zlib

    import numpy as np

    out = dict(_drawn_inputs(seed))
    spreads = {}
    factors = {'ffn_norm1': 4.048,
     'mix_norm': 3.57,
     'ffn_norm2': 4.658,
     'conv_norm': 3.602,
     'mla_q_norm': 8.0,
     'mla_kv_norm': 8.0,
     'ctx_2': 4.542,
     'b_mod_2': 3.941,
     'norm2_g_2': 3.02,
     'hg_norm_g_2': 4.694,
     'q_norm_g_2': 8.0,
     'k_norm_g_2': 8.0}
    for name, (base, spread) in spreads.items():
        noise = np.random.default_rng([zlib.crc32(name.encode()), seed]).standard_normal(out[name].shape)
        drawn = base * np.exp(spread * noise) if base else spread * noise
        out[name] = __import__('jax').numpy.asarray(drawn.astype(out[name].dtype))
    for name, factor in factors.items():
        out[name] = (out[name] * factor).astype(out[name].dtype)
    return out
```

```python
from contextlib import ExitStack

import numpy as np
import concourse.bass as bass
from concourse import mybir

F32 = mybir.dt.float32
F32R = mybir.dt.float32r
I32 = mybir.dt.int32
U8 = mybir.dt.uint8
BF16 = mybir.dt.bfloat16
ALU = mybir.AluOpType
ACT = mybir.ActivationFunctionType
AX_X = mybir.AxisListType.X

P = 128
D = 1024
KD = D // P
T = 256
TT = T // P
FF = 2816
EPS = 1e-6

SLOTS = 6
SLOT = 2048
FF_CHUNK = 256
FF_STEPS = FF // FF_CHUNK

CONV_W = 31
MLA_HEADS, NOPE, ROPE, VH = 8, 128, 64, 128
Q_LORA, KV_LORA = 512, 256
MLA_SCALE = (NOPE + ROPE) ** -0.5
MASKED = -1e30
CHUNK = 64

N_MOD = 6
HG_HEADS = 4
ATT_HEADS, ATT_HD, ATT_KV = 8, 64, 2
ATT_SCALE = ATT_HD ** -0.5
EXPERTS, CAP, EFF = 16, 32, 1024
LEVELS = [64, 32, 16, 8, 4, 2, 1]
ROUND_WIDE, ROUND_DIAG = len(LEVELS), len(LEVELS) + 1
ROUNDS = len(LEVELS) + 2

STREAM = [("ffn0", 33), ("pw1", 8), ("mod", 24), ("pw2", 4), ("ffn1", 33), ("ffn2", 33), ("mla_a", 4), ("uq", 4),
          ("ukv", 2), ("mla_o", 4), ("ffn3", 33), ("w_in", 21), ("branch", 4), ("w_out", 4), ("experts", 12 * EXPERTS)]
FIRST = {}
_at = 0
for _name, _n in STREAM:
    FIRST[_name] = _at
    _at += _n

SPLIT = ("ffn0", "pw1", "pw2", "ffn1", "ffn2", "ffn3")
HALF_BUFS = 4
HALF = {}
for _name, _n in STREAM:
    if _name in SPLIT:
        for _s in range(_n):
            HALF[FIRST[_name] + _s] = 2 * len(HALF)
X_SPLITS = {name: i for i, name in enumerate(SPLIT)}
XN_HALF = {m: i + 1 for i, m in enumerate((1, 2, 3, 4, 5, 9))}

ROWS_A = {"ffn_norm1": 0, "mix_norm": 16, "ffn_norm2": 32, "conv_norm": 48, "mla_q_norm": 56, "mla_kv_norm": 60,
          "final_norm": 62}
N_ROWS_A = 70
ROWS_B = {"c_2": 0, "c_ctx_2": 8, "b_mod_2": 16, "norm1_g_2": 64, "norm2_g_2": 72, "hg_lb_logits_2": 80,
          "hg_norm_g_2": 96, "final_norm_g_2": 100}
N_ROWS_B = 108

CONST = {}


def constant_table():
    p = np.arange(P)
    parts = {
        "ident": np.eye(P),
        "ones": np.ones((P, T)),
        "headsum": (p[:, None] // ATT_HD == p[None, :] // ATT_HD),
    }

    def rotation(half):
        m = np.zeros((P, P))
        for col in range(P):
            if col % (2 * half) < half:
                m[col + half, col] = -1.0
            else:
                m[col - half, col] = 1.0
        return m

    parts["rope_rot"] = rotation(ROPE // 2)
    parts["axial_rot"] = rotation(ATT_HD // 4)
    rows = np.repeat(np.arange(T // 64, dtype=np.float32), 64)
    cols = np.tile(np.arange(64, dtype=np.float32), T // 64)
    axis_dim = ATT_HD // 2
    freq = (np.float64(10000.0) ** (-np.arange(0, axis_dim, 2) / axis_dim)).astype(np.float32)
    d = p % ATT_HD
    ang = np.where((d // axis_dim == 0)[:, None], rows[None, :], cols[None, :]).astype(np.float32)
    ang = (ang * freq[d % (axis_dim // 2)][:, None]).astype(np.float32)
    parts["axial_cos"] = np.cos(ang.astype(np.float64))
    parts["axial_sin"] = np.sin(ang.astype(np.float64))
    parts["iota"] = np.tile(np.arange(1, CAP + 1), (P, 1))
    parts["cond_sel"] = (p[:, None] % 32 == np.arange(2)[None, :])
    parts["mask_rows"] = np.tile(p < CHUNK, (P, 1))
    parts["mask_cols"] = np.tile(np.where(p < CHUNK, 0.0, MASKED), (P, 1))
    parts["inv_freq"] = (np.float64(10000.0) ** (-2.0 * (p % (ROPE // 2)) / ROPE))[:, None]
    at = 0
    for name, a in parts.items():
        CONST[name] = (at, at + a.shape[1])
        at += a.shape[1]
    return np.concatenate([np.asarray(a, np.float64).astype(np.float32) for a in parts.values()], axis=1)


def level_masks():
    s, t = np.arange(P)[:, None], np.arange(P)[None, :]
    m = [(s // (2 * h) == t // (2 * h)) & (s // h != t // h) for h in LEVELS] + [s == t]
    return np.ascontiguousarray(np.stack(m, axis=1).astype(np.int32))


CONSTANTS = constant_table()
MASKS = level_masks()
TWO_PI = 2.0 * np.pi
PI_A = 6.28125
PI_B = float(np.float32(np.round((TWO_PI - PI_A) * 2.0 ** 20) / 2.0 ** 20))
PI_C = float(np.float32(TWO_PI - PI_A - PI_B))
ROUND_MAGIC = 1.5 * 2.0 ** 23
PI_LIMIT = 3.1415925


def build(nc, x, positions, ffn_norm1, ffn1_w1, ffn1_w3, ffn1_w2, mix_norm, ffn_norm2, ffn2_w1, ffn2_w3, ffn2_w2,
          conv_w_pw1, conv_w_dw, conv_norm, conv_w_pw2, mla_w_a, mla_q_norm, mla_kv_norm, mla_w_uq, mla_w_ukv,
          mla_w_o, final_norm, c_2, ctx_2, c_ctx_2, w_mod_2, b_mod_2, norm1_g_2, norm2_g_2, w_in_2,
          hg_lb_logits_2, hg_norm_g_2, q_norm_g_2, k_norm_g_2, w_branch_a_2, w_branch_b_2, w_out_2, w_router_2,
          w_exp_gate_2, w_exp_up_2, w_exp_down_2, final_norm_g_2, constants, masks, out):
    vectors_a = {"ffn_norm1": ffn_norm1, "mix_norm": mix_norm, "ffn_norm2": ffn_norm2, "conv_norm": conv_norm,
                 "mla_q_norm": mla_q_norm, "mla_kv_norm": mla_kv_norm, "final_norm": final_norm}
    vectors_b = {"c_2": c_2, "c_ctx_2": c_ctx_2, "b_mod_2": b_mod_2, "norm1_g_2": norm1_g_2, "norm2_g_2": norm2_g_2,
                 "hg_lb_logits_2": hg_lb_logits_2, "hg_norm_g_2": hg_norm_g_2, "final_norm_g_2": final_norm_g_2}

    def as_rows(a):
        names = " ".join("abc"[:len(a.shape)])
        flat = a if len(a.shape) == 1 else a.rearrange(f"{names} -> ({names})")
        return flat.rearrange("(r f) -> r f", f=P)

    with ExitStack() as ctx:
        def sb(name, shape, dt=F32):
            return ctx.enter_context(nc.sbuf_tensor(name, shape, dt))

        sems = {}

        def sem(name):
            if name not in sems:
                sems[name] = ctx.enter_context(nc.semaphore(name))
            return sems[name]

        ps = ctx.enter_context(nc.psum_tensor("banks", [P, 8, 512], F32))

        def banks(first, n):
            return ps[:, first:first + n, :].rearrange("p b c -> p (b c)")

        ring = sb("ring", [P, SLOTS, SLOT])
        h = sb("h", [P, KD, T])
        xn = sb("xn", [P, KD, 2 * T])
        squares = sb("squares", [P, KD, 2 * T])
        std = sb("std", [P, 2 * T])
        rstd = sb("rstd", [P, 2 * T])
        consts = sb("consts", [P, CONSTANTS.shape[1]])
        mask = sb("mask", [P, len(LEVELS) + 1, P], U8)
        vec_a = sb("vec_a", [P, N_ROWS_A])
        vec_b = sb("vec_b", [P, N_ROWS_B])
        qk_gain = sb("qk_gain", [P, 2])
        w_dw = sb("w_dw", [P, KD, CONV_W])
        mod = sb("mod", [P, N_MOD * KD, 2])
        gain_mod = sb("gain_mod", [P, 3, KD])
        tok = sb("tok", [P, TT, D])
        silu_gate = sb("silu_gate", [P, 2, 512])
        hidden = sb("hidden", [P, 2, 2, T])
        small = sb("small", [P, 64])
        router = sb("router", [P, KD, EXPERTS])
        pos_i = sb("pos_i", [P, T], I32)
        zero_w = sb("zero_w", [P, 512], BF16)
        eps_col = sb("eps_col", [P, 1])
        lb_tmp = sb("lb_tmp", [P, 3, 2, HG_HEADS])
        floor = sb("floor", [P, 2, 2, HG_HEADS])
        mla_stat = sb("mla_stat", [P, 4, MLA_HEADS, TT])
        att_stat = sb("att_stat", [P, 4, ATT_HEADS * TT])
        ARENA = 22100
        arena_at = -(-nc.sbuf_base // 32) * 32
        arena = sb("arena", [P, ARENA])
        LOW = (ARENA - HALF_BUFS * SLOT - 2 * KD * T - 8 * T) // 8 * 8

        def split_tensor(name, shape, first):
            return nc.alloc_sbuf_tensor_at(name, shape, F32R, offset=arena_at + 4 * first)

        w_split = split_tensor("w_split", [P, HALF_BUFS, 2, SLOT // 2], LOW)
        x_split = split_tensor("x_split", [P, 2, KD, T], LOW + HALF_BUFS * SLOT)
        hid_split = split_tensor("hid_split", [P, 2, 2, 2, T], LOW + HALF_BUFS * SLOT + 2 * KD * T)

        def const(name, rows=P):
            a, b = CONST[name]
            return consts[0:rows, a:b]

        ident, ones = const("ident"), const("ones")

        class Region:
            def __init__(self):
                self.at = 0

            def take(self, *shape, rows=P):
                n = int(np.prod(shape))
                view = arena[0:rows, self.at:self.at + n]
                self.at += n
                assert self.at <= ARENA, self.at
                names = [f"d{i}" for i in range(len(shape))]
                if len(shape) > 1:
                    sizes = dict(zip(names, shape))
                    view = view.rearrange(f"p ({' '.join(names)}) -> p {' '.join(names)}", **sizes)
                return view

        r0 = Region()
        rows_a, rows_b, rows_dw = r0.take(P, rows=N_ROWS_A), r0.take(P, rows=N_ROWS_B), r0.take(D, rows=CONV_W)
        mask_in = r0.take(len(LEVELS) + 1, P).bitcast(I32)
        r1 = Region()
        PAD = CONV_W - 1
        conv_in, conv_acc, glu_sig = r1.take(KD, PAD + T), r1.take(KD, T), r1.take(2, 2 * T)
        cond_pad, mod_rows = r1.take(KD, 32), r1.take(2, 512)
        assert max(r0.at, r1.at) <= LOW
        r2 = Region()
        latent, latent_n = r2.take(6, T), r2.take(6, T)
        q_nope, k_nope = r2.take(MLA_HEADS, T), r2.take(MLA_HEADS, T)
        rope_in, rope_a, rope_b = r2.take(5, T), r2.take(5, T), r2.take(5, T)
        v_tok, o_mla = r2.take(TT, MLA_HEADS, VH), r2.take(MLA_HEADS, T)
        mla_p, mla_pt = r2.take(2, 384), r2.take(2, 3, P)
        cos_t, sin_t, ang, turns, pos_f = (r2.take(T) for _ in range(5))
        r3 = Region()
        hg_q = r3.take(HG_HEADS, T)
        key_f, key_b = r3.take(HG_HEADS, 2 * T), r3.take(HG_HEADS, 2 * T)
        log_f, log_b = r3.take(HG_HEADS, 2 * T), r3.take(HG_HEADS, 2 * T)
        hg_v = r3.take(4, 512)
        att_q, att_k = r3.take(4, T), r3.take(ATT_KV, 2 * T)
        att_v = r3.take(4, P)
        gate_a, gate_b = r3.take(KD, T), r3.take(KD, T)
        pre_x, pre_c = r3.take(2, HG_HEADS, T + 1), r3.take(2, HG_HEADS, T + 1)
        hg_gate = silu_gate[:, :, :].rearrange("p a (b t) -> p (a b) t", t=T)
        state0 = hidden[:, :, :, :].rearrange("p a b t -> p (a b t)").rearrange("p (d h v) -> p d h v", d=2, h=HG_HEADS)
        decay = squares[:, :, :].rearrange("p k t -> p (k t)").rearrange("p (r d h t) -> p r d h t", r=2, d=2, h=HG_HEADS)
        q_lvl = log_f.rearrange("p a t -> p (a t)").rearrange("p (r h t) -> p r h t", r=2, h=HG_HEADS)
        k_lvl = log_b.rearrange("p a t -> p (a t)").rearrange("p (r h t) -> p r h t", r=2, h=HG_HEADS)
        hg_p = tok[:, :, :].rearrange("p s (h t) -> p s h t", h=HG_HEADS)
        key_dec = xn[:, 0:4, :].rearrange("p k t -> p (k t)").rearrange("p (d h t) -> p d h t", d=2, h=HG_HEADS)
        key_dec_t = xn[:, 4:8, :].rearrange("p k t -> p (k t)").rearrange("p (d s c) -> p d s c", d=2, s=TT)
        q_dec = decay[:, 0]
        o_sq = decay[:, 1, 0]
        o_hg = decay[:, 1, 1]
        att_rot = q_lvl.rearrange("p r h t -> p (r h t)")
        att_sq = k_lvl.rearrange("p r h t -> p (r h t)")
        att_qr = key_f.rearrange("p a t -> p (a t)")[:, 0:4 * T].rearrange("p (a t) -> p a t", t=T)
        att_kr = key_f.rearrange("p a t -> p (a t)")[:, 4 * T:8 * T].rearrange("p (a t) -> p a t", t=2 * T)
        att_p = key_b.rearrange("p a t -> p (a t)")[:, 0:1024].rearrange("p (r k) -> p r k", r=2)
        att_pt = key_b.rearrange("p a t -> p (a t)")[:, 1024:2048].rearrange("p (r k q) -> p r k q", r=2, k=4)
        att_rinv = pre_c.rearrange("p d h t -> p (d h t)")[:, 0:2048]
        o_att = hg_q
        merged = xn[:, :, 0:T]
        r4 = Region()
        x_exp = xn
        pick, pick_gate = r4.take(TT, EXPERTS * CAP), r4.take(TT, EXPERTS * CAP)
        spread = squares[0:64, :, :].rearrange("p k t -> p (k t)").rearrange("p (e t) -> p e t", t=T)
        x_cur, spread_cur = r4.take(2, KD, CAP), r4.take(2, T)
        half_g, half_u, half_y, gate_act = r4.take(512), r4.take(512), r4.take(512), r4.take(512)
        gate_sum, up_sum, hid_e, y_e = r4.take(512), r4.take(512), r4.take(512), r4.take(512)
        hid_t = r4.take(KD, CAP)
        aff, aff_e = r4.take(TT, EXPERTS), r4.take(TT, EXPERTS)
        aff_t, work_a, work_b, chosen, slot_t = (r4.take(T) for _ in range(5))
        slot_tok = r4.take(TT, EXPERTS)
        top8 = r4.take(8)

        slot_full = [sem(f"slot_full_{i}") for i in range(SLOTS)]
        slot_free = sem("slot_free")
        half_done = sem("half_done")

        def wait_free(sp, n, more=0):
            if n >= SLOTS:
                sp.wait_ge(slot_free, n - SLOTS + 1 + more)

        def wait_full(pe, n, more=0):
            pe.wait_ge(slot_full[n % SLOTS], 16 * (n // SLOTS + 1) + more)

        def wait_done(eng, n, more=0):
            if n in HALF:
                eng.wait_ge(half_done, HALF[n] + 2 + more)
            else:
                eng.wait_ge(slot_free, n + 1 + more)

        def slot(n):
            return ring[:, n % SLOTS, :]

        def half_slot(n, o, columns):
            if columns:
                return slot(n).rearrange("p (k c) -> p k c", k=KD)[:, :, o * P:o * P + P]
            return slot(n)[:, o * D:o * D + D].rearrange("p (k c) -> p k c", k=KD)

        def half_part(n, o, part):
            return w_split[:, (HALF[n] + o) % HALF_BUFS, part, :].rearrange("p (k c) -> p k c", k=KD)

        w_ffn = [(ffn1_w1[0], ffn1_w3[0], ffn1_w2[0]), (ffn2_w1[0], ffn2_w3[0], ffn2_w2[0]),
                 (ffn1_w1[1], ffn1_w3[1], ffn1_w2[1]), (ffn2_w1[1], ffn2_w3[1], ffn2_w2[1])]

        PROJ = [("q", 0), ("q", 1), ("ff", 2), ("ff", 3), ("fb", 4), ("fb", 5), ("i", 6), ("i", 7), ("g", 8), ("g", 9),
                ("aq", 10), ("aq", 11), ("ak", 12), ("av", 12)] + [("ga", 13 + i) for i in range(4)] + \
               [("gb", 17 + i) for i in range(4)]
        ROUND_AT = 8
        PAIRS = 3

        block = ctx.enter_context(nc.Block())

        @block.sync
        def _(sp):
            def load(n, src, view, more=0):
                wait_free(sp, n, more)
                sp.dma_start(view, src).then_inc(slot_full[n % SLOTS], 16)

            def cols(n, w, first, width, k_tiles):
                load(n, w.rearrange("(k p) c -> p k c", p=P)[:, :, first:first + width],
                     slot(n)[:, 0:k_tiles * width].rearrange("p (k c) -> p k c", k=k_tiles))

            sp.dma_start(consts[:, :], constants).then_inc(sem("consts_in"), 16)
            sp.dma_start(tok[:, :, :], x[0].rearrange("(t p) d -> p t d", p=P)).then_inc(sem("x_in"), 16)
            def ffn(f):
                n0 = FIRST[f"ffn{f}"]
                w1, w3, w2 = w_ffn[f]

                def up(n, w, c, more):
                    wait_free(sp, n, more)
                    src = w.rearrange("(k p) (s c) -> s p k c", p=P, c=FF_CHUNK)[bass.ds(c, 1)]
                    sp.dma_start(slot(n).rearrange("p (k c) -> p k c", k=KD),
                                 src.rearrange("o p k c -> p (o k) c")).then_inc(slot_full[n % SLOTS], 16)

                def down(n, c, more):
                    wait_free(sp, n, more)
                    src = w2.rearrange("(s k p) c -> s p k c", p=P, k=2)[bass.ds(c, 1)]
                    sp.dma_start(slot(n).rearrange("p (k c) -> p k c", k=2),
                                 src.rearrange("o p k c -> p (o k) c")).then_inc(slot_full[n % SLOTS], 16)

                up(n0, w1, 0, 0)
                up(n0 + 1, w3, 0, 0)
                first = 2 if f == 0 else 0
                for c in range(first):
                    n = n0 + 2 + 3 * c
                    up(n, w1, c + 1, 0)
                    up(n + 1, w3, c + 1, 0)
                    down(n + 2, c, 0)
                with sp.Fori(0, (FF_STEPS - 1 - first) // 2) as i:
                    for j in range(first, first + 2):
                        n = n0 + 2 + 3 * j
                        up(n, w1, 2 * i + (1 + j), 6 * i)
                        up(n + 1, w3, 2 * i + (1 + j), 6 * i)
                        down(n + 2, 2 * i + j, 6 * i)
                down(n0 + 32, FF_STEPS - 1, 0)

            ffn(0)
            for j in range(KD):
                cols(FIRST["pw1"] + j, conv_w_pw1[0], D * (j % 2) + 256 * (j // 2), 256, KD)
            for c in range(12):
                for half in range(2):
                    n = FIRST["mod"] + 2 * c + half
                    load(n, w_mod_2[0].rearrange("(k p) c -> p k c", p=P)[:, 4 * half:4 * half + 4, 512 * c:512 * c + 512],
                         slot(n).rearrange("p (k c) -> p k c", k=4))
            for j in range(4):
                cols(FIRST["pw2"] + j, conv_w_pw2[0], 256 * j, 256, KD)
            ffn(1)
            ffn(2)
            for j in range(4):
                cols(FIRST["mla_a"] + j, mla_w_a[0], 256 * j, 256 if j < 3 else ROPE, KD)
            for j in range(4):
                cols(FIRST["uq"] + j, mla_w_uq[0].rearrange("c h d -> c (h d)"), 384 * j, 384, 4)
            for j in range(2):
                cols(FIRST["ukv"] + j, mla_w_ukv[0].rearrange("c h d -> c (h d)"), 1024 * j, 1024, 2)
            for j in range(4):
                cols(FIRST["mla_o"] + j, mla_w_o[0], 256 * j, 256, KD)
            ffn(3)
            for j in range(21):
                cols(FIRST["w_in"] + j, w_in_2[0], 256 * j, 256, KD)
            for j in range(2):
                cols(FIRST["branch"] + j, w_branch_a_2[0], 512 * j, 512, 4)
            for j in range(2):
                cols(FIRST["branch"] + 2 + j, w_branch_b_2[0], 512 * j, 512, 4)
            for j in range(4):
                cols(FIRST["w_out"] + j, w_out_2[0], 256 * j, 256, KD)
            with sp.Fori(0, EXPERTS) as e:
                for m, w in enumerate((w_exp_gate_2, w_exp_up_2, w_exp_down_2)):
                    for j in range(4):
                        n = FIRST["experts"] + 4 * m + j
                        wait_free(sp, n, 12 * e)
                        src = w[0].rearrange("e (j k p) c -> j e p k c", p=P, k=2)[j][bass.ds(e, 1)]
                        sp.dma_start(slot(n).rearrange("p (k c) -> p k c", k=2),
                                     src.rearrange("o p k c -> p (o k) c")).then_inc(slot_full[n % SLOTS], 16)
            for t in range(TT):
                sp.wait_ge(sem("rows_out"), 2 * t + 2)
                sp.dma_start(out[0].rearrange("(t p) d -> t p d", p=P)[t], tok[:, t, :]).then_inc(sem("stored"), 16)
            sp.wait_ge(sem("stored"), 16 * TT)

        @block.tensor
        def _(pe):
            mm = pe.matmul

            def done(ins):
                ins.then_inc(slot_free, 1)

            def wait_split(n, o, more_slots=0):
                if o == 0:
                    pe.wait_ge(sem("half_split"), HALF[n] // 2 + 1 + more_slots)
                else:
                    pe.wait_ge(slot_free, n + 1 + more_slots)

            def mm3(out_, n, o, k, moving, start, stop, **kw):
                hi, lo = half_part(n, o, 0)[:, k, :], half_part(n, o, 1)[:, k, :]
                mm(out_, hi, moving(0), start=start, stop=False, **kw)
                mm(out_, hi, moving(1), start=False, stop=False, **kw)
                return mm(out_, lo, moving(0), start=False, stop=stop, **kw)

            def wait_x(name):
                pe.wait_ge(sem("x_split_ready"), 2 * X_SPLITS[name] + 2)

            pe.wait_ge(sem("consts_in"), 16)
            pe.wait_ge(sem("x_in"), 16)
            for k in range(KD):
                for t in range(TT):
                    last = pe.transpose(ps[:, 2 + k // 2, (k % 2) * T + t * P:(k % 2) * T + t * P + P],
                                        tok[:, t, k * P:k * P + P], ident)
            last.then_inc(sem("x_turned"), 1)
            pe.wait_ge(sem("rows_in"), 16 * (len(ROWS_A) + len(ROWS_B) + 1))
            pe.transpose(ps[:, 0, 0:N_ROWS_A], rows_a, ident[0:N_ROWS_A, 0:N_ROWS_A])
            pe.transpose(ps[:, 1, 0:N_ROWS_B], rows_b, ident[0:N_ROWS_B, 0:N_ROWS_B])
            for k in range(KD):
                last = pe.transpose(ps[:, 6, k * CONV_W:(k + 1) * CONV_W], rows_dw[:, k * P:k * P + P],
                                    ident[0:CONV_W, 0:CONV_W])
            last.then_inc(sem("rows_turned"), 1)

            def sum_squares(m, k_tiles, n, bank, first=0):
                pe.wait_ge(sem("squares_ready"), m)
                for k in range(k_tiles):
                    last = mm(ps[:, bank, 0:n], ones[:, 0:P], squares[:, first + k, 0:n],
                              start=(k == 0), stop=(k == k_tiles - 1))
                last.then_inc(sem("sumsq_ready"), 1)

            x_in = xn[:, :, T:2 * T]

            def ffn(f, norm):
                n0 = FIRST[f"ffn{f}"]
                steps = FF_STEPS * f
                sum_squares(norm, KD, T, 4)
                for b in range(4):
                    mm(banks(b, 1), zero_w[:, 0:P], zero_w[:, :], start=True, stop=False, skip_group_check=True)

                def up(n, bank, more):
                    for o in range(2):
                        wait_split(n, o, more)
                        for k in range(KD):
                            last = mm3(ps[:, bank, o * T:o * T + T], n, o, k, lambda part: x_split[:, part, k, :],
                                       start=(k == 0), stop=(k == KD - 1))
                        last.then_inc(half_done, 1)

                def down(n, c, more_slot, more):
                    pe.wait_ge(sem("hid_split_ready"), steps + c + 1 + more)
                    for o in range(2):
                        wait_split(n, o, more_slot)
                        for d in range(KD):
                            last = mm3(ps[:, d // 2, (d % 2) * T:(d % 2) * T + T], n, o, d,
                                       lambda part: hid_split[:, c % 2, part, o, :],
                                       start=False, stop=False, skip_group_check=True)
                        last.then_inc(half_done, 1)

                wait_x(f"ffn{f}")
                up(n0, 4, 0)
                up(n0 + 1, 6, 0)
                with pe.Fori(0, FF_STEPS // 2) as i:
                    for j in range(2):
                        n = n0 + 2 + 3 * j
                        b = 4 + (1 + j) % 2
                        up(n, b, 6 * i)
                        up(n + 1, b + 2, 6 * i)
                        down(n + 2, j, 6 * i, 2 * i)
                down(n0 + 32, FF_STEPS - 1, 0, 0)

            def split_product(n, bank):
                for o in range(2):
                    wait_split(n, o)
                    for k in range(KD):
                        last = mm3(ps[:, bank, o * T:o * T + T], n, o, k, lambda part: x_split[:, part, k, :],
                                   start=(k == 0), stop=(k == KD - 1))
                    last.then_inc(half_done, 1)

            def square_product(name, n_slots, src, bank0=0, k_tiles=KD, half_cols=256):
                for j in range(n_slots):
                    n = FIRST[name] + j
                    wait_full(pe, n)
                    per = half_cols // P
                    for o in range(per):
                        tile = j * per + o
                        for k in range(k_tiles):
                            last = mm(ps[:, bank0 + tile // 2, (tile % 2) * T:(tile % 2) * T + T],
                                      slot(n)[:, k * half_cols + o * P:k * half_cols + o * P + P], src[:, k, :],
                                      start=(k == 0), stop=(k == k_tiles - 1))
                    done(last)

            pe.wait_ge(sem("vectors_ready"), 1)
            ffn(0, 1)

            sum_squares(2, KD, T, 4)
            wait_x("pw1")
            for j in range(KD):
                n = FIRST["pw1"] + j
                if j >= 4 and j % 2 == 0:
                    pe.wait_ge(sem("glu_ready"), j // 2 - 1)
                split_product(n, j % 4)
            def turn_mod(c):
                pe.wait_ge(sem("mod_copied"), c + 1)
                for b in range(4):
                    last = mm(ps[:, 7, 2 * (4 * c + b):2 * (4 * c + b) + 2], mod_rows[:, c % 2, P * b:P * b + P],
                              const("cond_sel"), start=True, stop=True)
                last.then_inc(sem("mod_turned"), 1)

            pe.wait_ge(sem("cond_ready"), 1)
            for c in range(12):
                if c >= 2:
                    pe.wait_ge(sem("mod_copied"), c - 1)
                for half in range(2):
                    n = FIRST["mod"] + 2 * c + half
                    wait_full(pe, n)
                    for j in range(4):
                        last = mm(ps[32 * j:32 * j + 32, 5 + c % 2, :], cond_pad[:, 4 * half + j, :],
                                  slot(n)[:, 512 * j:512 * j + 512], start=(half == 0), stop=(half == 1))
                    done(last)
                if c >= 1:
                    turn_mod(c - 1)
            turn_mod(11)

            sum_squares(3, KD, T, 4)
            wait_x("pw2")
            for j in range(4):
                split_product(FIRST["pw2"] + j, j)

            pe.wait_ge(sem("mod_ready"), 3)
            ffn(1, 4)
            ffn(2, 5)

            sum_squares(6, KD, T, 4)
            pe.wait_ge(sem("xn_ready"), 6)
            for j in range(4):
                n = FIRST["mla_a"] + j
                wait_full(pe, n)
                for o in range(2):
                    for k in range(KD):
                        if j < 3:
                            last = mm(ps[:, j, o * T:o * T + T], slot(n)[:, k * 256 + o * P:k * 256 + o * P + P],
                                      x_in[:, k, :], start=(k == 0), stop=(k == KD - 1))
                        else:
                            last = mm(ps[64 * o:64 * o + 64, j, 0:T], slot(n)[:, k * ROPE:k * ROPE + ROPE],
                                      x_in[:, k, :], start=(k == 0), stop=(k == KD - 1))
                done(last)
            sum_squares(7, 4, T, 4)
            sum_squares(8, 2, T, 7, 4)
            pe.wait_ge(sem("xn_ready"), 8)
            for j in range(4):
                n = FIRST["uq"] + j
                wait_full(pe, n)
                if j >= 2:
                    pe.wait_ge(sem("uq_taken"), j - 1)
                b = 5 if j % 2 == 0 else 0
                for o in range(2):
                    for k in range(4):
                        mm(ps[:, b, o * T:o * T + T], slot(n)[:, k * 384 + 192 * o:k * 384 + 192 * o + P],
                           latent_n[:, k, :], start=(k == 0), stop=(k == 3))
                for k in range(4):
                    for o in range(2):
                        c = k * 384 + 192 * o + NOPE
                        last = mm(ps[64 * o:64 * o + 64, b + 1, 0:T], slot(n)[:, c:c + ROPE], latent_n[:, k, :],
                                  start=(k == 0), stop=(k == 3))
                done(last)
            pe.wait_ge(sem("uq_taken"), 4)
            for j in range(2):
                n = FIRST["ukv"] + j
                wait_full(pe, n)
                if j == 1:
                    pe.wait_ge(sem("ukv_taken"), 1)
                for o in range(4):
                    for k in range(2):
                        mm(ps[:, o // 2, (o % 2) * T:(o % 2) * T + T], slot(n)[:, k * D + 256 * o:k * D + 256 * o + P],
                           latent_n[:, 4 + k, :], start=(k == 0), stop=(k == 1))
                for t in range(TT):
                    for k in range(2):
                        w = slot(n)[:, k * D:(k + 1) * D].rearrange("p (o c) -> p o c", o=4)[:, :, NOPE:NOPE + VH]
                        last = mm(ps[:, 2 + t, :], latent_n[:, 4 + k, t * P:t * P + P], w, start=(k == 0), stop=(k == 1))
                done(last)
            flat = rope_in.rearrange("p a t -> p (a t)")
            for c, (a, b) in enumerate(((0, 512), (512, 1024), (1024, 1280))):
                last = mm(ps[:, 5 + c, 0:b - a], const("rope_rot"), flat[:, a:b], start=True, stop=True)
            last.then_inc(sem("rope_turned"), 1)
            pe.wait_ge(sem("ukv_taken"), 2)
            pe.wait_ge(sem("rope_ready"), 1)

            def mla_scores(hd):
                if hd >= 2:
                    pe.wait_ge(sem("mla_exp"), 2 * (hd - 1))
                base = 64 * (hd % 2)
                for t in range(TT):
                    o = ps[:, hd % 2, P * t:P * t + P * (t + 1)]
                    keys = P * (t + 1)
                    mm(o, q_nope[:, hd, t * P:t * P + P], k_nope[:, hd, 0:keys], start=True, stop=False)
                    mm(o, rope_a[base:base + 64, hd // 2, t * P:t * P + P], rope_a[base:base + 64, 4, 0:keys],
                       start=False, stop=False)
                    last = mm(ps[:, hd % 2, 2 * t * P:2 * t * P + P],
                              const("mask_rows", 1), const("mask_cols", 1), start=False, stop=True)
                last.then_inc(sem("mla_scores"), 1)

            def mla_turn(hd):
                pe.wait_ge(sem("mla_p"), hd + 1)
                if hd >= 2:
                    pe.wait_ge(sem("mla_pt"), hd - 1)
                for b in range(3):
                    last = pe.transpose(ps[:, 2 + hd % 2, b * P:b * P + P], mla_p[:, hd % 2, b * P:b * P + P], ident)
                last.then_inc(sem("mla_turned"), 1)

            def mla_values(hd):
                pe.wait_ge(sem("mla_pt"), hd + 1)
                if hd >= 2:
                    pe.wait_ge(sem("mla_out_taken"), hd - 1)
                mm(ps[:, 4 + hd % 2, 0:T], v_tok[:, 0, hd, :],
                   mla_pt[:, hd % 2, 0:2, :].rearrange("p b q -> p (b q)"), start=True, stop=False)
                last = mm(ps[:, 4 + hd % 2, P:T], v_tok[:, 1, hd, :], mla_pt[:, hd % 2, 2, :], start=False, stop=True)
                last.then_inc(sem("mla_out"), 1)

            for i in range(MLA_HEADS + 2):
                if i < MLA_HEADS:
                    mla_scores(i)
                if 1 <= i <= MLA_HEADS:
                    mla_turn(i - 1)
                if i >= 2:
                    mla_values(i - 2)
            pe.wait_ge(sem("mla_out_taken"), MLA_HEADS)
            square_product("mla_o", 4, o_mla)

            ffn(3, 9)

            pe.wait_ge(sem("ctx_in"), 16)
            pe.wait_ge(sem("h_updated"), 6)
            for k in range(KD):
                for t in range(TT):
                    last = pe.transpose(ps[:, k // 2, (k % 2) * T + t * P:(k % 2) * T + t * P + P],
                                        tok[:, t, k * P:k * P + P], ident)
            last.then_inc(sem("ctx_turned"), 1)
            sum_squares(10, KD, T, 4)
            sum_squares(11, KD, T, 5)
            sum_squares(12, KD, T, 6)
            pe.wait_ge(sem("modulated"), 2)

            def hg_round(r):
                pe.wait_ge(sem("round_ready"), r + 1)
                if r >= 1:
                    pe.wait_ge(sem("round_taken"), r)
                for s in range(TT):
                    t = 1 - s if r == ROUND_WIDE else s
                    for hd in range(HG_HEADS):
                        q = hg_q if r == ROUND_DIAG else q_lvl[:, r % 2]
                        last = mm(ps[:, 6 + s, hd * P:hd * P + P], k_lvl[:, r % 2, hd, s * P:s * P + P],
                                  q[:, hd, t * P:t * P + P], start=True, stop=True)
                last.then_inc(sem("round_scores"), 1)

            for step, (name, s) in enumerate(PROJ):
                n = FIRST["w_in"] + s
                b = 2 * (step % PAIRS)
                wait_full(pe, n)
                if step >= PAIRS:
                    pe.wait_ge(sem("proj_taken"), step - PAIRS + 1)
                if name in ("ff", "fb"):
                    for o in range(2):
                        for k in range(KD):
                            last = mm(ps[:, b + o, :], slot(n)[:, k * 256 + o * P:k * 256 + o * P + P], xn[:, k, :],
                                      start=(k == 0), stop=(k == KD - 1))
                elif name == "i":
                    for t in range(4):
                        for k in range(KD):
                            last = mm(ps[:, b + t // 2, (t % 2) * T:(t % 2) * T + T], xn[:, k, t * P:t * P + P],
                                      slot(n)[:, k * 256:k * 256 + 256], start=(k == 0), stop=(k == KD - 1))
                elif name == "ak":
                    for o in range(ATT_KV):
                        for k in range(KD):
                            for half in range(2):
                                c = k * 256 + o * ATT_HD
                                last = mm(ps[64 * half:64 * half + 64, b + o, :], slot(n)[:, c:c + ATT_HD], xn[:, k, :],
                                          start=(k == 0), stop=(k == KD - 1))
                elif name == "av":
                    for t in range(4):
                        for k in range(KD):
                            last = mm(ps[:, b, t * P:t * P + P], xn[:, k, t * P:t * P + P],
                                      slot(n)[:, k * 256 + P:k * 256 + 256], start=(k == 0), stop=(k == KD - 1))
                else:
                    for o in range(2):
                        for k in range(KD):
                            last = mm(ps[:, b, o * T:o * T + T], slot(n)[:, k * 256 + o * P:k * 256 + o * P + P],
                                      x_in[:, k, :], start=(k == 0), stop=(k == KD - 1))
                if name == "ak":
                    last.then_inc(sem("ak_product"), 1)
                else:
                    done(last)
                if step >= ROUND_AT and step - ROUND_AT < ROUNDS:
                    hg_round(step - ROUND_AT)

            pe.wait_ge(sem("key_dec_ready"), 1)
            pe.wait_ge(sem("proj_taken"), len(PROJ))
            for dr in range(2):
                for s in range(TT):
                    for hd in range(HG_HEADS):
                        last = pe.transpose(ps[:, 2 * dr + s, hd * P:hd * P + P], key_dec[:, dr, hd, s * P:s * P + P], ident)
            last.then_inc(sem("key_dec_turned"), 1)
            pe.wait_ge(sem("key_dec_t_ready"), 1)
            for dr in range(2):
                for hd in range(HG_HEADS):
                    for s in range(TT):
                        last = mm(ps[:, 4 + dr, hd * P:hd * P + P], key_dec_t[:, dr, s, hd * P:hd * P + P],
                                  hg_v[:, s, hd * P:hd * P + P], start=(s == 0), stop=(s == TT - 1))
            last.then_inc(sem("state_product"), 1)
            pe.wait_ge(sem("state_ready"), 1)
            pe.wait_ge(sem("round_taken"), ROUNDS)
            pe.wait_ge(sem("q_dec_ready"), 1)
            for hd in range(HG_HEADS):
                o = ps[:, hd // 2, (hd % 2) * T:(hd % 2) * T + T]
                for s in range(TT):
                    mm(o, hg_v[:, TT + s, hd * P:hd * P + P], hg_p[:, s, hd, :], start=(s == 0), stop=False)
                for dr in range(2):
                    last = mm(o, state0[:, dr, hd, :], q_dec[:, dr, hd, :], start=False, stop=(dr == 1))
            last.then_inc(sem("hg_out"), 1)
            pe.wait_ge(sem("hg_sq_ready"), 1)
            for c in range(2):
                last = mm(ps[:, 2 + c, :], ones[:, 0:P], o_sq[:, 2 * c:2 * c + 2, :].rearrange("p a t -> p (a t)"),
                          start=True, stop=True)
            last.then_inc(sem("hg_sumsq"), 1)

            pe.wait_ge(sem("att_sq_ready"), 1)
            for c in range(2):
                mm(ps[:, 4 + c, :], const("headsum"), att_sq[:, 512 * c:512 * c + 512], start=True, stop=True)
            pe.wait_ge(sem("round_taken"), ROUNDS)
            for c in range(2):
                last = mm(ps[:, 6 + c, :], const("headsum"), att_sq[:, 1024 + 512 * c:1536 + 512 * c], start=True, stop=True)
            last.then_inc(sem("att_sumsq"), 1)
            pe.wait_ge(sem("att_n_ready"), 1)
            qf = att_qr.rearrange("p a t -> p (a t)")
            for c in range(2):
                mm(ps[:, 4 + c, :], const("axial_rot"), qf[:, 512 * c:512 * c + 512], start=True, stop=True)
            for o in range(ATT_KV):
                last = mm(ps[:, 6, o * T:o * T + T], const("axial_rot"), att_kr[:, o, T:2 * T], start=True, stop=True)
            last.then_inc(sem("att_turned"), 1)
            pe.wait_ge(sem("att_ready"), 1)
            pe.wait_ge(sem("hg_normed"), 1)
            units = [(hd, t) for hd in range(ATT_HEADS) for t in range(TT)]

            def att_scores(u):
                hd, t = units[u]
                base = 64 * (hd % 2)
                if u >= 2:
                    pe.wait_ge(sem("att_exp"), u - 1)
                mm(ps[:, u % 2, :], att_qr[base:base + 64, hd // 2, t * P:t * P + P], att_kr[base:base + 64, hd // 4, :],
                   start=True, stop=True).then_inc(sem("att_scores"), 1)

            def att_turn(u):
                pe.wait_ge(sem("att_p"), u + 1)
                if u >= 2:
                    pe.wait_ge(sem("att_pt"), u - 1)
                for b in range(4):
                    last = pe.transpose(ps[:, 2 + u % 2, b * P:b * P + P], att_p[:, u % 2, b * P:b * P + P], ident)
                last.then_inc(sem("att_p_turned"), 1)

            def att_values(u):
                hd, t = units[u]
                base = 64 * (hd % 2)
                pe.wait_ge(sem("att_pt"), u + 1)
                pair = hd // 2
                for b in range(4):
                    last = mm(ps[base:base + 64, 4 + pair // 2, (pair % 2) * T + t * P:(pair % 2) * T + t * P + P],
                              att_v[:, b, (hd // 4) * ATT_HD:(hd // 4) * ATT_HD + ATT_HD], att_pt[:, u % 2, b, :],
                              start=(b == 0), stop=(b == 3))
                last.then_inc(sem("att_out"), 1)

            for i in range(len(units) + 2):
                if i < len(units):
                    att_scores(i)
                if 1 <= i <= len(units):
                    att_turn(i - 1)
                if i >= 2:
                    att_values(i - 2)

            pe.wait_ge(sem("att_exp"), len(units))
            pe.wait_ge(sem("att_pt"), len(units))
            for br, src in ((0, o_hg), (1, o_att)):
                if br == 1:
                    pe.wait_ge(sem("o_att_ready"), 1)
                for j in range(2):
                    n = FIRST["branch"] + 2 * br + j
                    wait_full(pe, n)
                    if br == 1:
                        pe.wait_ge(sem("branch_taken"), j + 1)
                    for o in range(4):
                        for k in range(4):
                            last = mm(ps[:, 2 * j + o // 2, (o % 2) * T:(o % 2) * T + T],
                                      slot(n)[:, k * 512 + o * P:k * 512 + o * P + P], src[:, k, :],
                                      start=(k == 0), stop=(k == 3))
                    done(last)
            pe.wait_ge(sem("merged_ready"), 1)
            square_product("w_out", 4, merged, bank0=4)

            sum_squares(13, KD, T, 0)
            pe.wait_ge(sem("modulated"), 3)
            pe.wait_ge(sem("router_in"), 16)
            for t in range(TT):
                for k in range(KD):
                    last = mm(ps[:, 1, t * EXPERTS:(t + 1) * EXPERTS], x_in[:, k, t * P:t * P + P], router[:, k, :],
                              start=(k == 0), stop=(k == KD - 1))
            last.then_inc(sem("router_scores"), 1)
            for k in range(KD):
                for t in range(TT):
                    last = pe.transpose(ps[:, 4 + 2 * t + k // 4, (k % 4) * P:(k % 4) * P + P],
                                        x_in[:, k, t * P:t * P + P], ident)
            last.then_inc(sem("rows_back"), 1)
            pe.wait_ge(sem("aff_ready"), 1)
            for t in range(TT):
                last = pe.transpose(ps[0:EXPERTS, 0, t * P:t * P + P], aff[:, t, :], ident)
            last.then_inc(sem("aff_turned"), 1)
            pe.wait_ge(sem("slots_chosen"), 1)
            for t in range(TT):
                last = pe.transpose(ps[:, 1, t * EXPERTS:(t + 1) * EXPERTS], slot_t[0:EXPERTS, t * P:t * P + P],
                                    ident[0:EXPERTS, 0:EXPERTS])
            last.then_inc(sem("slots_turned"), 1)
            pe.wait_ge(sem("pick_ready"), 1)
            pe.wait_ge(sem("rows_copied"), 1)
            for k in range(KD):
                if k >= 4:
                    pe.wait_ge(sem("x_exp_taken"), k - 3)
                for t in range(TT):
                    last = mm(ps[:, 4 + k % 4, :], tok[:, t, k * P:k * P + P], pick[:, t, :], start=(t == 0),
                              stop=(t == TT - 1))
                last.then_inc(sem("x_exp_product"), 1)
            for e in range(EXPERTS):
                if e >= 8 and e % 2 == 0:
                    pe.wait_ge(sem("spread_taken"), e // 2 - 3)
                for t in range(TT):
                    for g in (0, 32):
                        o = ps[g:g + 32, (e // 2) % 4, (e % 2) * T + t * P:(e % 2) * T + t * P + P]
                        last = mm(o, pick_gate[:, t, e * CAP:(e + 1) * CAP], ident, start=True, stop=True)
                if e % 2 == 1:
                    last.then_inc(sem("spread_turned"), 1)
            pe.wait_ge(sem("spread_taken"), EXPERTS // 2)
            pe.wait_ge(sem("x_exp_taken"), KD)
            for b in range(4):
                last = mm(banks(b, 1), zero_w[:, 0:P], zero_w[:, :], start=True, stop=False, skip_group_check=True)
            last.then_inc(sem("spread_free"), 1)

            with pe.Fori(0, EXPERTS) as e:
                def product(m, src):
                    for j in range(4):
                        n = FIRST["experts"] + 4 * m + j
                        wait_full(pe, n, 32 * e)
                        for k in range(2):
                            for half in range(2):
                                g = 32 * (2 * k + half)
                                last = mm(ps[g:g + 32, 4 + m, :], src[:, 2 * j + k, :],
                                          slot(n)[:, k * D + 512 * half:k * D + 512 * half + 512],
                                          start=(j == 0), stop=(j == 3))
                        done(last)

                pe.wait_ge(sem("x_cur_ready"), e + 1)
                product(0, x_cur[:, 0])
                product(1, x_cur[:, 0])
                pe.wait_ge(sem("hid_ready"), e + 1)
                for c in range(4):
                    last = mm(ps[:, 7, 64 * c:64 * c + 64], hid_e[0:64, P * c:P * c + P], ident[0:64, 0:64],
                              start=True, stop=True)
                last.then_inc(sem("hid_turned"), 1)
                pe.wait_ge(sem("hid_t_ready"), e + 1)
                product(2, hid_t)
                pe.wait_ge(sem("y_ready"), e + 1)
                for d in range(KD):
                    half = d // 4
                    last = mm(ps[:, d // 2, (d % 2) * T:(d % 2) * T + T],
                              y_e[32 * half:32 * half + 32, (d % 4) * P:(d % 4) * P + P],
                              spread_cur[32 * half:32 * half + 32, 0, :], start=False, stop=False, skip_group_check=True)
                last.then_inc(sem("spread_free"), 1)

            sum_squares(14, KD, T, 4)
            pe.wait_ge(sem("xn_ready"), 14)
            for t in range(TT):
                for k in range(KD):
                    last = pe.transpose(ps[:, 2 * t + k // 4, (k % 4) * P:(k % 4) * P + P], x_in[:, k, t * P:t * P + P], ident)
                    if k % 4 == 3:
                        last.then_inc(sem("out_turned"), 1)

        @block.scalar
        def _(act):
            fn = act.activation

            for rows, table, inputs in ((rows_a, ROWS_A, vectors_a), (rows_b, ROWS_B, vectors_b)):
                for name, first in table.items():
                    src = as_rows(inputs[name])
                    act.dma_start(rows[first:first + src.shape[0], :], src).then_inc(sem("rows_in"), 16)
            act.dma_start(rows_dw, conv_w_dw[0]).then_inc(sem("rows_in"), 16)
            for j, g in enumerate((q_norm_g_2, k_norm_g_2)):
                for half in range(2):
                    act.dma_start(qk_gain[64 * half:64 * half + 64, j:j + 1], g.rearrange("a d -> d a")
                                  ).then_inc(sem("gains_in"), 16)
            act.dma_start(mask_in, masks).then_inc(sem("masks_in"), 16)
            act.dma_start(router[:, :, :], w_router_2[0].rearrange("(k p) e -> p k e", p=P)).then_inc(sem("router_in"), 16)
            act.dma_start(pos_i[:, :], positions.partition_broadcast(P)).then_inc(sem("positions_in"), 16)

            act.wait_ge(sem("x_turned"), 1)
            fn(h[:, :, :].rearrange("p k t -> p (k t)"), banks(2, 4), ACT.Copy).then_inc(sem("h_loaded"), 1)
            act.dma_start(tok[:, :, :], ctx_2[0].rearrange("(t p) d -> p t d", p=P)).then_inc(sem("ctx_in"), 16)
            act.wait_ge(sem("vectors_ready"), 1)
            fn(cond_pad[:, :, 0:2], vec_b[:, 0:2 * KD].rearrange("p (c k) -> p k c", c=2), ACT.Silu
               ).then_inc(sem("cond_ready"), 1)
            act.wait_ge(sem("floor_logits"), 1)
            fn(lb_tmp[:, 0:2], lb_tmp[:, 0:2], ACT.Exp).then_inc(sem("floor_exp"), 1)
            def square(src, first, n):
                k_tiles = src.shape[1]
                fn(squares[:, first:first + k_tiles, 0:n], src, ACT.Square).then_inc(sem("squares_ready"), 1)

            def root(m, bank, dim, region=0, n=T):
                act.wait_ge(sem("sumsq_ready"), m)
                fn(std[:, region:region + n], ps[:, bank, 0:n], ACT.Ln, bias=eps_col[:, 0:1],
                   scale=1.0 / dim).then_inc(sem("log_ready"), 1)
                act.wait_ge(sem("log_ready"), m)
                fn(rstd[:, region:region + n], std[:, region:region + n], ACT.Exp, scale=-0.5
                   ).then_inc(sem("rstd_ready"), 1)

            x_in = xn[:, :, T:2 * T]

            def split_hi(n, o, columns=True, more_halves=0, more_full=0):
                q = HALF[n] + o
                if q >= HALF_BUFS:
                    act.wait_ge(half_done, q - HALF_BUFS + 1 + more_halves)
                if o == 0:
                    if n >= 1 and n - 1 not in HALF:
                        act.wait_ge(slot_free, n)
                    wait_full(act, n, more_full)
                fn(half_part(n, o, 0), half_slot(n, o, columns), ACT.Copy).then_inc(sem("half_hi"), 1)

            def split_hi_slot(n, columns=True):
                for o in range(2):
                    split_hi(n, o, columns)

            def x_hi(norm):
                for g in range(2):
                    if g == 0:
                        act.wait_ge(sem("xn_half"), XN_HALF[norm])
                    else:
                        act.wait_ge(sem("xn_ready"), norm)
                    fn(x_split[:, 0, 4 * g:4 * g + 4, :], x_in[:, 4 * g:4 * g + 4, :], ACT.Copy).then_inc(sem("x_hi"), 1)

            def ffn(f, norm):
                n0 = FIRST[f"ffn{f}"]
                steps = FF_STEPS * f
                split_hi_slot(n0)
                if f > 0:
                    act.wait_ge(sem("h_updated"), {1: 2, 2: 3, 3: 5}[f])
                square(h[:, :, :], 0, T)
                split_hi_slot(n0 + 1)
                root(norm, 4, D)
                x_hi(norm)

                def gate(n, c, more_slot, more):
                    wait_done(act, n, more_slot)
                    if c > 0:
                        act.wait_ge(sem("hidden_ready"), steps + c + more)
                    fn(silu_gate[:, c % 2, :], ps[:, 4 + c % 2, :], ACT.Silu).then_inc(sem("silu_ready"), 1)

                def hidden_hi(c, more):
                    act.wait_ge(sem("hidden_ready"), steps + c + 1 + more)
                    fn(hid_split[:, c % 2, 0, :, :], hidden[:, c % 2, :, :], ACT.Copy).then_inc(sem("hid_hi"), 1)

                gate(n0, 0, 0, 0)
                with act.Fori(0, FF_STEPS // 2) as i:
                    for j in range(2):
                        n = n0 + 2 + 3 * j
                        for s in range(3):
                            for o in range(2):
                                split_hi(n + s, o, s < 2, 12 * i, 16 * i)
                            if s == 0:
                                hidden_hi(j, 2 * i)
                        gate(n, 1 + j, 12 * i, 2 * i)
                split_hi_slot(n0 + 32, columns=False)
                hidden_hi(FF_STEPS - 1, 0)

            act.wait_ge(sem("h_loaded"), 1)
            ffn(0, 1)

            split_hi_slot(FIRST["pw1"])
            act.wait_ge(sem("h_updated"), 1)
            square(h[:, :, :], 0, T)
            split_hi_slot(FIRST["pw1"] + 1)
            root(2, 4, D)
            x_hi(2)
            for i in range(KD // 2):
                if i < KD // 2 - 1:
                    split_hi_slot(FIRST["pw1"] + 2 * i + 2)
                    split_hi_slot(FIRST["pw1"] + 2 * i + 3)
                wait_done(act, FIRST["pw1"] + 2 * i + 1)
                if i >= 2:
                    act.wait_ge(sem("glu_ready"), i - 1)
                fn(glu_sig[:, i % 2, :], ps[:, (2 * i + 1) % 4, :], ACT.Sigmoid).then_inc(sem("glu_sig_ready"), 1)
            for c in range(12):
                wait_done(act, FIRST["mod"] + 2 * c + 1)
                if c >= 2:
                    act.wait_ge(sem("mod_turned"), c - 1)
                fn(mod_rows[:, c % 2, :], ps[:, 5 + c % 2, :], ACT.Copy).then_inc(sem("mod_copied"), 1)
            split_hi_slot(FIRST["pw2"])
            split_hi_slot(FIRST["pw2"] + 1)
            act.wait_ge(sem("conv_done"), KD)
            square(conv_acc, 0, T)
            root(3, 4, D)
            for g in range(2):
                if g == 0:
                    act.wait_ge(sem("xn_half"), XN_HALF[3])
                else:
                    act.wait_ge(sem("xn_ready"), 3)
                x_g = x_in[:, 4 * g:4 * g + 4, :]
                fn(x_split[:, 0, 4 * g:4 * g + 4, :], x_g, ACT.Silu)
                fn(x_g, x_g, ACT.Silu).then_inc(sem("x_hi"), 1)
            split_hi_slot(FIRST["pw2"] + 2)
            split_hi_slot(FIRST["pw2"] + 3)
            ffn(1, 4)
            ffn(2, 5)

            act.wait_ge(sem("h_updated"), 4)
            square(h[:, :, :], 0, T)
            root(6, 4, D)
            act.wait_ge(sem("angles_ready"), 1)
            fn(sin_t, ang, ACT.Sin).then_inc(sem("trig_ready"), 1)
            fn(cos_t, turns, ACT.Sin).then_inc(sem("trig_ready"), 1)
            wait_done(act, FIRST["mla_a"] + 1)
            square(banks(0, 2).rearrange("p (k t) -> p k t", t=T), 0, T)
            wait_done(act, FIRST["mla_a"] + 2)
            square(banks(2, 1).rearrange("p (k t) -> p k t", t=T), 4, T)
            wait_done(act, FIRST["mla_a"] + 3)
            fn(rope_in[:, 4, :], ps[:, 3, 0:T], ACT.Copy)
            root(7, 4, Q_LORA)
            root(8, 7, KV_LORA, region=T)
            for j in range(4):
                b = 5 if j % 2 == 0 else 0
                wait_done(act, FIRST["uq"] + j)
                fn(q_nope[:, 2 * j:2 * j + 2, :].rearrange("p a t -> p (a t)"), ps[:, b, :], ACT.Copy)
                fn(rope_in[:, j, :], ps[:, b + 1, 0:T], ACT.Copy).then_inc(sem("uq_taken"), 1)
            for j in range(2):
                wait_done(act, FIRST["ukv"] + j)
                fn(k_nope[:, 4 * j:4 * j + 4, :].rearrange("p a t -> p (a t)"), banks(0, 2), ACT.Copy)
                fn(v_tok[:, :, 4 * j:4 * j + 4, :].rearrange("p s a v -> p s (a v)"), ps[:, 2:4, :], ACT.Copy
                   ).then_inc(sem("ukv_taken"), 1)

            def mla_exp(hd):
                act.wait_ge(sem("mla_max"), hd + 1)
                if hd >= 2:
                    act.wait_ge(sem("mla_turned"), hd - 1)
                for t in range(TT):
                    a, b = (0, P) if t == 0 else (P, 3 * P)
                    fn(mla_p[:, hd % 2, a:b], ps[:, hd % 2, a:b], ACT.Exp, bias=mla_stat[:, 0, hd, t:t + 1],
                       scale=MLA_SCALE, accum_out=mla_stat[:, 1, hd, t:t + 1]).then_inc(sem("mla_exp"), 1)

            def mla_copy(hd):
                act.wait_ge(sem("mla_turned"), hd + 1)
                if hd >= 2:
                    act.wait_ge(sem("mla_out"), hd - 1)
                fn(mla_pt[:, hd % 2, :, :].rearrange("p b q -> p (b q)"), ps[:, 2 + hd % 2, 0:3 * P], ACT.Copy
                   ).then_inc(sem("mla_pt"), 1)

            for i in range(MLA_HEADS + 1):
                if i < MLA_HEADS:
                    mla_exp(i)
                if i >= 1:
                    mla_copy(i - 1)
            ffn(3, 9)

            act.wait_ge(sem("h_updated"), 6)
            square(h[:, :, :], 0, T)
            root(10, 4, D)
            act.wait_ge(sem("ctx_turned"), 1)
            square(banks(0, 4).rearrange("p (k t) -> p k t", t=T), 0, T)
            root(11, 5, D, region=T)
            act.wait_ge(sem("xn_ready"), 10)
            square(h[:, :, :], 0, T)
            root(12, 6, D)
            for m, c, half in ((11, 1, 0), (12, 0, 1)):
                act.wait_ge(sem("xn_ready"), m)
                for k in range(KD):
                    o = xn[:, k, half * T:half * T + T]
                    last = fn(o, o, ACT.Identity, bias=mod[:, k, c:c + 1])
                last.then_inc(sem("modulated"), 1)

            def decay_exp(r):
                act.wait_ge(sem("decay_ready"), r + 1)
                d = decay[:, r % 2].rearrange("p d h t -> p (d h t)")
                fn(d, d, ACT.Exp).then_inc(sem("decay_exp"), 1)

            for step, (name, s) in enumerate(PROJ):
                b = 2 * (step % PAIRS)
                if name == "ak":
                    act.wait_ge(sem("ak_product"), 1)
                else:
                    wait_done(act, FIRST["w_in"] + s)
                one, two = ps[:, b, :], ps[:, b:b + 2, :]
                i = s % 2 if s < 12 else 0
                if name == "q":
                    last = fn(hg_q[:, 2 * s:2 * s + 2, :].rearrange("p a t -> p (a t)"), one, ACT.Copy)
                elif name in ("ff", "fb"):
                    key, log = (key_f, log_f) if name == "ff" else (key_b, log_b)
                    fn(key[:, 2 * i:2 * i + 2, :], two, ACT.Sigmoid, scale=-1.0)
                    last = fn(log[:, 2 * i:2 * i + 2, :], two, ACT.Sigmoid)
                elif name == "i":
                    last = fn(hg_v[:, :, 256 * i:256 * i + 256].rearrange("p (b t) c -> p b t c", b=2),
                              two.rearrange("p b (t c) -> p b t c", c=256), ACT.Copy)
                elif name == "g":
                    last = fn(hg_gate[:, 2 * i:2 * i + 2, :].rearrange("p a t -> p (a t)"), one, ACT.Silu)
                elif name == "aq":
                    last = fn(att_q[:, 2 * i:2 * i + 2, :].rearrange("p a t -> p (a t)"), one, ACT.Copy)
                elif name == "ak":
                    last = fn(att_k, two, ACT.Copy)
                elif name == "av":
                    last = fn(att_v.rearrange("p b c -> p (b c)"), one, ACT.Copy)
                else:
                    g, i = (gate_a, s - 13) if name == "ga" else (gate_b, s - 17)
                    last = fn(g[:, 2 * i:2 * i + 2, :].rearrange("p a t -> p (a t)"), one, ACT.Sigmoid)
                last.then_inc(sem("proj_taken"), 1)
                if step == 5:
                    act.wait_ge(sem("proj_taken"), 6)
                    for dr, log in ((0, log_f), (1, log_b)):
                        for hd in range(HG_HEADS):
                            fn(log[:, hd, :], log[:, hd, :], ACT.Ln, bias=floor[:, 0, dr, hd:hd + 1],
                               scale=floor[:, 1, dr, hd:hd + 1]).then_inc(sem("forget_ready"), 1)
                if step >= ROUND_AT - 2 and step - (ROUND_AT - 2) < ROUNDS - 1:
                    decay_exp(step - (ROUND_AT - 2))

            act.wait_ge(sem("round_ready"), ROUND_WIDE)
            fn(q_dec[:, 0], pre_x[:, 0, :, 1:T + 1], ACT.Exp).then_inc(sem("q_dec_exp"), 1)
            act.wait_ge(sem("end_ready"), 1)
            fn(q_dec[:, 1], q_dec[:, 1], ACT.Exp).then_inc(sem("q_dec_exp"), 1)
            fn(key_dec[:, 0], key_dec[:, 0], ACT.Exp).then_inc(sem("key_dec_exp"), 1)
            fn(key_dec[:, 1], pre_c[:, 1, :, 0:T], ACT.Exp).then_inc(sem("key_dec_exp"), 1)
            act.wait_ge(sem("key_dec_turned"), 1)
            fn(key_dec_t.rearrange("p d s c -> p (d s c)"), banks(0, 4), ACT.Copy).then_inc(sem("key_dec_t_ready"), 1)
            act.wait_ge(sem("state_product"), 1)
            fn(state0.rearrange("p d h v -> p (d h v)"), banks(4, 2), ACT.Copy).then_inc(sem("state_ready"), 1)
            act.wait_ge(sem("round_scores"), ROUNDS)
            fn(att_sq[:, 0:4 * T], att_q.rearrange("p a t -> p (a t)"), ACT.Square)
            fn(att_sq[:, 4 * T:8 * T], att_k.rearrange("p a t -> p (a t)"), ACT.Square).then_inc(sem("att_sq_ready"), 1)
            act.wait_ge(sem("hg_out"), 1)
            act.wait_ge(sem("round_ready"), ROUNDS)
            fn(o_sq.rearrange("p a t -> p (a t)"), banks(0, 2), ACT.Square).then_inc(sem("hg_sq_ready"), 1)
            act.wait_ge(sem("hg_sumsq"), 1)
            o_flat = o_hg.rearrange("p a t -> p (a t)")
            fn(o_flat, banks(2, 2), ACT.Ln, bias=eps_col[:, 0:1], scale=1.0 / P).then_inc(sem("hg_log"), 1)
            act.wait_ge(sem("hg_log"), 1)
            fn(o_flat, o_flat, ACT.Exp, scale=-0.5).then_inc(sem("hg_rstd"), 1)
            act.wait_ge(sem("att_sumsq"), 1)
            fn(att_rinv, banks(4, 4), ACT.Ln, bias=eps_col[:, 0:1], scale=1.0 / ATT_HD).then_inc(sem("att_log"), 1)
            act.wait_ge(sem("att_log"), 1)
            fn(att_rinv, att_rinv, ACT.Exp, scale=-0.5).then_inc(sem("att_rstd"), 1)

            n_units = ATT_HEADS * TT

            def att_exp(u):
                act.wait_ge(sem("att_max"), u + 1)
                if u >= 2:
                    act.wait_ge(sem("att_p_turned"), u - 1)
                fn(att_p[:, u % 2, :], ps[:, u % 2, :], ACT.Exp, bias=att_stat[:, 0, u:u + 1], scale=ATT_SCALE,
                   accum_out=att_stat[:, 1, u:u + 1]).then_inc(sem("att_exp"), 1)

            def att_copy(u):
                act.wait_ge(sem("att_p_turned"), u + 1)
                if u >= 2:
                    act.wait_ge(sem("att_out"), u - 1)
                fn(att_pt[:, u % 2, :, :].rearrange("p k q -> p (k q)"), ps[:, 2 + u % 2, :], ACT.Copy
                   ).then_inc(sem("att_pt"), 1)

            for i in range(n_units + 1):
                if i < n_units:
                    att_exp(i)
                if i >= 1:
                    att_copy(i - 1)
            act.wait_ge(sem("att_out"), n_units)
            fn(o_att.rearrange("p a t -> p (a t)"), banks(4, 2), ACT.Copy).then_inc(sem("o_att_ready"), 1)

            act.wait_ge(sem("h_updated"), 7)
            square(h[:, :, :], 0, T)
            root(13, 0, D)
            act.wait_ge(sem("xn_ready"), 13)
            for k in range(KD):
                last = fn(x_in[:, k, :], x_in[:, k, :], ACT.Identity, bias=mod[:, 3 * KD + k, 0:1])
            last.then_inc(sem("modulated"), 1)
            act.wait_ge(sem("logits_ready"), 1)
            fn(aff_e.rearrange("p t e -> p (t e)"), aff_e.rearrange("p t e -> p (t e)"), ACT.Exp).then_inc(sem("aff_exp"), 1)
            act.wait_ge(sem("rows_back"), 1)
            fn(tok[:, :, :].rearrange("p t d -> p (t d)"), banks(4, 4), ACT.Copy).then_inc(sem("rows_copied"), 1)
            for k in range(KD):
                act.wait_ge(sem("x_exp_product"), k + 1)
                fn(x_exp[:, k, :], ps[:, 4 + k % 4, :], ACT.Copy).then_inc(sem("x_exp_taken"), 1)
            act.wait_ge(sem("spread_taken"), EXPERTS // 2)
            act.wait_ge(sem("x_exp_taken"), KD)
            with act.Fori(0, EXPERTS) as e:
                n = FIRST["experts"]
                wait_done(act, n - 5, 12 * e)
                fn(x_cur[:, 0], x_exp[:, :, bass.ds(e * CAP, CAP)], ACT.Copy).then_inc(sem("x_cur_ready"), 1)
                wait_done(act, n + 3, 12 * e)
                fn(half_g[0:64, :], ps[64:128, 4, :], ACT.Copy).then_inc(sem("half_g_ready"), 1)
                act.wait_ge(sem("gate_sum_ready"), e + 1)
                fn(gate_act[0:64, :], gate_sum[0:64, :], ACT.Silu).then_inc(sem("gate_act_ready"), 1)
                wait_done(act, n + 7, 12 * e)
                fn(half_u[0:64, :], ps[64:128, 5, :], ACT.Copy).then_inc(sem("half_u_ready"), 1)
                act.wait_ge(sem("spread_free"), e + 1)
                fn(spread_cur[0:64, 0, :], spread[:, bass.ds(e, 1), :].rearrange("p o t -> p (o t)"), ACT.Copy
                   ).then_inc(sem("spread_cur_ready"), 1)
                act.wait_ge(sem("hid_turned"), e + 1)
                fn(hid_t.rearrange("p (h c) s -> p h c s", h=2),
                   ps[:, 7, 0:256].rearrange("p (c h s) -> p h c s", c=4, h=2), ACT.Copy).then_inc(sem("hid_t_ready"), 1)
                wait_done(act, n + 11, 12 * e)
                fn(half_y[0:64, :], ps[64:128, 6, :], ACT.Copy).then_inc(sem("half_y_ready"), 1)

            act.wait_ge(sem("h_updated"), 8)
            square(h[:, :, :], 0, T)
            root(14, 4, D)
            for t in range(TT):
                for c in range(2):
                    act.wait_ge(sem("out_turned"), 2 * t + c + 1)
                    fn(tok[:, t, 512 * c:512 * c + 512], ps[:, 2 * t + c, :], ACT.Copy).then_inc(sem("rows_out"), 1)

        @block.vector
        def _(dve):
            steps = [0]

            def step(ins):
                ins.then_inc(sem("dve_step"), 1)
                steps[0] += 1

            def settle():
                dve.wait_ge(sem("dve_step"), steps[0])

            x_in = xn[:, :, T:2 * T]

            dve.memset(cond_pad, 0.0).then_inc(sem("pad_cleared"), 1)
            step(dve.memset(zero_w[:, :], 0.0))
            dve.memset(eps_col[:, :], EPS).then_inc(sem("eps_set"), 1)
            dve.wait_ge(sem("rows_turned"), 1)
            step(dve.tensor_copy(vec_a[:, :], ps[:, 0, 0:N_ROWS_A]))
            step(dve.tensor_copy(vec_b[:, :], ps[:, 1, 0:N_ROWS_B]))
            dve.tensor_copy(w_dw[:, :, :].rearrange("p k w -> p (k w)"), ps[:, 6, 0:KD * CONV_W]
                            ).then_inc(sem("vectors_ready"), 1)
            dve.wait_ge(sem("masks_in"), 16)
            step(dve.tensor_copy(mask[:, :, :], mask_in))
            settle()
            r = ROWS_B["hg_lb_logits_2"]
            lg = vec_b[:, r:r + 16].rearrange("p (d l h) -> p l d h", d=2, l=2)
            a, b, m = (lb_tmp[:, i] for i in range(3))
            step(dve.tensor_tensor(m, lg[:, 0], lg[:, 1], ALU.max))
            settle()
            step(dve.tensor_tensor(a, lg[:, 0], m, ALU.subtract))
            dve.tensor_tensor(b, lg[:, 1], m, ALU.subtract).then_inc(sem("floor_logits"), 1)
            dve.wait_ge(sem("floor_exp"), 1)
            step(dve.tensor_tensor(m, a, b, ALU.add))
            settle()
            step(dve.reciprocal(m, m))
            settle()
            step(dve.tensor_tensor(floor[:, 0], a, m, ALU.mult))
            settle()
            step(dve.tensor_scalar(floor[:, 1], floor[:, 0], -1.0, 1.0, ALU.mult, ALU.add))
            def normed(m, dst, src, gain, region=0):
                dve.wait_ge(sem("rstd_ready"), m)
                k_tiles = dst.shape[1]
                for k in range(k_tiles):
                    last = dve.scalar_tensor_tensor(dst[:, k, :], src[:, k, :], gain[:, k:k + 1],
                                                    rstd[:, region:region + T], ALU.mult, ALU.mult)
                    if m in XN_HALF and k == 3:
                        last.then_inc(sem("xn_half"), 1)
                last.then_inc(sem("xn_ready"), 1)

            def x_lo(name):
                for g in range(2):
                    dve.wait_ge(sem("x_hi"), 2 * X_SPLITS[name] + g + 1)
                    hi, lo = (x_split[:, part, 4 * g:4 * g + 4, :] for part in range(2))
                    dve.tensor_tensor(lo, x_in[:, 4 * g:4 * g + 4, :], hi.bitcast(F32), ALU.subtract
                                      ).then_inc(sem("x_split_ready"), 1)

            def split_lo(n, o, columns=True, more_halves=0):
                dve.wait_ge(sem("half_hi"), HALF[n] + o + 1 + more_halves)
                ins = dve.tensor_tensor(half_part(n, o, 1), half_slot(n, o, columns), half_part(n, o, 0).bitcast(F32),
                                        ALU.subtract)
                ins.then_inc(sem("half_split") if o == 0 else slot_free, 1)

            def split_lo_slot(n, columns=True):
                for o in range(2):
                    split_lo(n, o, columns)

            def gains(name, layer=0):
                return vec_a[:, ROWS_A[name] + KD * layer:ROWS_A[name] + KD * layer + KD]

            def ffn(f, norm, gain, after=None):
                n0 = FIRST[f"ffn{f}"]
                done = FF_STEPS * f
                split_lo_slot(n0 + 1)
                normed(norm, x_in, h[:, :, :], gain)
                x_lo(f"ffn{f}")

                def combine(n, c, more_slot, more):
                    dve.wait_ge(sem("silu_ready"), done + c + 1 + more)
                    wait_done(dve, n, more_slot)
                    dve.tensor_tensor(hidden[:, c % 2, :, :].rearrange("p k t -> p (k t)"), silu_gate[:, c % 2, :],
                                      ps[:, 6 + c % 2, :], ALU.mult).then_inc(sem("hidden_ready"), 1)
                    dve.wait_ge(sem("hid_hi"), done + c + 1 + more)
                    dve.tensor_tensor(hid_split[:, c % 2, 1, :, :], hidden[:, c % 2, :, :],
                                      hid_split[:, c % 2, 0, :, :].bitcast(F32), ALU.subtract
                                      ).then_inc(sem("hid_split_ready"), 1)

                with dve.Fori(0, FF_STEPS // 2) as i:
                    for j in range(2):
                        n = n0 + 2 + 3 * j
                        for s in range(3):
                            for o in range(2):
                                split_lo(n + s, o, s < 2, 12 * i)
                            if s == 0:
                                combine(n - 1 - (j > 0), j, 12 * i, 2 * i)
                split_lo_slot(n0 + 32, columns=False)
                combine(n0 + 30, FF_STEPS - 1, 0, 0)
                if after is not None:
                    split_lo_slot(after)
                wait_done(dve, n0 + 32)
                hf = h[:, :, :].rearrange("p k t -> p (k t)")
                dve.scalar_tensor_tensor(hf, banks(0, 4), 0.5, hf, ALU.mult, ALU.add).then_inc(sem("h_updated"), 1)

            def add_product(last_slot, after=None):
                if after is not None:
                    split_lo_slot(after)
                wait_done(dve, last_slot)
                hf = h[:, :, :].rearrange("p k t -> p (k t)")
                dve.tensor_tensor(hf, banks(0, 4), hf, ALU.add).then_inc(sem("h_updated"), 1)

            split_lo_slot(FIRST["ffn0"])
            ffn(0, 1, gains("ffn_norm1", 0), after=FIRST["pw1"])

            dve.wait_ge(sem("h_updated"), 1)
            step(dve.memset(conv_in[:, :, 0:PAD], 0.0))
            split_lo_slot(FIRST["pw1"] + 1)
            normed(2, x_in, h[:, :, :], gains("mix_norm", 0))
            x_lo("pw1")
            split_lo_slot(FIRST["pw1"] + 2)
            split_lo_slot(FIRST["pw1"] + 3)
            tap_done = {}

            def glu(pair):
                dve.wait_ge(sem("glu_sig_ready"), pair + 1)
                dve.tensor_tensor(conv_in[:, 2 * pair:2 * pair + 2, PAD:PAD + T],
                                  ps[:, (2 * pair) % 4, :].rearrange("p (a t) -> p a t", t=T),
                                  glu_sig[:, pair % 2, :].rearrange("p (a t) -> p a t", t=T), ALU.mult
                                  ).then_inc(sem("glu_ready"), 1)

            def taps(pair, first, last):
                if first == 0:
                    dve.wait_ge(sem("glu_ready"), pair + 1)
                    settle()
                for w in range(first, last):
                    for j in (2 * pair, 2 * pair + 1):
                        u = conv_in[:, j, w:w + T]
                        if w == 0:
                            step(dve.tensor_scalar(conv_acc[:, j, :], u, w_dw[:, j, 0:1], None, ALU.mult))
                            tap_done[j] = steps[0]
                        else:
                            dve.wait_ge(sem("dve_step"), tap_done[j])
                            ins = dve.scalar_tensor_tensor(conv_acc[:, j, :], u, w_dw[:, j, w:w + 1],
                                                           conv_acc[:, j, :], ALU.mult, ALU.add)
                            if w < CONV_W - 1:
                                step(ins)
                                tap_done[j] = steps[0]
                            else:
                                ins.then_inc(sem("conv_done"), 1)

            glu(0)
            taps(0, 0, 4)
            split_lo_slot(FIRST["pw1"] + 4)
            taps(0, 4, 8)
            split_lo_slot(FIRST["pw1"] + 5)
            glu(1)
            taps(0, 8, 12)
            split_lo_slot(FIRST["pw1"] + 6)
            taps(0, 12, 16)
            split_lo_slot(FIRST["pw1"] + 7)
            taps(0, 16, CONV_W)
            glu(2)
            taps(1, 0, CONV_W)
            glu(3)
            taps(2, 0, CONV_W)
            taps(3, 0, CONV_W)
            split_lo_slot(FIRST["pw2"])
            split_lo_slot(FIRST["pw2"] + 1)
            normed(3, x_in, conv_acc, gains("conv_norm"))
            x_lo("pw2")
            split_lo_slot(FIRST["pw2"] + 2)
            split_lo_slot(FIRST["pw2"] + 3)
            dve.wait_ge(sem("mod_turned"), 12)
            bias = vec_b[:, ROWS_B["b_mod_2"]:ROWS_B["b_mod_2"] + 48].unsqueeze(2).to_broadcast([P, 48, 2])
            step(dve.tensor_tensor(mod[:, :, :], ps[:, 7, 0:96].rearrange("p (f c) -> p f c", c=2), bias, ALU.add))
            settle()
            for i, (first, c, g) in enumerate(((KD, 0, "norm1_g_2"), (KD, 1, "norm1_g_2"), (4 * KD, 0, "norm2_g_2"))):
                ins = dve.scalar_tensor_tensor(gain_mod[:, i, :], mod[:, first:first + KD, c], 1.0,
                                               vec_b[:, ROWS_B[g]:ROWS_B[g] + KD], ALU.add, ALU.mult)
                ins.then_inc(sem("mod_ready"), 1)
            dve.wait_ge(sem("mod_ready"), 3)
            add_product(FIRST["pw2"] + 3, after=FIRST["ffn1"])
            dve.wait_ge(sem("h_updated"), 2)
            ffn(1, 4, gains("ffn_norm2", 0), after=FIRST["ffn2"])
            dve.wait_ge(sem("h_updated"), 3)
            ffn(2, 5, gains("ffn_norm1", 1))

            dve.wait_ge(sem("positions_in"), 16)
            step(dve.tensor_copy(pos_f, pos_i[:, :]))
            settle()
            step(dve.tensor_scalar(ang, pos_f, const("inv_freq"), None, ALU.mult))
            settle()
            step(dve.tensor_scalar(turns, ang, 1.0 / TWO_PI, ROUND_MAGIC, ALU.mult, ALU.add))
            settle()
            step(dve.tensor_scalar(turns, turns, ROUND_MAGIC, None, ALU.subtract))
            for part in (PI_A, PI_B, PI_C):
                settle()
                step(dve.scalar_tensor_tensor(ang, turns, -part, ang, ALU.mult, ALU.add))
            settle()
            step(dve.tensor_scalar(turns, ang, TWO_PI / 4, -TWO_PI, ALU.is_gt, ALU.mult))
            settle()
            step(dve.scalar_tensor_tensor(turns, ang, TWO_PI / 4, turns, ALU.add, ALU.add))
            settle()
            step(dve.tensor_scalar(turns, turns, PI_LIMIT, -PI_LIMIT, ALU.min, ALU.max))
            dve.tensor_scalar(ang, ang, PI_LIMIT, -PI_LIMIT, ALU.min, ALU.max).then_inc(sem("angles_ready"), 1)
            dve.wait_ge(sem("h_updated"), 4)
            normed(6, x_in, h[:, :, :], gains("mix_norm", 1))
            latent_ps = banks(0, 3).rearrange("p (k t) -> p k t", t=T)
            r = ROWS_A["mla_q_norm"]
            normed(7, latent_n[:, 0:4, :], latent_ps[:, 0:4, :], vec_a[:, r:r + 4])
            normed(8, latent_n[:, 4:6, :], latent_ps[:, 4:6, :], vec_a[:, r + 4:r + 6], region=T)
            dve.wait_ge(sem("trig_ready"), 2)
            dve.wait_ge(sem("uq_taken"), 4)
            for a in range(5):
                last = dve.tensor_tensor(rope_a[:, a, :], rope_in[:, a, :], cos_t, ALU.mult)
            step(last)
            dve.wait_ge(sem("rope_turned"), 1)
            turned = banks(5, 3)[:, 0:5 * T].rearrange("p (a t) -> p a t", t=T)
            step(dve.tensor_tensor(rope_b, turned, sin_t.unsqueeze(1).to_broadcast([P, 5, T]), ALU.mult))
            settle()
            dve.tensor_tensor(rope_a, rope_a, rope_b, ALU.add).then_inc(sem("rope_ready"), 1)

            def mla_max(hd):
                dve.wait_ge(sem("mla_scores"), hd + 1)
                for t in range(TT):
                    a, b = (0, P) if t == 0 else (P, 3 * P)
                    step(dve.tensor_reduce(mla_stat[:, 2, hd, t:t + 1], ps[:, hd % 2, a:b], AX_X, ALU.max))
                settle()
                dve.tensor_scalar(mla_stat[:, 0, hd, :], mla_stat[:, 2, hd, :], -MLA_SCALE, None, ALU.mult
                                  ).then_inc(sem("mla_max"), 1)

            def mla_norm(hd):
                dve.wait_ge(sem("mla_exp"), 2 * hd + 2)
                step(dve.reciprocal(mla_stat[:, 3, hd, :], mla_stat[:, 1, hd, :]))
                settle()
                for t in range(TT):
                    a, b = (0, P) if t == 0 else (P, 3 * P)
                    last = dve.tensor_scalar(mla_p[:, hd % 2, a:b], mla_p[:, hd % 2, a:b], mla_stat[:, 3, hd, t:t + 1],
                                             None, ALU.mult)
                last.then_inc(sem("mla_p"), 1)

            def mla_take(hd):
                dve.wait_ge(sem("mla_out"), hd + 1)
                dve.tensor_copy(o_mla[:, hd, :], ps[:, 4 + hd % 2, 0:T]).then_inc(sem("mla_out_taken"), 1)

            for i in range(MLA_HEADS + 2):
                if i < MLA_HEADS:
                    mla_max(i)
                if i < MLA_HEADS:
                    mla_norm(i)
                if i >= 2:
                    mla_take(i - 2)
            add_product(FIRST["mla_o"] + 3)
            dve.wait_ge(sem("h_updated"), 5)
            split_lo_slot(FIRST["ffn3"])
            ffn(3, 9, gains("ffn_norm2", 1))

            dve.wait_ge(sem("h_updated"), 6)
            normed(10, h[:, :, :], h[:, :, :], gains("final_norm"))
            normed(11, xn[:, :, 0:T], banks(0, 4).rearrange("p (k t) -> p k t", t=T), gain_mod[:, 1, :], region=T)
            dve.wait_ge(sem("xn_ready"), 10)
            normed(12, x_in, h[:, :, :], gain_mod[:, 0, :])

            step(dve.memset(pre_x[:, :, :, 0:1], 0.0))
            step(dve.memset(pre_c[:, :, :, 0:1], 0.0))
            for dr, (key, log) in enumerate(((key_f, log_f), (key_b, log_b))):
                dve.wait_ge(sem("proj_taken"), 4 + 2 * dr)
                for hd in range(HG_HEADS):
                    step(dve.tensor_scalar(key[:, hd, :], key[:, hd, :], floor[:, 1, dr, hd:hd + 1], None, ALU.mult))
            for dr, log in enumerate((log_f, log_b)):
                for hd in range(HG_HEADS):
                    dve.wait_ge(sem("forget_ready"), HG_HEADS * dr + hd + 1)
                    step(dve.tensor_tensor_scan(pre_c[:, dr, hd, 1:T + 1], ones, log[:, hd, 0:T], 0.0, ALU.mult, ALU.add))
                    step(dve.tensor_tensor_scan(pre_x[:, dr, hd, 1:T + 1], ones, log[:, hd, T:2 * T], 0.0, ALU.mult, ALU.add))
            settle()

            def halves(a, h_):
                v = a.rearrange("p h (n two w) -> p h n two w", two=2, w=h_)
                return v[:, :, :, 0, :], v[:, :, :, 1, :]

            half_of = LEVELS + [P]

            def decay_args(r_):
                h_ = half_of[r_]
                n = T // (2 * h_)
                for dr in range(2):
                    run = pre_x[:, dr, :, 1 - dr:1 - dr + T]
                    left, right = halves(run, h_)
                    d_left, d_right = halves(decay[:, r_ % 2, dr], h_)
                    mid = pre_x[:, dr, :, 0:T].rearrange("p h (n two w) -> p h n two w", two=2, w=h_)[:, :, :, 1, 0:1]
                    mid = mid.to_broadcast([P, HG_HEADS, n, h_])
                    dve.tensor_tensor(d_left, mid, left, ALU.subtract)
                    last = dve.tensor_tensor(d_right, right, mid, ALU.subtract)
                last.then_inc(sem("decay_ready"), 1)

            def decayed(r_):
                if r_ >= 2:
                    dve.wait_ge(sem("round_scores"), r_ - 1)
                q_out, k_out = q_lvl[:, r_ % 2], k_lvl[:, r_ % 2]
                if r_ == ROUND_DIAG:
                    dve.tensor_tensor(k_out, key_f[:, :, T:2 * T], key_b[:, :, T:2 * T], ALU.add
                                      ).then_inc(sem("round_ready"), 1)
                    return
                dve.wait_ge(sem("decay_exp"), r_ + 1)
                h_ = half_of[r_]
                q_l, q_r = halves(q_out, h_)
                k_l, k_r = halves(k_out, h_)
                src_l, src_r = halves(hg_q, h_)
                kf_l, _ = halves(key_f[:, :, T:2 * T], h_)
                _, kb_r = halves(key_b[:, :, T:2 * T], h_)
                f_l, f_r = halves(decay[:, r_ % 2, 0], h_)
                b_l, b_r = halves(decay[:, r_ % 2, 1], h_)
                dve.tensor_tensor(q_r, src_r, f_r, ALU.mult)
                dve.tensor_tensor(q_l, src_l, b_l, ALU.mult)
                dve.tensor_tensor(k_l, kf_l, f_l, ALU.mult)
                dve.tensor_tensor(k_r, kb_r, b_r, ALU.mult).then_inc(sem("round_ready"), 1)

            def take_scores(r_):
                dve.wait_ge(sem("round_scores"), r_ + 1)
                for s in range(TT):
                    t = 1 - s if r_ == ROUND_WIDE else s
                    o = hg_p[:, s, :, t * P:t * P + P]
                    data = ps[:, 6 + s, :].rearrange("p (h t) -> p h t", h=HG_HEADS)
                    if r_ == ROUND_WIDE:
                        last = dve.tensor_copy(o, data)
                    else:
                        m_ = mask[:, r_ if r_ < ROUND_WIDE else len(LEVELS), :].unsqueeze(1).to_broadcast([P, HG_HEADS, P])
                        last = dve.copy_predicated(o, m_, data)
                last.then_inc(sem("round_taken"), 1)

            dve.wait_ge(sem("ctx_turned"), 1)
            step(dve.memset(tok[:, :, :].rearrange("p t d -> p (t d)"), 0.0))
            decay_args(0)
            decay_args(1)
            for r_ in range(ROUNDS):
                decayed(r_)
                if r_ + 2 < ROUNDS - 1:
                    dve.wait_ge(sem("round_ready"), r_ + 1)
                    decay_args(r_ + 2)
                if r_ >= 1:
                    if r_ == 1:
                        settle()
                    take_scores(r_ - 1)
            take_scores(ROUNDS - 1)
            wait_done(dve, FIRST["w_in"] + 20)
            dve.tensor_tensor(q_dec[:, 1], pre_x[:, 1, :, T:T + 1].to_broadcast([P, HG_HEADS, T]), pre_x[:, 1, :, 0:T],
                              ALU.subtract)
            dve.tensor_tensor(key_dec[:, 0], pre_c[:, 0, :, T:T + 1].to_broadcast([P, HG_HEADS, T]), pre_c[:, 0, :, 1:T + 1],
                              ALU.subtract).then_inc(sem("end_ready"), 1)
            dve.wait_ge(sem("key_dec_exp"), 2)
            dve.tensor_tensor(key_dec[:, 0], key_dec[:, 0], key_f[:, :, 0:T], ALU.mult)
            dve.tensor_tensor(key_dec[:, 1], key_dec[:, 1], key_b[:, :, 0:T], ALU.mult).then_inc(sem("key_dec_ready"), 1)
            dve.wait_ge(sem("q_dec_exp"), 2)
            for dr in range(2):
                last = dve.tensor_tensor(q_dec[:, dr], q_dec[:, dr], hg_q, ALU.mult)
            last.then_inc(sem("q_dec_ready"), 1)
            dve.wait_ge(sem("hg_rstd"), 1)
            step(dve.tensor_tensor(o_sq, o_hg, hg_gate, ALU.mult))
            settle()
            r = ROWS_B["hg_norm_g_2"]
            for hd in range(HG_HEADS):
                last = dve.scalar_tensor_tensor(o_hg[:, hd, :], ps[:, hd // 2, (hd % 2) * T:(hd % 2) * T + T],
                                                vec_b[:, r + hd:r + hd + 1], o_sq[:, hd, :], ALU.mult, ALU.mult)
            last.then_inc(sem("hg_normed"), 1)

            dve.wait_ge(sem("att_rstd"), 1)
            dve.wait_ge(sem("gains_in"), 64)
            qf, kf = att_qr.rearrange("p a t -> p (a t)"), att_kr.rearrange("p a t -> p (a t)")
            dve.wait_ge(sem("key_dec_ready"), 1)
            dve.scalar_tensor_tensor(qf, att_q.rearrange("p a t -> p (a t)"), qk_gain[:, 0:1], att_rinv[:, 0:4 * T],
                                     ALU.mult, ALU.mult)
            dve.scalar_tensor_tensor(kf, att_k.rearrange("p a t -> p (a t)"), qk_gain[:, 1:2], att_rinv[:, 4 * T:8 * T],
                                     ALU.mult, ALU.mult).then_inc(sem("att_n_ready"), 1)
            dve.wait_ge(sem("att_turned"), 1)
            cos_q = const("axial_cos").unsqueeze(1).to_broadcast([P, 4, T])
            sin_q = const("axial_sin").unsqueeze(1).to_broadcast([P, 4, T])
            cos_k = const("axial_cos").unsqueeze(1).to_broadcast([P, ATT_KV, T])
            sin_k = const("axial_sin").unsqueeze(1).to_broadcast([P, ATT_KV, T])
            rot = att_rot.rearrange("p (a t) -> p a t", t=T)
            sq = att_sq.rearrange("p (a t) -> p a t", t=T)
            dve.wait_ge(sem("att_n_ready"), 1)
            step(dve.tensor_tensor(rot[:, 0:4, :], att_qr, cos_q, ALU.mult))
            step(dve.tensor_tensor(rot[:, 4:6, :], att_kr[:, :, T:2 * T], cos_k, ALU.mult))
            step(dve.tensor_tensor(sq[:, 0:4, :], banks(4, 2).rearrange("p (a t) -> p a t", t=T), sin_q, ALU.mult))
            step(dve.tensor_tensor(sq[:, 4:6, :], banks(6, 1).rearrange("p (a t) -> p a t", t=T), sin_k, ALU.mult))
            settle()
            dve.tensor_tensor(att_qr, rot[:, 0:4, :], sq[:, 0:4, :], ALU.add)
            dve.tensor_tensor(att_kr[:, :, T:2 * T], rot[:, 4:6, :], sq[:, 4:6, :], ALU.add).then_inc(sem("att_ready"), 1)

            def att_max(u):
                dve.wait_ge(sem("att_scores"), u + 1)
                step(dve.tensor_reduce(att_stat[:, 2, u:u + 1], ps[:, u % 2, :], AX_X, ALU.max))
                settle()
                dve.tensor_scalar(att_stat[:, 0, u:u + 1], att_stat[:, 2, u:u + 1], -ATT_SCALE, None, ALU.mult
                                  ).then_inc(sem("att_max"), 1)

            def att_norm(u):
                dve.wait_ge(sem("att_exp"), u + 1)
                step(dve.reciprocal(att_stat[:, 3, u:u + 1], att_stat[:, 1, u:u + 1]))
                settle()
                dve.tensor_scalar(att_p[:, u % 2, :], att_p[:, u % 2, :], att_stat[:, 3, u:u + 1], None, ALU.mult
                                  ).then_inc(sem("att_p"), 1)

            for u in range(ATT_HEADS * TT):
                att_max(u)
                att_norm(u)

            for br, gate in ((0, gate_a), (1, gate_b)):
                for j in range(2):
                    wait_done(dve, FIRST["branch"] + 2 * br + j)
                    o = (merged if br == 0 else gate_b)[:, 4 * j:4 * j + 4, :]
                    dve.tensor_tensor(o, banks(2 * j, 2).rearrange("p (a t) -> p a t", t=T), gate[:, 4 * j:4 * j + 4, :],
                                      ALU.mult).then_inc(sem("branch_taken"), 1)
            dve.wait_ge(sem("branch_taken"), 4)
            dve.tensor_tensor(merged, merged, gate_b, ALU.add).then_inc(sem("merged_ready"), 1)
            wait_done(dve, FIRST["w_out"] + 3)
            for k in range(KD):
                last = dve.scalar_tensor_tensor(h[:, k, :], ps[:, 4 + k // 2, (k % 2) * T:(k % 2) * T + T],
                                                mod[:, 2 * KD + k, 0:1], h[:, k, :], ALU.mult, ALU.add)
            last.then_inc(sem("h_updated"), 1)

            dve.wait_ge(sem("h_updated"), 7)
            normed(13, x_in, h[:, :, :], gain_mod[:, 2, :])
            dve.wait_ge(sem("router_scores"), 1)
            scores = ps[:, 1, 0:TT * EXPERTS].rearrange("p (t e) -> p t e", t=TT)
            step(dve.tensor_reduce(small[:, 8:10], scores, AX_X, ALU.max))
            settle()
            dve.tensor_tensor(aff_e, scores, small[:, 8:10].unsqueeze(2).to_broadcast([P, TT, EXPERTS]), ALU.subtract
                              ).then_inc(sem("logits_ready"), 1)
            dve.wait_ge(sem("aff_exp"), 1)
            step(dve.tensor_reduce(small[:, 10:12], aff_e, AX_X, ALU.add))
            settle()
            step(dve.reciprocal(small[:, 12:14], small[:, 10:12]))
            settle()
            dve.tensor_tensor(aff, aff_e, small[:, 12:14].unsqueeze(2).to_broadcast([P, TT, EXPERTS]), ALU.mult
                              ).then_inc(sem("aff_ready"), 1)
            dve.wait_ge(sem("aff_turned"), 1)
            E16 = slice(0, EXPERTS)
            step(dve.tensor_copy(aff_t[E16, :], ps[E16, 0, 0:T]))
            src, other = aff_t, (work_a, work_b)
            for i in range(CAP // 8):
                settle()
                step(dve.max(top8[E16, :], src[E16, :]))
                settle()
                dst = other[i % 2]
                step(dve.match_replace(dst[E16, :], top8[E16, :], src[E16, :], -1.0))
                src = dst
            settle()
            step(dve.tensor_scalar(chosen[E16, :], src[E16, :], 0.0, None, ALU.is_lt))
            settle()
            step(dve.tensor_tensor_scan(slot_t[E16, :], ones[E16, :], chosen[E16, :], 0.0, ALU.mult, ALU.add))
            settle()
            dve.tensor_tensor(slot_t[E16, :], slot_t[E16, :], chosen[E16, :], ALU.mult).then_inc(sem("slots_chosen"), 1)
            dve.wait_ge(sem("slots_turned"), 1)
            step(dve.tensor_copy(slot_tok.rearrange("p t e -> p (t e)"), ps[:, 1, 0:TT * EXPERTS]))
            settle()
            iota = const("iota").unsqueeze(1).to_broadcast([P, EXPERTS, CAP])
            for t in range(TT):
                step(dve.tensor_tensor(pick[:, t, :].rearrange("p (e s) -> p e s", e=EXPERTS), iota,
                                       slot_tok[:, t, :].unsqueeze(2).to_broadcast([P, EXPERTS, CAP]), ALU.is_equal))
            settle()
            for t in range(TT):
                last = dve.tensor_tensor(pick_gate[:, t, :].rearrange("p (e s) -> p e s", e=EXPERTS),
                                         pick[:, t, :].rearrange("p (e s) -> p e s", e=EXPERTS),
                                         aff[:, t, :].unsqueeze(2).to_broadcast([P, EXPERTS, CAP]), ALU.mult)
            last.then_inc(sem("pick_ready"), 1)
            for i in range(EXPERTS // 2):
                dve.wait_ge(sem("spread_turned"), i + 1)
                dve.tensor_copy(spread[:, 2 * i:2 * i + 2, :].rearrange("p e t -> p (e t)"), ps[0:64, i % 4, :]
                                ).then_inc(sem("spread_taken"), 1)

            with dve.Fori(0, EXPERTS) as e:
                dve.wait_ge(sem("half_g_ready"), e + 1)
                dve.tensor_tensor(gate_sum[0:64, :], ps[0:64, 4, :], half_g[0:64, :], ALU.add
                                  ).then_inc(sem("gate_sum_ready"), 1)
                dve.wait_ge(sem("half_u_ready"), e + 1)
                dve.tensor_tensor(up_sum[0:64, :], ps[0:64, 5, :], half_u[0:64, :], ALU.add).then_inc(sem("up_sum_ready"), 1)
                dve.wait_ge(sem("up_sum_ready"), e + 1)
                dve.wait_ge(sem("gate_act_ready"), e + 1)
                dve.tensor_tensor(hid_e[0:64, :], gate_act[0:64, :], up_sum[0:64, :], ALU.mult).then_inc(sem("hid_ready"), 1)
                dve.wait_ge(sem("half_y_ready"), e + 1)
                dve.tensor_tensor(y_e[0:64, :], ps[0:64, 6, :], half_y[0:64, :], ALU.add).then_inc(sem("y_ready"), 1)
            dve.wait_ge(sem("spread_free"), EXPERTS + 1)
            for k in range(KD):
                last = dve.scalar_tensor_tensor(h[:, k, :], ps[:, k // 2, (k % 2) * T:(k % 2) * T + T],
                                                mod[:, 5 * KD + k, 0:1], h[:, k, :], ALU.mult, ALU.add)
            last.then_inc(sem("h_updated"), 1)
            dve.wait_ge(sem("h_updated"), 8)
            r = ROWS_B["final_norm_g_2"]
            normed(14, x_in, h[:, :, :], vec_b[:, r:r + KD])


_INS = ['x', 'positions', 'ffn_norm1', 'ffn1_w1', 'ffn1_w3', 'ffn1_w2', 'mix_norm', 'ffn_norm2', 'ffn2_w1', 'ffn2_w3',
        'ffn2_w2', 'conv_w_pw1', 'conv_w_dw', 'conv_norm', 'conv_w_pw2', 'mla_w_a', 'mla_q_norm', 'mla_kv_norm',
        'mla_w_uq', 'mla_w_ukv', 'mla_w_o', 'final_norm', 'c_2', 'ctx_2', 'c_ctx_2', 'w_mod_2', 'b_mod_2', 'norm1_g_2',
        'norm2_g_2', 'w_in_2', 'hg_lb_logits_2', 'hg_norm_g_2', 'q_norm_g_2', 'k_norm_g_2', 'w_branch_a_2',
        'w_branch_b_2', 'w_out_2', 'w_router_2', 'w_exp_gate_2', 'w_exp_up_2', 'w_exp_down_2', 'final_norm_g_2']
_OUT = (1, T, D)


def kernel(**inputs):
    import concourse.bacc as bacc
    from concourse.bass_utils import run_bass_kernel_spmd

    nc = bacc.Bacc("TRN2", target_bir_lowering=False, num_devices=1)
    arrays = {f"in_{name}": np.ascontiguousarray(inputs[name]) for name in _INS}
    arrays["in_constants"], arrays["in_masks"] = CONSTANTS, MASKS
    args = [nc.dram_tensor(name, a.shape, mybir.dt.from_np(a.dtype), kind="ExternalInput").ap()
            for name, a in arrays.items()]
    args.append(nc.dram_tensor("out_0", _OUT, F32, kind="ExternalOutput").ap())
    build(nc, *args)
    r = run_bass_kernel_spmd(nc, [arrays], core_ids=[0])
    return r.results[0]["out_0"]
```

```python
from contextlib import ExitStack

import numpy as np
import concourse.bass as bass
from concourse import mybir

F32 = mybir.dt.float32
F32R = mybir.dt.float32r
I32 = mybir.dt.int32
U8 = mybir.dt.uint8
BF16 = mybir.dt.bfloat16
ALU = mybir.AluOpType
ACT = mybir.ActivationFunctionType
AX_X = mybir.AxisListType.X

P = 128
D = 1024
KD = D // P
T = 256
TT = T // P
FF = 2816
EPS = 1e-6

SLOTS = 6
SLOT = 2048
FF_CHUNK = 256
FF_STEPS = FF // FF_CHUNK

CONV_W = 31
MLA_HEADS, NOPE, ROPE, VH = 8, 128, 64, 128
Q_LORA, KV_LORA = 512, 256
MLA_SCALE = (NOPE + ROPE) ** -0.5
MASKED = -1e30
CHUNK = 64

N_MOD = 6
HG_HEADS = 4
ATT_HEADS, ATT_HD, ATT_KV = 8, 64, 2
ATT_SCALE = ATT_HD ** -0.5
EXPERTS, CAP, EFF = 16, 32, 1024
LEVELS = [64, 32, 16, 8, 4, 2, 1]
ROUND_WIDE, ROUND_DIAG = len(LEVELS), len(LEVELS) + 1
ROUNDS = len(LEVELS) + 2

STREAM = [("ffn0", 33), ("pw1", 8), ("mod", 24), ("pw2", 4), ("ffn1", 33), ("ffn2", 33), ("mla_a", 4), ("uq", 4),
          ("ukv", 2), ("mla_o", 4), ("ffn3", 33), ("w_in", 21), ("branch", 4), ("w_out", 4), ("experts", 12 * EXPERTS)]
FIRST = {}
_at = 0
for _name, _n in STREAM:
    FIRST[_name] = _at
    _at += _n

SPLIT = ("ffn0", "pw1", "pw2", "ffn1", "ffn2", "ffn3")
HALF_BUFS = 4
HALF = {}
for _name, _n in STREAM:
    if _name in SPLIT:
        for _s in range(_n):
            HALF[FIRST[_name] + _s] = 2 * len(HALF)
X_PIECES = {"ffn0": 4, "pw1": 2, "pw2": 2, "ffn1": 4, "ffn2": 4, "ffn3": 4}
X_BEFORE = {name: sum(list(X_PIECES.values())[:i]) for i, name in enumerate(X_PIECES)}
NORMS = ("ffn0", "conv_in", "context", "conv_out", "ffn1", "ffn2", "mla", "mla_q", "mla_kv", "ffn3", "final1", "tokens",
         "experts", "final2")
NORM = {name: i + 1 for i, name in enumerate(NORMS)}
SQ_PIECES = {name: 4 if name in ("conv_in", "mla", "final1", "tokens", "experts", "final2") else 1 for name in NORMS}
SQ_BEFORE = {name: sum(SQ_PIECES[m] for m in NORMS[:i]) for i, name in enumerate(NORMS)}
NORMED = ("conv_in", "conv_out", "context", "mla", "mla_q", "mla_kv", "tokens", "experts", "final2")
XN = {name: i + 1 for i, name in enumerate(NORMED)}
XN_HALF = {"conv_in": 1, "conv_out": 2}
UPDATES = {0: 0, 1: 2, 2: 3, 3: 5}

ROWS_FIRST = 32
ROWS_A = {"ffn_norm1": 0, "mix_norm": 16, "ffn_norm2": 32, "conv_norm": 48, "mla_q_norm": 56, "mla_kv_norm": 60,
          "final_norm": 62}
N_ROWS_A = 70
ROWS_B = {"c_2": 0, "c_ctx_2": 8, "b_mod_2": 16, "norm1_g_2": 64, "norm2_g_2": 72, "hg_lb_logits_2": 80,
          "hg_norm_g_2": 96, "final_norm_g_2": 100}
N_ROWS_B = 108

CONST = {}


def constant_table():
    p = np.arange(P)
    parts = {
        "ident": np.eye(P),
        "ones": np.ones((P, T)),
        "headsum": (p[:, None] // ATT_HD == p[None, :] // ATT_HD),
    }

    def rotation(half):
        m = np.zeros((P, P))
        for col in range(P):
            if col % (2 * half) < half:
                m[col + half, col] = -1.0
            else:
                m[col - half, col] = 1.0
        return m

    parts["rope_rot"] = rotation(ROPE // 2)
    parts["axial_rot"] = rotation(ATT_HD // 4)
    rows = np.repeat(np.arange(T // 64, dtype=np.float32), 64)
    cols = np.tile(np.arange(64, dtype=np.float32), T // 64)
    axis_dim = ATT_HD // 2
    freq = (np.float64(10000.0) ** (-np.arange(0, axis_dim, 2) / axis_dim)).astype(np.float32)
    d = p % ATT_HD
    ang = np.where((d // axis_dim == 0)[:, None], rows[None, :], cols[None, :]).astype(np.float32)
    ang = (ang * freq[d % (axis_dim // 2)][:, None]).astype(np.float32)
    parts["axial_cos"] = np.cos(ang.astype(np.float64))
    parts["axial_sin"] = np.sin(ang.astype(np.float64))
    parts["iota"] = np.tile(np.arange(1, CAP + 1), (P, 1))
    parts["cond_sel"] = (p[:, None] % 32 == np.arange(2)[None, :])
    parts["mask_rows"] = np.tile(p < CHUNK, (P, 1))
    parts["mask_cols"] = np.tile(np.where(p < CHUNK, 0.0, MASKED), (P, 1))
    parts["inv_freq"] = (np.float64(10000.0) ** (-2.0 * (p % (ROPE // 2)) / ROPE))[:, None]
    at = 0
    for name, a in parts.items():
        CONST[name] = (at, at + a.shape[1])
        at += a.shape[1]
    return np.concatenate([np.asarray(a, np.float64).astype(np.float32) for a in parts.values()], axis=1)


def level_masks():
    s, t = np.arange(P)[:, None], np.arange(P)[None, :]
    m = [(s // (2 * h) == t // (2 * h)) & (s // h != t // h) for h in LEVELS] + [s == t]
    return np.ascontiguousarray(np.stack(m, axis=1).astype(np.int32))


CONSTANTS = constant_table()
MASKS = level_masks()
TWO_PI = 2.0 * np.pi
PI_A = 6.28125
PI_B = float(np.float32(np.round((TWO_PI - PI_A) * 2.0 ** 20) / 2.0 ** 20))
PI_C = float(np.float32(TWO_PI - PI_A - PI_B))
ROUND_MAGIC = 1.5 * 2.0 ** 23
PI_LIMIT = 3.1415925


def build(nc, x, positions, ffn_norm1, ffn1_w1, ffn1_w3, ffn1_w2, mix_norm, ffn_norm2, ffn2_w1, ffn2_w3, ffn2_w2,
          conv_w_pw1, conv_w_dw, conv_norm, conv_w_pw2, mla_w_a, mla_q_norm, mla_kv_norm, mla_w_uq, mla_w_ukv,
          mla_w_o, final_norm, c_2, ctx_2, c_ctx_2, w_mod_2, b_mod_2, norm1_g_2, norm2_g_2, w_in_2,
          hg_lb_logits_2, hg_norm_g_2, q_norm_g_2, k_norm_g_2, w_branch_a_2, w_branch_b_2, w_out_2, w_router_2,
          w_exp_gate_2, w_exp_up_2, w_exp_down_2, final_norm_g_2, constants, masks, out):
    vectors_a = {"ffn_norm1": ffn_norm1, "mix_norm": mix_norm, "ffn_norm2": ffn_norm2, "conv_norm": conv_norm,
                 "mla_q_norm": mla_q_norm, "mla_kv_norm": mla_kv_norm, "final_norm": final_norm}
    vectors_b = {"c_2": c_2, "c_ctx_2": c_ctx_2, "b_mod_2": b_mod_2, "norm1_g_2": norm1_g_2, "norm2_g_2": norm2_g_2,
                 "hg_lb_logits_2": hg_lb_logits_2, "hg_norm_g_2": hg_norm_g_2, "final_norm_g_2": final_norm_g_2}

    def as_rows(a):
        names = " ".join("abc"[:len(a.shape)])
        flat = a if len(a.shape) == 1 else a.rearrange(f"{names} -> ({names})")
        return flat.rearrange("(r f) -> r f", f=P)

    with ExitStack() as ctx:
        def sb(name, shape, dt=F32):
            return ctx.enter_context(nc.sbuf_tensor(name, shape, dt))

        sems = {}

        def sem(name):
            if name not in sems:
                sems[name] = ctx.enter_context(nc.semaphore(name))
            return sems[name]

        ps = ctx.enter_context(nc.psum_tensor("banks", [P, 8, 512], F32))

        def banks(first, n):
            return ps[:, first:first + n, :].rearrange("p b c -> p (b c)")

        ring = sb("ring", [P, SLOTS, SLOT])
        h = sb("h", [P, KD, T])
        xn = sb("xn", [P, KD, 2 * T])
        squares = sb("squares", [P, KD, 2 * T])
        std = sb("std", [P, 2 * T])
        rstd = sb("rstd", [P, 2 * T])
        consts = sb("consts", [P, CONSTANTS.shape[1]])
        mask = sb("mask", [P, len(LEVELS) + 1, P], U8)
        vec_a = sb("vec_a", [P, N_ROWS_A])
        vec_b = sb("vec_b", [P, N_ROWS_B])
        qk_gain = sb("qk_gain", [P, 2])
        w_dw = sb("w_dw", [P, KD, CONV_W])
        mod = sb("mod", [P, N_MOD * KD, 2])
        gain_mod = sb("gain_mod", [P, 3, KD])
        tok = sb("tok", [P, TT, D])
        silu_gate = sb("silu_gate", [P, 2, 512])
        hidden = sb("hidden", [P, 2, 2, T])
        small = sb("small", [P, 64])
        router = sb("router", [P, KD, EXPERTS])
        pos_i = sb("pos_i", [P, T], I32)
        zero_w = sb("zero_w", [P, 512], BF16)
        eps_col = sb("eps_col", [P, 1])
        lb_tmp = sb("lb_tmp", [P, 3, 2, HG_HEADS])
        floor = sb("floor", [P, 2, 2, HG_HEADS])
        mla_stat = sb("mla_stat", [P, 4, MLA_HEADS, TT])
        att_stat = sb("att_stat", [P, 4, ATT_HEADS * TT])
        ARENA = 22100
        arena_at = -(-nc.sbuf_base // 32) * 32
        arena = sb("arena", [P, ARENA])
        LOW = (ARENA - HALF_BUFS * SLOT - 2 * KD * T - 8 * T) // 8 * 8

        def split_tensor(name, shape, first):
            return nc.alloc_sbuf_tensor_at(name, shape, F32R, offset=arena_at + 4 * first)

        w_split = split_tensor("w_split", [P, HALF_BUFS, 2, SLOT // 2], LOW)
        x_split = split_tensor("x_split", [P, 2, KD, T], LOW + HALF_BUFS * SLOT)
        hid_split = split_tensor("hid_split", [P, 2, 2, 2, T], LOW + HALF_BUFS * SLOT + 2 * KD * T)

        def const(name, rows=P):
            a, b = CONST[name]
            return consts[0:rows, a:b]

        ident, ones = const("ident"), const("ones")

        class Region:
            def __init__(self):
                self.at = 0

            def take(self, *shape, rows=P):
                n = int(np.prod(shape))
                view = arena[0:rows, self.at:self.at + n]
                self.at += n
                assert self.at <= ARENA, self.at
                names = [f"d{i}" for i in range(len(shape))]
                if len(shape) > 1:
                    sizes = dict(zip(names, shape))
                    view = view.rearrange(f"p ({' '.join(names)}) -> p {' '.join(names)}", **sizes)
                return view

        r0 = Region()
        rows_a, rows_b, rows_dw = r0.take(P, rows=N_ROWS_A), r0.take(P, rows=N_ROWS_B), r0.take(D, rows=CONV_W)
        mask_in = r0.take(len(LEVELS) + 1, P).bitcast(I32)
        r1 = Region()
        PAD = CONV_W - 1
        conv_in, conv_acc, glu_sig = r1.take(KD, PAD + T), r1.take(KD, T), r1.take(2, 2 * T)
        cond_pad, mod_rows = r1.take(KD, 32), r1.take(2, 512)
        DIAGS, PE_TILES = 8, 2
        diag = r1.take(DIAGS, P)
        assert max(r0.at, r1.at) <= LOW
        r2 = Region()
        latent, latent_n = r2.take(6, T), r2.take(6, T)
        q_nope, k_nope = r2.take(MLA_HEADS, T), r2.take(MLA_HEADS, T)
        rope_in, rope_a, rope_b = r2.take(5, T), r2.take(5, T), r2.take(5, T)
        v_tok, o_mla = r2.take(TT, MLA_HEADS, VH), r2.take(MLA_HEADS, T)
        mla_p, mla_pt = r2.take(2, 384), r2.take(2, 3, P)
        cos_t, sin_t, ang, turns, pos_f = (r2.take(T) for _ in range(5))
        r3 = Region()
        hg_q = r3.take(HG_HEADS, T)
        key_f, key_b = r3.take(HG_HEADS, 2 * T), r3.take(HG_HEADS, 2 * T)
        log_f, log_b = r3.take(HG_HEADS, 2 * T), r3.take(HG_HEADS, 2 * T)
        hg_v = r3.take(4, 512)
        att_q, att_k = r3.take(4, T), r3.take(ATT_KV, 2 * T)
        att_v = r3.take(4, P)
        gate_a, gate_b = r3.take(KD, T), r3.take(KD, T)
        pre_x, pre_c = r3.take(2, HG_HEADS, T + 1), r3.take(2, HG_HEADS, T + 1)
        hg_gate = silu_gate[:, :, :].rearrange("p a (b t) -> p (a b) t", t=T)
        state0 = hidden[:, :, :, :].rearrange("p a b t -> p (a b t)").rearrange("p (d h v) -> p d h v", d=2, h=HG_HEADS)
        decay = squares[:, :, :].rearrange("p k t -> p (k t)").rearrange("p (r d h t) -> p r d h t", r=2, d=2, h=HG_HEADS)
        q_lvl = log_f.rearrange("p a t -> p (a t)").rearrange("p (r h t) -> p r h t", r=2, h=HG_HEADS)
        k_lvl = log_b.rearrange("p a t -> p (a t)").rearrange("p (r h t) -> p r h t", r=2, h=HG_HEADS)
        hg_p = tok[:, :, :].rearrange("p s (h t) -> p s h t", h=HG_HEADS)
        key_dec = xn[:, :, 0:T].rearrange("p (d h) t -> p d h t", d=2)
        key_dec_t = decay[:, 1].rearrange("p d h t -> p (d h t)").rearrange("p (d s c) -> p d s c", d=2, s=TT)
        q_dec = decay[:, 0]
        o_sq = decay[:, 1, 0]
        o_hg = decay[:, 1, 1]
        att_rot = q_lvl.rearrange("p r h t -> p (r h t)")
        att_sq = k_lvl.rearrange("p r h t -> p (r h t)")
        att_qr = key_f.rearrange("p a t -> p (a t)")[:, 0:4 * T].rearrange("p (a t) -> p a t", t=T)
        att_kr = key_f.rearrange("p a t -> p (a t)")[:, 4 * T:8 * T].rearrange("p (a t) -> p a t", t=2 * T)
        att_p = key_b.rearrange("p a t -> p (a t)")[:, 0:1024].rearrange("p (r k) -> p r k", r=2)
        att_pt = key_b.rearrange("p a t -> p (a t)")[:, 1024:2048].rearrange("p (r k q) -> p r k q", r=2, k=4)
        att_rinv = pre_c.rearrange("p d h t -> p (d h t)")[:, 0:2048]
        o_att = hg_q
        merged = xn[:, :, 0:T]
        r4 = Region()
        x_exp = xn
        FIRST_EXPERTS = 4
        picks = r4.take(2 * TT, EXPERTS, CAP)
        pick_cur, x_cur, spread_cur = r4.take(TT, CAP), r4.take(KD, CAP), r4.take(T)
        half_g, half_u, half_y, gate_act = r4.take(512), r4.take(512), r4.take(512), r4.take(512)
        gate_sum, up_sum, hid_e, y_e = r4.take(512), r4.take(512), r4.take(512), r4.take(512)
        hid_t = r4.take(KD, CAP)
        aff, aff_e = r4.take(TT, EXPERTS), r4.take(TT, EXPERTS)
        aff_t, work_a, work_b, chosen, slot_t = (r4.take(T) for _ in range(5))
        slot_tok = r4.take(TT, EXPERTS)
        top8 = r4.take(8)
        AHEAD = SLOTS
        ahead = r4.take(AHEAD, SLOT)
        assert r4.at <= ARENA

        slot_full = [sem(f"slot_full_{i}") for i in range(SLOTS)]
        slot_free = sem("slot_free")
        half_done = sem("half_done")

        def wait_free(sp, n, more=0):
            if n >= SLOTS:
                sp.wait_ge(slot_free, n - SLOTS + 1 + more)

        def wait_full(pe, n, more=0):
            pe.wait_ge(slot_full[n % SLOTS], 16 * (n // SLOTS + 1) + more)

        def wait_done(eng, n, more=0):
            if n in HALF:
                eng.wait_ge(half_done, HALF[n] + 2 + more)
            else:
                eng.wait_ge(slot_free, n + 1 + more)

        def slot(n):
            return ring[:, n % SLOTS, :]

        def half_slot(n, o, columns):
            if columns:
                return slot(n).rearrange("p (k c) -> p k c", k=KD)[:, :, o * P:o * P + P]
            return slot(n)[:, o * D:o * D + D].rearrange("p (k c) -> p k c", k=KD)

        def half_part(n, o, part):
            return w_split[:, (HALF[n] + o) % HALF_BUFS, part, :].rearrange("p (k c) -> p k c", k=KD)

        w_ffn = [(ffn1_w1[0], ffn1_w3[0], ffn1_w2[0]), (ffn2_w1[0], ffn2_w3[0], ffn2_w2[0]),
                 (ffn1_w1[1], ffn1_w3[1], ffn1_w2[1]), (ffn2_w1[1], ffn2_w3[1], ffn2_w2[1])]

        PROJ = [("q", 0), ("q", 1), ("ff", 2), ("ff", 3), ("fb", 4), ("fb", 5), ("i", 6), ("i", 7), ("g", 8), ("g", 9),
                ("aq", 10), ("aq", 11), ("ak", 12), ("av", 12)] + [("ga", 13 + i) for i in range(4)] + \
               [("gb", 17 + i) for i in range(4)]
        ROUND_AT = 8
        PAIRS = 3
        LATER = 4
        EARLY = len(PROJ) - LATER
        LATER_BANK = (4, 2, 3, 7)
        LATER_UNIT = 3

        block = ctx.enter_context(nc.Block())

        @block.sync
        def _(sp):
            def load(n, src, view, more=0):
                wait_free(sp, n, more)
                sp.dma_start(view, src).then_inc(slot_full[n % SLOTS], 16)

            def cols(n, w, first, width, k_tiles):
                load(n, w.rearrange("(k p) c -> p k c", p=P)[:, :, first:first + width],
                     slot(n)[:, 0:k_tiles * width].rearrange("p (k c) -> p k c", k=k_tiles))

            sp.dma_start(consts[:, :], constants).then_inc(sem("consts_in"), 16)
            sp.dma_start(tok[:, :, :], x[0].rearrange("(t p) d -> p t d", p=P)).then_inc(sem("x_in"), 16)
            def rows_in(names):
                for name, rows, row, a in names:
                    src = as_rows(a)
                    sp.dma_start(rows[row:row + src.shape[0], :], src
                                 ).then_inc(sem("first_gains_in" if row < ROWS_FIRST and rows is rows_a else "rows_in"), 16)

            vectors = [(name, rows_a, row, vectors_a[name]) for name, row in ROWS_A.items()] + \
                      [(name, rows_b, row, vectors_b[name]) for name, row in ROWS_B.items()]
            rows_in(vectors[:2])

            def small_inputs():
                rows_in(vectors[2:])
                sp.dma_start(rows_dw, conv_w_dw[0]).then_inc(sem("rows_in"), 16)
                for j, g in enumerate((q_norm_g_2, k_norm_g_2)):
                    for half in range(2):
                        sp.dma_start(qk_gain[64 * half:64 * half + 64, j:j + 1], g.rearrange("a d -> d a")
                                     ).then_inc(sem("gains_in"), 16)
                sp.dma_start(mask_in, masks).then_inc(sem("masks_in"), 16)
                sp.dma_start(router[:, :, :], w_router_2[0].rearrange("(k p) e -> p k e", p=P)).then_inc(sem("router_in"), 16)
                sp.dma_start(pos_i[:, :], positions.partition_broadcast(P)).then_inc(sem("positions_in"), 16)
                sp.wait_ge(sem("x_turned"), 4)
                sp.dma_start(tok[:, :, :], ctx_2[0].rearrange("(t p) d -> p t d", p=P)).then_inc(sem("ctx_in"), 16)

            def ffn(f):
                n0 = FIRST[f"ffn{f}"]
                w1, w3, w2 = w_ffn[f]

                def up(n, w, c, more):
                    wait_free(sp, n, more)
                    src = w.rearrange("(k p) (s c) -> s p k c", p=P, c=FF_CHUNK)[bass.ds(c, 1)]
                    sp.dma_start(slot(n).rearrange("p (k c) -> p k c", k=KD),
                                 src.rearrange("o p k c -> p (o k) c")).then_inc(slot_full[n % SLOTS], 16)

                def down(n, c, more):
                    wait_free(sp, n, more)
                    src = w2.rearrange("(s k p) c -> s p k c", p=P, k=2)[bass.ds(c, 1)]
                    sp.dma_start(slot(n).rearrange("p (k c) -> p k c", k=2),
                                 src.rearrange("o p k c -> p (o k) c")).then_inc(slot_full[n % SLOTS], 16)

                up(n0, w1, 0, 0)
                up(n0 + 1, w3, 0, 0)
                if f == 0:
                    small_inputs()
                first = 2 if f == 0 else 0
                for c in range(first):
                    n = n0 + 2 + 3 * c
                    up(n, w1, c + 1, 0)
                    up(n + 1, w3, c + 1, 0)
                    down(n + 2, c, 0)
                with sp.Fori(0, (FF_STEPS - 1 - first) // 2) as i:
                    for j in range(first, first + 2):
                        n = n0 + 2 + 3 * j
                        up(n, w1, 2 * i + (1 + j), 6 * i)
                        up(n + 1, w3, 2 * i + (1 + j), 6 * i)
                        down(n + 2, 2 * i + j, 6 * i)
                down(n0 + 32, FF_STEPS - 1, 0)

            ffn(0)
            for j in range(KD):
                cols(FIRST["pw1"] + j, conv_w_pw1[0], D * (j % 2) + 256 * (j // 2), 256, KD)
            for c in range(12):
                for half in range(2):
                    n = FIRST["mod"] + 2 * c + half
                    load(n, w_mod_2[0].rearrange("(k p) c -> p k c", p=P)[:, 4 * half:4 * half + 4, 512 * c:512 * c + 512],
                         slot(n).rearrange("p (k c) -> p k c", k=4))
            for j in range(4):
                cols(FIRST["pw2"] + j, conv_w_pw2[0], 256 * j, 256, KD)
            ffn(1)
            ffn(2)
            for j in range(4):
                cols(FIRST["mla_a"] + j, mla_w_a[0], 256 * j, 256 if j < 3 else ROPE, KD)
            for j in range(4):
                cols(FIRST["uq"] + j, mla_w_uq[0].rearrange("c h d -> c (h d)"), 384 * j, 384, 4)
            for j in range(2):
                cols(FIRST["ukv"] + j, mla_w_ukv[0].rearrange("c h d -> c (h d)"), 1024 * j, 1024, 2)
            for j in range(4):
                cols(FIRST["mla_o"] + j, mla_w_o[0], 256 * j, 256, KD)
            ffn(3)
            for j in range(21):
                cols(FIRST["w_in"] + j, w_in_2[0], 256 * j, 256, KD)
            for j in range(2):
                cols(FIRST["branch"] + j, w_branch_a_2[0], 512 * j, 512, 4)
            for j in range(2):
                cols(FIRST["branch"] + 2 + j, w_branch_b_2[0], 512 * j, 512, 4)
            for j in range(4):
                cols(FIRST["w_out"] + j, w_out_2[0], 256 * j, 256, KD)
            exp_tiles = [w[0].rearrange("e (j k p) c -> j e p k c", p=P, k=2)[j]
                         for w in (w_exp_gate_2, w_exp_up_2, w_exp_down_2) for j in range(4)]
            def expert_slot(s, e, more=None):
                n = FIRST["experts"] + 12 * e + s
                view = slot(n).rearrange("p (k c) -> p k c", k=2)
                src = exp_tiles[s][e] if more is None else exp_tiles[s][e:][bass.ds(more, 1)].rearrange("o p k c -> p (o k) c")
                sp.dma_start(view, src).then_inc(slot_full[n % SLOTS], 16)

            for s in range(SLOTS):
                wait_free(sp, FIRST["experts"] + s)
                expert_slot(s, 0)
            sp.wait_ge(sem("merged_ready"), 1)
            for i in range(AHEAD):
                sp.dma_start(ahead[:, i, :].rearrange("p (k c) -> p k c", k=2), exp_tiles[SLOTS + i][0]
                             ).then_inc(sem(f"ahead_{i}"), 16)
            for s in range(SLOTS):
                sp.wait_ge(slot_free, FIRST["experts"] + s + 1)
                expert_slot(s, 1)
            with sp.Fori(0, EXPERTS - 2) as i:
                for s in range(12):
                    e, s = (1, s + 6) if s < 6 else (2, s - 6)
                    wait_free(sp, FIRST["experts"] + 12 * e + s, 12 * i)
                    expert_slot(s, e, i)
            for s in range(SLOTS, 12):
                wait_free(sp, FIRST["experts"] + 12 * (EXPERTS - 1) + s)
                expert_slot(s, EXPERTS - 1)
            for t in range(TT):
                sp.wait_ge(sem("rows_out"), 2 * t + 2)
                sp.dma_start(out[0].rearrange("(t p) d -> t p d", p=P)[t], tok[:, t, :]).then_inc(sem("stored"), 16)
            sp.wait_ge(sem("stored"), 16 * TT)

        @block.tensor
        def _(pe):
            mm = pe.matmul

            def done(ins):
                ins.then_inc(slot_free, 1)

            def wait_split(n, o, more_slots=0):
                if o == 0:
                    pe.wait_ge(sem("half_split"), HALF[n] // 2 + 1 + more_slots)
                else:
                    pe.wait_ge(slot_free, n + 1 + more_slots)

            def mm3(out_, n, o, k, moving, start, stop, **kw):
                hi, lo = half_part(n, o, 0)[:, k, :], half_part(n, o, 1)[:, k, :]
                mm(out_, hi, moving(0), start=start, stop=False, **kw)
                mm(out_, hi, moving(1), start=False, stop=False, **kw)
                return mm(out_, lo, moving(0), start=False, stop=stop, **kw)

            def wait_x(name, pieces=None):
                pe.wait_ge(sem("x_split_ready"), X_BEFORE[name] + (pieces or X_PIECES[name]))

            pe.wait_ge(sem("consts_in"), 16)
            pe.wait_ge(sem("x_in"), 16)
            for k in range(KD):
                for t in range(TT):
                    last = pe.transpose(ps[:, 2 + k // 2, (k % 2) * T + t * P:(k % 2) * T + t * P + P],
                                        tok[:, t, k * P:k * P + P], ident)
                if k % 2 == 1:
                    last.then_inc(sem("x_turned"), 1)
            pe.wait_ge(sem("first_gains_in"), 32)
            pe.transpose(ps[:, 0, 0:ROWS_FIRST], rows_a[0:ROWS_FIRST, :], ident[0:ROWS_FIRST, 0:ROWS_FIRST]
                         ).then_inc(sem("first_gains_turned"), 1)

            def sum_squares(m, k_tiles, n, bank, first=0):
                per = k_tiles // SQ_PIECES[m]
                for k in range(k_tiles):
                    if k % per == 0:
                        pe.wait_ge(sem("squares_ready"), SQ_BEFORE[m] + k // per + 1)
                    last = mm(ps[:, bank, 0:n], ones[:, 0:P], squares[:, first + k, 0:n],
                              start=(k == 0), stop=(k == k_tiles - 1))
                last.then_inc(sem("sumsq_ready"), 1)

            x_in = xn[:, :, T:2 * T]

            def ffn(f):
                n0 = FIRST[f"ffn{f}"]
                steps = FF_STEPS * f

                def up(n, bank, more, first=False):
                    for o in range(2):
                        wait_split(n, o, more)
                        for k in range(KD):
                            if first and o == 0 and k % 2 == 0:
                                wait_x(f"ffn{f}", k // 2 + 1)
                            last = mm3(ps[:, bank, o * T:o * T + T], n, o, k, lambda part: x_split[:, part, k, :],
                                       start=(k == 0), stop=(k == KD - 1))
                        last.then_inc(half_done, 1)

                def down(n, c, more_slot, more):
                    pe.wait_ge(sem("hid_split_ready"), steps + c + 1 + more)
                    for o in range(2):
                        wait_split(n, o, more_slot)
                        for d in range(KD):
                            last = mm3(ps[:, d // 2, (d % 2) * T:(d % 2) * T + T], n, o, d,
                                       lambda part: hid_split[:, c % 2, part, o, :],
                                       start=False, stop=False, skip_group_check=True)
                        last.then_inc(half_done, 1)

                up(n0, 4, 0, first=True)
                sum_squares(f"ffn{f}", KD, T, 7)
                if f > 0:
                    pe.wait_ge(sem("h_updated"), 4 * UPDATES[f])
                for b in range(4):
                    mm(banks(b, 1), zero_w[:, 0:P], zero_w[:, :], start=True, stop=False, skip_group_check=True)
                up(n0 + 1, 6, 0)
                pe.wait_ge(sem("rstd_ready"), NORM[f"ffn{f}"])
                with pe.Fori(0, FF_STEPS // 2) as i:
                    for j in range(2):
                        n = n0 + 2 + 3 * j
                        b = 4 + (1 + j) % 2
                        up(n, b, 6 * i)
                        up(n + 1, b + 2, 6 * i)
                        down(n + 2, j, 6 * i, 2 * i)
                down(n0 + 32, FF_STEPS - 1, 0, 0)

            def split_product(n, bank):
                for o in range(2):
                    wait_split(n, o)
                    for k in range(KD):
                        last = mm3(ps[:, bank, o * T:o * T + T], n, o, k, lambda part: x_split[:, part, k, :],
                                   start=(k == 0), stop=(k == KD - 1))
                    last.then_inc(half_done, 1)

            def square_product(name, n_slots, src, bank0=0, k_tiles=KD, half_cols=256):
                for j in range(n_slots):
                    n = FIRST[name] + j
                    wait_full(pe, n)
                    per = half_cols // P
                    for o in range(per):
                        tile = j * per + o
                        for k in range(k_tiles):
                            last = mm(ps[:, bank0 + tile // 2, (tile % 2) * T:(tile % 2) * T + T],
                                      slot(n)[:, k * half_cols + o * P:k * half_cols + o * P + P], src[:, k, :],
                                      start=(k == 0), stop=(k == k_tiles - 1))
                    done(last)

            pe.wait_ge(sem("gains_ready"), 1)
            ffn(0)

            sum_squares("conv_in", KD, T, 4)
            pe.wait_ge(sem("rows_in"), 16 * (len(ROWS_A) - 2 + len(ROWS_B) + 1))
            pe.transpose(ps[:, 5, 0:N_ROWS_B], rows_b, ident[0:N_ROWS_B, 0:N_ROWS_B])
            pe.transpose(ps[:, 5, N_ROWS_B:N_ROWS_B + N_ROWS_A], rows_a, ident[0:N_ROWS_A, 0:N_ROWS_A])
            for k in range(KD):
                last = pe.transpose(ps[:, 6, k * CONV_W:(k + 1) * CONV_W], rows_dw[:, k * P:k * P + P],
                                    ident[0:CONV_W, 0:CONV_W])
            last.then_inc(sem("rows_turned"), 1)
            wait_x("pw1")
            for j in range(KD):
                n = FIRST["pw1"] + j
                if j >= 4 and j % 2 == 0:
                    pe.wait_ge(sem("glu_ready"), j // 2 - 1)
                split_product(n, j % 4)
            def turn_mod(c):
                pe.wait_ge(sem("mod_copied"), c + 1)
                for b in range(4):
                    last = mm(ps[:, 4, T + 2 * (4 * c + b):T + 2 * (4 * c + b) + 2], mod_rows[:, c % 2, P * b:P * b + P],
                              const("cond_sel"), start=True, stop=True)
                last.then_inc(sem("mod_turned"), 1)

            taps = [(j, w) for j in range(KD - PE_TILES, KD) for w in range(CONV_W)]

            def tap(q):
                j, w = taps[q]
                pe.wait_ge(sem("diag_ready"), q + 1)
                if q == 0:
                    pe.wait_ge(sem("glu_ready"), KD // 2)
                c = (j - (KD - PE_TILES)) * T
                mm(ps[:, 7, c:c + T], diag[:, q % DIAGS, :], conv_in[:, j, w:w + T], start=(w == 0),
                   stop=(w == CONV_W - 1)).then_inc(sem("diag_used"), 1)

            pe.wait_ge(sem("cond_ready"), 1)
            for c in range(12):
                if c >= 2:
                    pe.wait_ge(sem("mod_copied"), c - 1)
                for half in range(2):
                    n = FIRST["mod"] + 2 * c + half
                    wait_full(pe, n)
                    for j in range(4):
                        last = mm(ps[32 * j:32 * j + 32, 5 + c % 2, :], cond_pad[:, 4 * half + j, :],
                                  slot(n)[:, 512 * j:512 * j + 512], start=(half == 0), stop=(half == 1))
                    done(last)
                if c >= 1:
                    turn_mod(c - 1)
                for q in range(len(taps) * c // 12, len(taps) * (c + 1) // 12):
                    tap(q)
            turn_mod(11)

            pe.wait_ge(sem("ctx_in"), 16)
            for k in range(KD):
                for t in range(TT):
                    last = pe.transpose(ps[:, k // 2, (k % 2) * T + t * P:(k % 2) * T + t * P + P],
                                        tok[:, t, k * P:k * P + P], ident)
            last.then_inc(sem("ctx_turned"), 1)
            sum_squares("context", KD, T, 4)

            sum_squares("conv_out", KD, T, 4)
            wait_x("pw2")
            pe.wait_ge(sem("squares_ready"), SQ_BEFORE["context"] + 1)
            for j in range(4):
                split_product(FIRST["pw2"] + j, j)

            pe.wait_ge(sem("mod_ready"), 3)
            ffn(1)
            ffn(2)

            sum_squares("mla", KD, T, 4)
            pe.wait_ge(sem("xn_ready"), XN["mla"])
            for j in range(4):
                n = FIRST["mla_a"] + j
                wait_full(pe, n)
                for o in range(2):
                    for k in range(KD):
                        if j < 3:
                            last = mm(ps[:, j, o * T:o * T + T], slot(n)[:, k * 256 + o * P:k * 256 + o * P + P],
                                      x_in[:, k, :], start=(k == 0), stop=(k == KD - 1))
                        else:
                            last = mm(ps[64 * o:64 * o + 64, j, 0:T], slot(n)[:, k * ROPE:k * ROPE + ROPE],
                                      x_in[:, k, :], start=(k == 0), stop=(k == KD - 1))
                done(last)
            sum_squares("mla_q", 4, T, 4)
            sum_squares("mla_kv", 2, T, 7, 4)
            pe.wait_ge(sem("xn_ready"), XN["mla_kv"])
            for j in range(4):
                n = FIRST["uq"] + j
                wait_full(pe, n)
                if j >= 2:
                    pe.wait_ge(sem("uq_taken"), j - 1)
                b = 5 if j % 2 == 0 else 0
                for o in range(2):
                    for k in range(4):
                        mm(ps[:, b, o * T:o * T + T], slot(n)[:, k * 384 + 192 * o:k * 384 + 192 * o + P],
                           latent_n[:, k, :], start=(k == 0), stop=(k == 3))
                for k in range(4):
                    for o in range(2):
                        c = k * 384 + 192 * o + NOPE
                        last = mm(ps[64 * o:64 * o + 64, b + 1, 0:T], slot(n)[:, c:c + ROPE], latent_n[:, k, :],
                                  start=(k == 0), stop=(k == 3))
                done(last)
            pe.wait_ge(sem("uq_taken"), 4)
            for j in range(2):
                n = FIRST["ukv"] + j
                wait_full(pe, n)
                if j == 1:
                    pe.wait_ge(sem("ukv_taken"), 1)
                for o in range(4):
                    for k in range(2):
                        mm(ps[:, o // 2, (o % 2) * T:(o % 2) * T + T], slot(n)[:, k * D + 256 * o:k * D + 256 * o + P],
                           latent_n[:, 4 + k, :], start=(k == 0), stop=(k == 1))
                for t in range(TT):
                    for k in range(2):
                        w = slot(n)[:, k * D:(k + 1) * D].rearrange("p (o c) -> p o c", o=4)[:, :, NOPE:NOPE + VH]
                        last = mm(ps[:, 2 + t, :], latent_n[:, 4 + k, t * P:t * P + P], w, start=(k == 0), stop=(k == 1))
                done(last)
            flat = rope_in.rearrange("p a t -> p (a t)")
            for c, (a, b) in enumerate(((0, 512), (512, 1024), (1024, 1280))):
                last = mm(ps[:, 5 + c, 0:b - a], const("rope_rot"), flat[:, a:b], start=True, stop=True)
            last.then_inc(sem("rope_turned"), 1)
            pe.wait_ge(sem("ukv_taken"), 2)
            pe.wait_ge(sem("rope_ready"), 1)

            def mla_scores(hd):
                if hd >= 2:
                    pe.wait_ge(sem("mla_exp"), 2 * (hd - 1))
                base = 64 * (hd % 2)
                for t in range(TT):
                    o = ps[:, hd % 2, P * t:P * t + P * (t + 1)]
                    keys = P * (t + 1)
                    mm(o, q_nope[:, hd, t * P:t * P + P], k_nope[:, hd, 0:keys], start=True, stop=False)
                    mm(o, rope_a[base:base + 64, hd // 2, t * P:t * P + P], rope_a[base:base + 64, 4, 0:keys],
                       start=False, stop=False)
                    last = mm(ps[:, hd % 2, 2 * t * P:2 * t * P + P],
                              const("mask_rows", 1), const("mask_cols", 1), start=False, stop=True)
                last.then_inc(sem("mla_scores"), 1)

            def mla_turn(hd):
                pe.wait_ge(sem("mla_p"), hd + 1)
                if hd >= 2:
                    pe.wait_ge(sem("mla_pt"), hd - 1)
                for b in range(3):
                    last = pe.transpose(ps[:, 2 + hd % 2, b * P:b * P + P], mla_p[:, hd % 2, b * P:b * P + P], ident)
                last.then_inc(sem("mla_turned"), 1)

            def mla_values(hd):
                pe.wait_ge(sem("mla_pt"), hd + 1)
                if hd >= 2:
                    pe.wait_ge(sem("mla_out_taken"), hd - 1)
                mm(ps[:, 4 + hd % 2, 0:T], v_tok[:, 0, hd, :],
                   mla_pt[:, hd % 2, 0:2, :].rearrange("p b q -> p (b q)"), start=True, stop=False)
                last = mm(ps[:, 4 + hd % 2, P:T], v_tok[:, 1, hd, :], mla_pt[:, hd % 2, 2, :], start=False, stop=True)
                last.then_inc(sem("mla_out"), 1)

            for i in range(MLA_HEADS + 2):
                if i < MLA_HEADS:
                    mla_scores(i)
                if 1 <= i <= MLA_HEADS:
                    mla_turn(i - 1)
                if i >= 2:
                    mla_values(i - 2)
            pe.wait_ge(sem("mla_out_taken"), MLA_HEADS)
            square_product("mla_o", 4, o_mla)

            ffn(3)

            sum_squares("final1", KD, T, 4)
            sum_squares("tokens", KD, T, 6)
            pe.wait_ge(sem("modulated"), 2)

            def hg_round(r):
                pe.wait_ge(sem("round_ready"), r + 1)
                if r >= 1:
                    pe.wait_ge(sem("round_taken"), r)
                for s in range(TT):
                    t = 1 - s if r == ROUND_WIDE else s
                    for hd in range(HG_HEADS):
                        q = hg_q if r == ROUND_DIAG else q_lvl[:, r % 2]
                        last = mm(ps[:, 6 + s, hd * P:hd * P + P], k_lvl[:, r % 2, hd, s * P:s * P + P],
                                  q[:, hd, t * P:t * P + P], start=True, stop=True)
                last.then_inc(sem("round_scores"), 1)

            def project(step):
                name, s = PROJ[step]
                n = FIRST["w_in"] + s
                b = 2 * (step % PAIRS) if step < EARLY else LATER_BANK[step - EARLY]
                wait_full(pe, n)
                if PAIRS <= step < EARLY:
                    pe.wait_ge(sem("proj_taken"), step - PAIRS + 1)
                if name in ("ff", "fb"):
                    for o in range(2):
                        for k in range(KD):
                            last = mm(ps[:, b + o, :], slot(n)[:, k * 256 + o * P:k * 256 + o * P + P], xn[:, k, :],
                                      start=(k == 0), stop=(k == KD - 1))
                elif name == "i":
                    for t in range(4):
                        for k in range(KD):
                            last = mm(ps[:, b + t // 2, (t % 2) * T:(t % 2) * T + T], xn[:, k, t * P:t * P + P],
                                      slot(n)[:, k * 256:k * 256 + 256], start=(k == 0), stop=(k == KD - 1))
                elif name == "ak":
                    for o in range(ATT_KV):
                        for k in range(KD):
                            for half in range(2):
                                c = k * 256 + o * ATT_HD
                                last = mm(ps[64 * half:64 * half + 64, b + o, :], slot(n)[:, c:c + ATT_HD], xn[:, k, :],
                                          start=(k == 0), stop=(k == KD - 1))
                elif name == "av":
                    for t in range(4):
                        for k in range(KD):
                            last = mm(ps[:, b, t * P:t * P + P], xn[:, k, t * P:t * P + P],
                                      slot(n)[:, k * 256 + P:k * 256 + 256], start=(k == 0), stop=(k == KD - 1))
                else:
                    for o in range(2):
                        for k in range(KD):
                            last = mm(ps[:, b, o * T:o * T + T], slot(n)[:, k * 256 + o * P:k * 256 + o * P + P],
                                      x_in[:, k, :], start=(k == 0), stop=(k == KD - 1))
                if name == "ak":
                    last.then_inc(sem("ak_product"), 1)
                else:
                    done(last)

            for step in range(EARLY):
                project(step)
                if step >= ROUND_AT and step - ROUND_AT < ROUNDS:
                    hg_round(step - ROUND_AT)

            pe.wait_ge(sem("proj_taken"), EARLY)
            project(EARLY)
            pe.wait_ge(sem("key_dec_ready"), 1)
            for dr in range(2):
                for s in range(TT):
                    for hd in range(HG_HEADS):
                        last = pe.transpose(ps[:, 2 * dr + s, hd * P:hd * P + P], key_dec[:, dr, hd, s * P:s * P + P], ident)
            last.then_inc(sem("key_dec_turned"), 1)
            pe.wait_ge(sem("proj_taken"), EARLY + 1)
            pe.wait_ge(sem("key_dec_t_ready"), 1)
            for dr in range(2):
                for hd in range(HG_HEADS):
                    for s in range(TT):
                        last = mm(ps[:, 4 + dr, hd * P:hd * P + P], key_dec_t[:, dr, s, hd * P:hd * P + P],
                                  hg_v[:, s, hd * P:hd * P + P], start=(s == 0), stop=(s == TT - 1))
            last.then_inc(sem("state_product"), 1)
            pe.wait_ge(sem("state_ready"), 1)
            pe.wait_ge(sem("round_taken"), ROUNDS)
            pe.wait_ge(sem("q_dec_ready"), 1)
            for hd in range(HG_HEADS):
                o = ps[:, hd // 2, (hd % 2) * T:(hd % 2) * T + T]
                for s in range(TT):
                    mm(o, hg_v[:, TT + s, hd * P:hd * P + P], hg_p[:, s, hd, :], start=(s == 0), stop=False)
                for dr in range(2):
                    last = mm(o, state0[:, dr, hd, :], q_dec[:, dr, hd, :], start=False, stop=(dr == 1))
            last.then_inc(sem("hg_out"), 1)
            pe.wait_ge(sem("hg_sq_ready"), 1)
            for c in range(2):
                last = mm(ps[:, 2 + c, :], ones[:, 0:P], o_sq[:, 2 * c:2 * c + 2, :].rearrange("p a t -> p (a t)"),
                          start=True, stop=True)
            last.then_inc(sem("hg_sumsq"), 1)

            pe.wait_ge(sem("att_sq_ready"), 1)
            for c in range(2):
                mm(ps[:, 4 + c, :], const("headsum"), att_sq[:, 512 * c:512 * c + 512], start=True, stop=True)
            pe.wait_ge(sem("round_taken"), ROUNDS)
            for c in range(2):
                last = mm(ps[:, 6 + c, :], const("headsum"), att_sq[:, 1024 + 512 * c:1536 + 512 * c], start=True, stop=True)
            last.then_inc(sem("att_sumsq"), 1)
            pe.wait_ge(sem("hg_log"), 1)
            project(EARLY + 1)
            pe.wait_ge(sem("att_n_ready"), 1)
            qf = att_qr.rearrange("p a t -> p (a t)")
            for c in range(2):
                mm(ps[:, 4 + c, :], const("axial_rot"), qf[:, 512 * c:512 * c + 512], start=True, stop=True)
            for o in range(ATT_KV):
                last = mm(ps[:, 6, o * T:o * T + T], const("axial_rot"), att_kr[:, o, T:2 * T], start=True, stop=True)
            last.then_inc(sem("att_turned"), 1)
            project(EARLY + 2)
            pe.wait_ge(sem("att_ready"), 1)
            pe.wait_ge(sem("hg_normed"), 1)
            pe.wait_ge(sem("proj_taken"), EARLY + 3)
            units = [(hd, t) for hd in range(ATT_HEADS) for t in range(TT)]

            def att_scores(u):
                hd, t = units[u]
                base = 64 * (hd % 2)
                if u >= 2:
                    pe.wait_ge(sem("att_exp"), u - 1)
                mm(ps[:, u % 2, :], att_qr[base:base + 64, hd // 2, t * P:t * P + P], att_kr[base:base + 64, hd // 4, :],
                   start=True, stop=True).then_inc(sem("att_scores"), 1)

            def att_turn(u):
                pe.wait_ge(sem("att_p"), u + 1)
                if u >= 2:
                    pe.wait_ge(sem("att_pt"), u - 1)
                for b in range(4):
                    last = pe.transpose(ps[:, 2 + u % 2, b * P:b * P + P], att_p[:, u % 2, b * P:b * P + P], ident)
                last.then_inc(sem("att_p_turned"), 1)

            def att_values(u):
                hd, t = units[u]
                base = 64 * (hd % 2)
                pe.wait_ge(sem("att_pt"), u + 1)
                pair = hd // 2
                for b in range(4):
                    last = mm(ps[base:base + 64, 4 + pair // 2, (pair % 2) * T + t * P:(pair % 2) * T + t * P + P],
                              att_v[:, b, (hd // 4) * ATT_HD:(hd // 4) * ATT_HD + ATT_HD], att_pt[:, u % 2, b, :],
                              start=(b == 0), stop=(b == 3))
                last.then_inc(sem("att_out"), 1)

            for i in range(len(units) + 2):
                if i < len(units):
                    att_scores(i)
                if i == LATER_UNIT:
                    project(EARLY + 3)
                if 1 <= i <= len(units):
                    att_turn(i - 1)
                if i >= 2:
                    att_values(i - 2)

            pe.wait_ge(sem("att_exp"), len(units))
            pe.wait_ge(sem("att_pt"), len(units))
            for br, src in ((0, o_hg), (1, o_att)):
                if br == 1:
                    pe.wait_ge(sem("o_att_ready"), 1)
                for j in range(2):
                    n = FIRST["branch"] + 2 * br + j
                    wait_full(pe, n)
                    if br == 1:
                        pe.wait_ge(sem("branch_taken"), j + 1)
                    for o in range(4):
                        for k in range(4):
                            last = mm(ps[:, 2 * j + o // 2, (o % 2) * T:(o % 2) * T + T],
                                      slot(n)[:, k * 512 + o * P:k * 512 + o * P + P], src[:, k, :],
                                      start=(k == 0), stop=(k == 3))
                    done(last)
            pe.wait_ge(sem("merged_ready"), 1)
            square_product("w_out", 4, merged, bank0=4)

            sum_squares("experts", KD, T, 0)
            pe.wait_ge(sem("modulated"), 3)
            pe.wait_ge(sem("router_in"), 16)
            for t in range(TT):
                for k in range(KD):
                    last = mm(ps[:, 1, t * EXPERTS:(t + 1) * EXPERTS], x_in[:, k, t * P:t * P + P], router[:, k, :],
                              start=(k == 0), stop=(k == KD - 1))
            last.then_inc(sem("router_scores"), 1)
            for k in range(KD):
                for t in range(TT):
                    last = pe.transpose(ps[:, 4 + 2 * t + k // 4, (k % 4) * P:(k % 4) * P + P],
                                        x_in[:, k, t * P:t * P + P], ident)
            last.then_inc(sem("rows_back"), 1)
            pe.wait_ge(sem("aff_ready"), 1)
            for t in range(TT):
                last = pe.transpose(ps[0:EXPERTS, 0, t * P:t * P + P], aff[:, t, :], ident)
            last.then_inc(sem("aff_turned"), 1)
            pe.wait_ge(sem("slots_chosen"), 1)
            for t in range(TT):
                last = pe.transpose(ps[:, 1, t * EXPERTS:(t + 1) * EXPERTS], slot_t[0:EXPERTS, t * P:t * P + P],
                                    ident[0:EXPERTS, 0:EXPERTS])
            last.then_inc(sem("slots_turned"), 1)
            pe.wait_ge(sem("pick_ready"), 1)
            pe.wait_ge(sem("rows_copied"), 1)
            for b in range(4):
                mm(banks(b, 1), zero_w[:, 0:P], zero_w[:, :], start=True, stop=False, skip_group_check=True)

            def gather(k, bank, column, first, n):
                o = ps[:, bank, column:column + n * CAP]
                for t in range(TT):
                    last = mm(o, tok[:, t, k * P:k * P + P], picks[:, t, first:first + n, :], start=(t == 0),
                              stop=(t == TT - 1))
                return last

            def spread(more, e):
                pe.wait_ge(sem("pick_cur_ready"), more + (e + 1))
                for t in range(TT):
                    for g in (0, 32):
                        last = mm(ps[g:g + 32, 7, T + t * P:T + t * P + P], pick_cur[:, t, :], ident, start=True, stop=True)
                last.then_inc(sem("spread_turned"), 1)

            def expert(more, e, take, first=False, final=False):
                def product(m, j, src):
                    w = take(4 * m + j)
                    for k in range(2):
                        for half in range(2):
                            g = 32 * (2 * k + half)
                            last = mm(ps[g:g + 32, 4 + m, :], src[:, 2 * j + k, :],
                                      w[:, k * D + 512 * half:k * D + 512 * half + 512],
                                      start=(j == 0), stop=(j == 3))
                    done(last)

                pe.wait_ge(sem("x_cur_ready"), more + (e + 1))
                pe.wait_ge(sem("x_exp_taken"), 2 if first else 2 + KD)
                for m in range(2):
                    for j in range(4):
                        product(m, j, x_cur)
                pe.wait_ge(sem("hid_ready"), more + (e + 1))
                pe.wait_ge(sem("spread_cur_ready"), more + (e + 1))
                for c in range(4):
                    last = mm(ps[:, 7, 64 * c:64 * c + 64], hid_e[0:64, P * c:P * c + P], ident[0:64, 0:64],
                              start=True, stop=True)
                last.then_inc(sem("hid_turned"), 1)
                pe.wait_ge(sem("hid_t_ready"), more + (e + 1))
                for j in range(4):
                    if j == 2 and not final:
                        spread(more, e + 1)
                        if first:
                            gather_others()
                    product(2, j, hid_t)
                pe.wait_ge(sem("y_ready"), more + (e + 1))
                for d in range(KD):
                    half = d // 4
                    last = mm(ps[:, d // 2, (d % 2) * T:(d % 2) * T + T],
                              y_e[32 * half:32 * half + 32, (d % 4) * P:(d % 4) * P + P],
                              spread_cur[32 * half:32 * half + 32, :], start=False, stop=False, skip_group_check=True)
                last.then_inc(sem("spread_free"), 1)

            def take_first(s):
                if s < SLOTS:
                    wait_full(pe, FIRST["experts"] + s)
                    return slot(FIRST["experts"] + s)
                pe.wait_ge(sem(f"ahead_{s - SLOTS}"), 16)
                return ahead[:, s - SLOTS, :]

            def gather_others():
                for k in range(KD):
                    if k >= 2:
                        pe.wait_ge(sem("x_exp_taken"), 2 + k - 1)
                    gather(k, 4 + k % 2, 0, FIRST_EXPERTS, EXPERTS - FIRST_EXPERTS).then_inc(sem("x_exp_product"), 1)

            for k in range(KD):
                last = gather(k, 4 + k // 4, (k % 4) * P, 0, FIRST_EXPERTS)
                if k % 4 == 3:
                    last.then_inc(sem("x_exp_product"), 1)
            spread(0, 0)
            expert(0, 0, take_first, first=True)

            def take_later(s, more, e):
                n = FIRST["experts"] + 12 * e + s
                wait_full(pe, n - AHEAD, more * 32)
                return slot(n)

            with pe.Fori(0, EXPERTS - 2) as i:
                expert(i, 1, lambda s: take_later(s, i, 1))
            expert(0, EXPERTS - 1, lambda s: take_later(s, 0, EXPERTS - 1), final=True)

            sum_squares("final2", KD, T, 4)
            pe.wait_ge(sem("xn_ready"), XN["final2"])
            for t in range(TT):
                for k in range(KD):
                    last = pe.transpose(ps[:, 2 * t + k // 4, (k % 4) * P:(k % 4) * P + P], x_in[:, k, t * P:t * P + P], ident)
                    if k % 4 == 3:
                        last.then_inc(sem("out_turned"), 1)

        @block.scalar
        def _(act):
            fn = act.activation

            for piece in range(4):
                act.wait_ge(sem("x_turned"), piece + 1)
                fn(h[:, 2 * piece:2 * piece + 2, :].rearrange("p k t -> p (k t)"), ps[:, 2 + piece, :], ACT.Copy
                   ).then_inc(sem("h_loaded"), 1)
            act.wait_ge(sem("gains_ready"), 1)

            def square(src, first, n):
                k_tiles = src.shape[1]
                fn(squares[:, first:first + k_tiles, 0:n], src, ACT.Square).then_inc(sem("squares_ready"), 1)

            def square_pieces(count, before):
                for piece in range(4):
                    act.wait_ge(sem(count), before + piece + 1)
                    square(h[:, 2 * piece:2 * piece + 2, :], 2 * piece, T)

            def root(m, bank, dim, region=0, n=T):
                act.wait_ge(sem("sumsq_ready"), NORM[m])
                fn(std[:, region:region + n], ps[:, bank, 0:n], ACT.Ln, bias=eps_col[:, 0:1],
                   scale=1.0 / dim).then_inc(sem("log_ready"), 1)
                act.wait_ge(sem("log_ready"), NORM[m])
                fn(rstd[:, region:region + n], std[:, region:region + n], ACT.Exp, scale=-0.5
                   ).then_inc(sem("rstd_ready"), 1)

            x_in = xn[:, :, T:2 * T]

            def split_hi(n, o, columns=True, more_halves=0, more_full=0):
                q = HALF[n] + o
                if q >= HALF_BUFS:
                    act.wait_ge(half_done, q - HALF_BUFS + 1 + more_halves)
                if o == 0:
                    if n >= 1 and n - 1 not in HALF:
                        act.wait_ge(slot_free, n)
                    wait_full(act, n, more_full)
                fn(half_part(n, o, 0), half_slot(n, o, columns), ACT.Copy).then_inc(sem("half_hi"), 1)

            def split_hi_slot(n, columns=True):
                for o in range(2):
                    split_hi(n, o, columns)

            def x_hi(norm):
                for g in range(2):
                    if g == 0:
                        act.wait_ge(sem("xn_half"), XN_HALF[norm])
                    else:
                        act.wait_ge(sem("xn_ready"), XN[norm])
                    fn(x_split[:, 0, 4 * g:4 * g + 4, :], x_in[:, 4 * g:4 * g + 4, :], ACT.Copy).then_inc(sem("x_hi"), 1)

            def ffn(f, gain):
                n0 = FIRST[f"ffn{f}"]
                steps = FF_STEPS * f
                split_hi_slot(n0)
                for k in range(KD):
                    if k % 2 == 0 and f > 0:
                        act.wait_ge(sem("h_updated"), 4 * (UPDATES[f] - 1) + k // 2 + 1)
                    ins = fn(x_split[:, 0, k, :], h[:, k, :], ACT.Copy, scale=gain[:, k:k + 1])
                    if k % 2 == 1:
                        ins.then_inc(sem("x_hi"), 1)
                split_hi(n0 + 1, 0)
                square(h[:, :, :], 0, T)
                split_hi(n0 + 1, 1)
                root(f"ffn{f}", 7, D)

                def gate(c, more):
                    act.wait_ge(sem("gate_scaled"), steps + c + 1 + more)
                    fn(silu_gate[:, c % 2, :], silu_gate[:, c % 2, :], ACT.Silu).then_inc(sem("silu_ready"), 1)

                def hidden_hi(c, more):
                    act.wait_ge(sem("hidden_ready"), steps + c + 1 + more)
                    fn(hid_split[:, c % 2, 0, :, :], hidden[:, c % 2, :, :], ACT.Copy).then_inc(sem("hid_hi"), 1)

                gate(0, 0)
                with act.Fori(0, FF_STEPS // 2) as i:
                    for j in range(2):
                        n = n0 + 2 + 3 * j
                        for s in range(3):
                            for o in range(2):
                                split_hi(n + s, o, s < 2, 12 * i, 16 * i)
                            if s == 0:
                                hidden_hi(j, 2 * i)
                        gate(1 + j, 2 * i)
                split_hi_slot(n0 + 32, columns=False)
                hidden_hi(FF_STEPS - 1, 0)

            def gains(name, layer):
                return vec_a[:, ROWS_A[name] + KD * layer:ROWS_A[name] + KD * layer + KD]

            def shift(m, c, half):
                act.wait_ge(sem("xn_ready"), XN[m])
                for k in range(KD):
                    o = xn[:, k, half * T:half * T + T]
                    last = fn(o, o, ACT.Identity, bias=mod[:, k, c:c + 1])
                last.then_inc(sem("modulated"), 1)

            act.wait_ge(sem("h_loaded"), 4)
            ffn(0, gains("ffn_norm1", 0))

            split_hi_slot(FIRST["pw1"])
            square_pieces("h_updated", 0)
            split_hi_slot(FIRST["pw1"] + 1)
            root("conv_in", 4, D)
            x_hi("conv_in")
            act.wait_ge(sem("vectors_ready"), 1)
            fn(cond_pad[:, :, 0:2], vec_b[:, 0:2 * KD].rearrange("p (c k) -> p k c", c=2), ACT.Silu
               ).then_inc(sem("cond_ready"), 1)
            for i in range(KD // 2):
                if i < KD // 2 - 1:
                    split_hi_slot(FIRST["pw1"] + 2 * i + 2)
                    split_hi_slot(FIRST["pw1"] + 2 * i + 3)
                wait_done(act, FIRST["pw1"] + 2 * i + 1)
                if i >= 2:
                    act.wait_ge(sem("glu_ready"), i - 1)
                fn(glu_sig[:, i % 2, :], ps[:, (2 * i + 1) % 4, :], ACT.Sigmoid).then_inc(sem("glu_sig_ready"), 1)
            taps = [(j, w) for j in range(KD - PE_TILES, KD) for w in range(CONV_W)]
            for c in range(12):
                for q in range(len(taps) * c // 12, len(taps) * (c + 1) // 12):
                    j, w = taps[q]
                    if q >= DIAGS:
                        act.wait_ge(sem("diag_used"), q - DIAGS + 1)
                    fn(diag[:, q % DIAGS, :], ident, ACT.Copy, scale=w_dw[:, j, w:w + 1]).then_inc(sem("diag_ready"), 1)
                wait_done(act, FIRST["mod"] + 2 * c + 1)
                if c >= 2:
                    act.wait_ge(sem("mod_turned"), c - 1)
                fn(mod_rows[:, c % 2, :], ps[:, 5 + c % 2, :], ACT.Copy).then_inc(sem("mod_copied"), 1)
            split_hi_slot(FIRST["pw2"])
            split_hi_slot(FIRST["pw2"] + 1)
            act.wait_ge(sem("diag_used"), PE_TILES * CONV_W)
            fn(conv_acc[:, KD - PE_TILES:KD, :].rearrange("p k t -> p (k t)"), ps[:, 7, 0:PE_TILES * T], ACT.Copy
               ).then_inc(sem("taps_copied"), 1)
            act.wait_ge(sem("ctx_turned"), 1)
            fn(xn[:, :, 0:T], banks(0, 4).rearrange("p (k t) -> p k t", t=T), ACT.Copy).then_inc(sem("ctx_copied"), 1)
            square(banks(0, 4).rearrange("p (k t) -> p k t", t=T), 0, T)
            root("context", 4, D, region=T)
            act.wait_ge(sem("taps_copied"), 1)
            act.wait_ge(sem("conv_done"), KD - PE_TILES)
            square(conv_acc, 0, T)
            root("conv_out", 4, D)
            for g in range(2):
                if g == 0:
                    act.wait_ge(sem("xn_half"), XN_HALF["conv_out"])
                else:
                    act.wait_ge(sem("xn_ready"), XN["conv_out"])
                x_g = x_in[:, 4 * g:4 * g + 4, :]
                fn(x_split[:, 0, 4 * g:4 * g + 4, :], x_g, ACT.Silu)
                fn(x_g, x_g, ACT.Silu).then_inc(sem("x_hi"), 1)
            split_hi_slot(FIRST["pw2"] + 2)
            split_hi_slot(FIRST["pw2"] + 3)
            act.wait_ge(sem("floor_logits"), 1)
            fn(lb_tmp[:, 0:2], lb_tmp[:, 0:2], ACT.Exp).then_inc(sem("floor_exp"), 1)
            shift("context", 1, 0)
            ffn(1, gains("ffn_norm2", 0))
            ffn(2, gains("ffn_norm1", 1))

            square_pieces("h_updated", 4 * 3)
            root("mla", 4, D)
            act.wait_ge(sem("angles_ready"), 1)
            fn(sin_t, ang, ACT.Sin).then_inc(sem("trig_ready"), 1)
            fn(cos_t, turns, ACT.Sin).then_inc(sem("trig_ready"), 1)
            wait_done(act, FIRST["mla_a"] + 1)
            square(banks(0, 2).rearrange("p (k t) -> p k t", t=T), 0, T)
            wait_done(act, FIRST["mla_a"] + 2)
            square(banks(2, 1).rearrange("p (k t) -> p k t", t=T), 4, T)
            wait_done(act, FIRST["mla_a"] + 3)
            fn(rope_in[:, 4, :], ps[:, 3, 0:T], ACT.Copy)
            root("mla_q", 4, Q_LORA)
            root("mla_kv", 7, KV_LORA, region=T)
            for j in range(4):
                b = 5 if j % 2 == 0 else 0
                wait_done(act, FIRST["uq"] + j)
                fn(q_nope[:, 2 * j:2 * j + 2, :].rearrange("p a t -> p (a t)"), ps[:, b, :], ACT.Copy)
                fn(rope_in[:, j, :], ps[:, b + 1, 0:T], ACT.Copy).then_inc(sem("uq_taken"), 1)
            for j in range(2):
                wait_done(act, FIRST["ukv"] + j)
                fn(k_nope[:, 4 * j:4 * j + 4, :].rearrange("p a t -> p (a t)"), banks(0, 2), ACT.Copy)
                fn(v_tok[:, :, 4 * j:4 * j + 4, :].rearrange("p s a v -> p s (a v)"), ps[:, 2:4, :], ACT.Copy
                   ).then_inc(sem("ukv_taken"), 1)

            def mla_exp(hd):
                act.wait_ge(sem("mla_max"), hd + 1)
                if hd >= 2:
                    act.wait_ge(sem("mla_turned"), hd - 1)
                for t in range(TT):
                    a, b = (0, P) if t == 0 else (P, 3 * P)
                    fn(mla_p[:, hd % 2, a:b], ps[:, hd % 2, a:b], ACT.Exp, bias=mla_stat[:, 0, hd, t:t + 1],
                       scale=MLA_SCALE, accum_out=mla_stat[:, 1, hd, t:t + 1]).then_inc(sem("mla_exp"), 1)

            def mla_copy(hd):
                act.wait_ge(sem("mla_turned"), hd + 1)
                if hd >= 2:
                    act.wait_ge(sem("mla_out"), hd - 1)
                fn(mla_pt[:, hd % 2, :, :].rearrange("p b q -> p (b q)"), ps[:, 2 + hd % 2, 0:3 * P], ACT.Copy
                   ).then_inc(sem("mla_pt"), 1)

            for i in range(MLA_HEADS + 1):
                if i < MLA_HEADS:
                    mla_exp(i)
                if i >= 1:
                    mla_copy(i - 1)
            ffn(3, gains("ffn_norm2", 1))

            square_pieces("h_updated", 4 * 5)
            root("final1", 4, D)
            square_pieces("h_normed", 0)
            root("tokens", 6, D)
            shift("tokens", 0, 1)

            def decay_exp(r):
                act.wait_ge(sem("decay_ready"), r + 1)
                d = decay[:, r % 2].rearrange("p d h t -> p (d h t)")
                fn(d, d, ACT.Exp).then_inc(sem("decay_exp"), 1)

            def taken(step):
                name, s = PROJ[step]
                b = 2 * (step % PAIRS) if step < EARLY else LATER_BANK[step - EARLY]
                if name == "ak":
                    act.wait_ge(sem("ak_product"), 1)
                else:
                    wait_done(act, FIRST["w_in"] + s)
                one, two = ps[:, b, :], ps[:, b:min(b + 2, 8), :]
                i = s % 2 if s < 12 else 0
                if name == "q":
                    last = fn(hg_q[:, 2 * s:2 * s + 2, :].rearrange("p a t -> p (a t)"), one, ACT.Copy)
                elif name in ("ff", "fb"):
                    key, log = (key_f, log_f) if name == "ff" else (key_b, log_b)
                    fn(key[:, 2 * i:2 * i + 2, :], two, ACT.Sigmoid, scale=-1.0)
                    last = fn(log[:, 2 * i:2 * i + 2, :], two, ACT.Sigmoid)
                elif name == "i":
                    last = fn(hg_v[:, :, 256 * i:256 * i + 256].rearrange("p (b t) c -> p b t c", b=2),
                              two.rearrange("p b (t c) -> p b t c", c=256), ACT.Copy)
                elif name == "g":
                    last = fn(hg_gate[:, 2 * i:2 * i + 2, :].rearrange("p a t -> p (a t)"), one, ACT.Silu)
                elif name == "aq":
                    last = fn(att_q[:, 2 * i:2 * i + 2, :].rearrange("p a t -> p (a t)"), one, ACT.Copy)
                elif name == "ak":
                    last = fn(att_k, two, ACT.Copy)
                elif name == "av":
                    last = fn(att_v.rearrange("p b c -> p (b c)"), one, ACT.Copy)
                else:
                    g, i = (gate_a, s - 13) if name == "ga" else (gate_b, s - 17)
                    last = fn(g[:, 2 * i:2 * i + 2, :].rearrange("p a t -> p (a t)"), one, ACT.Sigmoid)
                last.then_inc(sem("proj_taken"), 1)

            for step in range(EARLY):
                taken(step)
                if step == 5:
                    act.wait_ge(sem("proj_taken"), 6)
                    for dr, log in ((0, log_f), (1, log_b)):
                        for hd in range(HG_HEADS):
                            fn(log[:, hd, :], log[:, hd, :], ACT.Ln, bias=floor[:, 0, dr, hd:hd + 1],
                               scale=floor[:, 1, dr, hd:hd + 1]).then_inc(sem("forget_ready"), 1)
                if step >= ROUND_AT - 2 and step - (ROUND_AT - 2) < ROUNDS - 1:
                    decay_exp(step - (ROUND_AT - 2))

            act.wait_ge(sem("round_ready"), ROUND_WIDE)
            fn(q_dec[:, 0], pre_x[:, 0, :, 1:T + 1], ACT.Exp).then_inc(sem("q_dec_exp"), 1)
            act.wait_ge(sem("end_ready"), 1)
            fn(q_dec[:, 1], q_dec[:, 1], ACT.Exp).then_inc(sem("q_dec_exp"), 1)
            fn(key_dec[:, 0], key_dec[:, 0], ACT.Exp).then_inc(sem("key_dec_exp"), 1)
            fn(key_dec[:, 1], pre_c[:, 1, :, 0:T], ACT.Exp).then_inc(sem("key_dec_exp"), 1)
            taken(EARLY)
            act.wait_ge(sem("key_dec_turned"), 1)
            fn(key_dec_t.rearrange("p d s c -> p (d s c)"), banks(0, 4), ACT.Copy).then_inc(sem("key_dec_t_ready"), 1)
            act.wait_ge(sem("state_product"), 1)
            fn(state0.rearrange("p d h v -> p (d h v)"), banks(4, 2), ACT.Copy).then_inc(sem("state_ready"), 1)
            act.wait_ge(sem("round_scores"), ROUNDS)
            fn(att_sq[:, 0:4 * T], att_q.rearrange("p a t -> p (a t)"), ACT.Square)
            fn(att_sq[:, 4 * T:8 * T], att_k.rearrange("p a t -> p (a t)"), ACT.Square).then_inc(sem("att_sq_ready"), 1)
            act.wait_ge(sem("hg_out"), 1)
            act.wait_ge(sem("round_ready"), ROUNDS)
            fn(o_sq.rearrange("p a t -> p (a t)"), banks(0, 2), ACT.Square).then_inc(sem("hg_sq_ready"), 1)
            act.wait_ge(sem("hg_sumsq"), 1)
            o_flat = o_hg.rearrange("p a t -> p (a t)")
            fn(o_flat, banks(2, 2), ACT.Ln, bias=eps_col[:, 0:1], scale=1.0 / P).then_inc(sem("hg_log"), 1)
            act.wait_ge(sem("hg_log"), 1)
            fn(o_flat, o_flat, ACT.Exp, scale=-0.5).then_inc(sem("hg_rstd"), 1)
            act.wait_ge(sem("att_sumsq"), 1)
            fn(att_rinv, banks(4, 4), ACT.Ln, bias=eps_col[:, 0:1], scale=1.0 / ATT_HD).then_inc(sem("att_log"), 1)
            act.wait_ge(sem("att_log"), 1)
            fn(att_rinv, att_rinv, ACT.Exp, scale=-0.5).then_inc(sem("att_rstd"), 1)

            taken(EARLY + 1)
            taken(EARLY + 2)

            n_units = ATT_HEADS * TT

            def att_exp(u):
                act.wait_ge(sem("att_max"), u + 1)
                if u >= 2:
                    act.wait_ge(sem("att_p_turned"), u - 1)
                fn(att_p[:, u % 2, :], ps[:, u % 2, :], ACT.Exp, bias=att_stat[:, 0, u:u + 1], scale=ATT_SCALE,
                   accum_out=att_stat[:, 1, u:u + 1]).then_inc(sem("att_exp"), 1)

            def att_copy(u):
                act.wait_ge(sem("att_p_turned"), u + 1)
                if u >= 2:
                    act.wait_ge(sem("att_out"), u - 1)
                fn(att_pt[:, u % 2, :, :].rearrange("p k q -> p (k q)"), ps[:, 2 + u % 2, :], ACT.Copy
                   ).then_inc(sem("att_pt"), 1)

            for i in range(n_units + 1):
                if i < n_units:
                    att_exp(i)
                if i == LATER_UNIT + 1:
                    taken(EARLY + 3)
                if i >= 1:
                    att_copy(i - 1)
            act.wait_ge(sem("att_out"), n_units)
            fn(o_att.rearrange("p a t -> p (a t)"), banks(4, 2), ACT.Copy).then_inc(sem("o_att_ready"), 1)

            square_pieces("h_updated", 4 * 6)
            root("experts", 0, D)
            act.wait_ge(sem("xn_ready"), XN["experts"])
            for k in range(KD):
                last = fn(x_in[:, k, :], x_in[:, k, :], ACT.Identity, bias=mod[:, 3 * KD + k, 0:1])
            last.then_inc(sem("modulated"), 1)
            act.wait_ge(sem("logits_ready"), 1)
            fn(aff_e.rearrange("p t e -> p (t e)"), aff_e.rearrange("p t e -> p (t e)"), ACT.Exp).then_inc(sem("aff_exp"), 1)
            act.wait_ge(sem("rows_back"), 1)
            fn(tok[:, :, :].rearrange("p t d -> p (t d)"), banks(4, 4), ACT.Copy).then_inc(sem("rows_copied"), 1)
            def pick_of(more, e):
                fn(pick_cur, picks[:, TT:2 * TT, e:, :][:, :, bass.ds(more, 1), :].rearrange("p k o c -> p k (o c)"),
                   ACT.Copy).then_inc(sem("pick_cur_ready"), 1)

            def rows_of(more, e):
                fn(x_cur, x_exp[:, :, e * CAP:][:, :, bass.ds(more * CAP, CAP)], ACT.Copy).then_inc(sem("x_cur_ready"), 1)

            def spread_of(more, e):
                act.wait_ge(sem("spread_turned"), more + (e + 1))
                fn(spread_cur[0:64, :], ps[0:64, 7, T:2 * T], ACT.Copy).then_inc(sem("spread_cur_ready"), 1)

            def expert(more, first=False, final=False):
                n = FIRST["experts"]
                wait_done(act, n + 3, more * 12)
                fn(half_g[0:64, :], ps[64:128, 4, :], ACT.Copy).then_inc(sem("half_g_ready"), 1)
                act.wait_ge(sem("gate_sum_ready"), more + 1)
                fn(gate_act[0:64, :], gate_sum[0:64, :], ACT.Silu).then_inc(sem("gate_act_ready"), 1)
                wait_done(act, n + 7, more * 12)
                fn(half_u[0:64, :], ps[64:128, 5, :], ACT.Copy).then_inc(sem("half_u_ready"), 1)
                if not final:
                    pick_of(more, 1)
                act.wait_ge(sem("hid_turned"), more + 1)
                fn(hid_t.rearrange("p (h c) s -> p h c s", h=2),
                   ps[:, 7, 0:256].rearrange("p (c h s) -> p h c s", c=4, h=2), ACT.Copy).then_inc(sem("hid_t_ready"), 1)
                if first:
                    for k in range(KD):
                        act.wait_ge(sem("x_exp_product"), 2 + k + 1)
                        fn(x_exp[:, k, FIRST_EXPERTS * CAP:], ps[:, 4 + k % 2, 0:(EXPERTS - FIRST_EXPERTS) * CAP], ACT.Copy
                           ).then_inc(sem("x_exp_taken"), 1)
                    act.wait_ge(sem("x_exp_taken"), 2 + KD)
                if not final:
                    rows_of(more, 1)
                wait_done(act, n + 11, more * 12)
                fn(half_y[0:64, :], ps[64:128, 6, :], ACT.Copy).then_inc(sem("half_y_ready"), 1)
                if not final:
                    act.wait_ge(sem("spread_free"), more + 1)
                    spread_of(more, 1)

            act.wait_ge(sem("pick_ready"), 1)
            pick_of(0, 0)
            for b in range(2):
                act.wait_ge(sem("x_exp_product"), b + 1)
                fn(x_exp[:, 4 * b:4 * b + 4, 0:FIRST_EXPERTS * CAP],
                   ps[:, 4 + b, :].rearrange("p (k c) -> p k c", k=4), ACT.Copy).then_inc(sem("x_exp_taken"), 1)
            act.wait_ge(sem("x_exp_taken"), 2)
            rows_of(0, 0)
            spread_of(0, 0)
            expert(0, first=True)
            with act.Fori(1, EXPERTS - 1) as e:
                expert(e)
            expert(EXPERTS - 1, final=True)

            square_pieces("h_updated", 4 * 7)
            root("final2", 4, D)
            for t in range(TT):
                for c in range(2):
                    act.wait_ge(sem("out_turned"), 2 * t + c + 1)
                    fn(tok[:, t, 512 * c:512 * c + 512], ps[:, 2 * t + c, :], ACT.Copy).then_inc(sem("rows_out"), 1)

        @block.vector
        def _(dve):
            steps = [0]

            def step(ins):
                ins.then_inc(sem("dve_step"), 1)
                steps[0] += 1

            def settle():
                dve.wait_ge(sem("dve_step"), steps[0])

            x_in = xn[:, :, T:2 * T]

            dve.memset(cond_pad, 0.0).then_inc(sem("pad_cleared"), 1)
            step(dve.memset(zero_w[:, :], 0.0))
            dve.memset(eps_col[:, :], EPS).then_inc(sem("eps_set"), 1)
            dve.wait_ge(sem("first_gains_turned"), 1)
            dve.tensor_copy(vec_a[:, 0:ROWS_FIRST], ps[:, 0, 0:ROWS_FIRST]).then_inc(sem("gains_ready"), 1)

            def normed(m, dst, src, gain, region=0):
                dve.wait_ge(sem("rstd_ready"), NORM[m])
                k_tiles = dst.shape[1]
                for k in range(k_tiles):
                    last = dve.scalar_tensor_tensor(dst[:, k, :], src[:, k, :], gain[:, k:k + 1],
                                                    rstd[:, region:region + T], ALU.mult, ALU.mult)
                    if m in XN_HALF and k == 3:
                        last.then_inc(sem("xn_half"), 1)
                last.then_inc(sem("xn_ready"), 1)

            def x_lo(name):
                for g in range(2):
                    dve.wait_ge(sem("x_hi"), X_BEFORE[name] + g + 1)
                    hi, lo = (x_split[:, part, 4 * g:4 * g + 4, :] for part in range(2))
                    dve.tensor_tensor(lo, x_in[:, 4 * g:4 * g + 4, :], hi.bitcast(F32), ALU.subtract
                                      ).then_inc(sem("x_split_ready"), 1)

            def split_lo(n, o, columns=True, more_halves=0):
                dve.wait_ge(sem("half_hi"), HALF[n] + o + 1 + more_halves)
                ins = dve.tensor_tensor(half_part(n, o, 1), half_slot(n, o, columns), half_part(n, o, 0).bitcast(F32),
                                        ALU.subtract)
                ins.then_inc(sem("half_split") if o == 0 else slot_free, 1)

            def split_lo_slot(n, columns=True):
                for o in range(2):
                    split_lo(n, o, columns)

            def gains(name, layer=0):
                return vec_a[:, ROWS_A[name] + KD * layer:ROWS_A[name] + KD * layer + KD]

            def update(factor, after, slots=None):
                def lo(piece):
                    dve.wait_ge(sem("x_hi"), X_BEFORE[after[0]] + piece + 1)
                    for k in (2 * piece, 2 * piece + 1):
                        ins = dve.scalar_tensor_tensor(x_split[:, 1, k, :], h[:, k, :], after[1][:, k:k + 1],
                                                       x_split[:, 0, k, :].bitcast(F32), ALU.mult, ALU.subtract)
                    ins.then_inc(sem("x_split_ready"), 1)

                for piece in range(4):
                    if factor is not None:
                        if slots is not None:
                            wait_done(dve, slots + piece)
                        hp = h[:, 2 * piece:2 * piece + 2, :].rearrange("p k t -> p (k t)")
                        dve.scalar_tensor_tensor(hp, ps[:, piece, :], factor, hp, ALU.mult, ALU.add
                                                 ).then_inc(sem("h_updated"), 1)
                    if after is not None and piece >= 1:
                        lo(piece - 1)
                if after is not None:
                    lo(3)

            def ffn(f, after_slot=None, after=None):
                n0 = FIRST[f"ffn{f}"]
                done = FF_STEPS * f
                split_lo_slot(n0 + 1)
                dve.wait_ge(sem("rstd_ready"), NORM[f"ffn{f}"])
                scale = rstd[:, 0:T].unsqueeze(1).to_broadcast([P, 2, T])

                def scaled(c, dst, bank):
                    return dve.tensor_tensor(dst, ps[:, bank + c % 2, :].rearrange("p (k t) -> p k t", t=T), scale, ALU.mult)

                def gate(n, c, more_halves, more):
                    wait_done(dve, n, more_halves)
                    scaled(c, silu_gate[:, c % 2, :].rearrange("p (k t) -> p k t", t=T), 4
                           ).then_inc(sem("gate_scaled"), 1)

                def combine(n, c, more_halves, more):
                    wait_done(dve, n, more_halves)
                    scaled(c, hidden[:, c % 2, :, :], 6).then_inc(sem("up_scaled"), 1)
                    dve.wait_ge(sem("up_scaled"), done + c + 1 + more)
                    dve.wait_ge(sem("silu_ready"), done + c + 1 + more)
                    flat = hidden[:, c % 2, :, :].rearrange("p k t -> p (k t)")
                    dve.tensor_tensor(flat, silu_gate[:, c % 2, :], flat, ALU.mult).then_inc(sem("hidden_ready"), 1)
                    dve.wait_ge(sem("hid_hi"), done + c + 1 + more)
                    dve.tensor_tensor(hid_split[:, c % 2, 1, :, :], hidden[:, c % 2, :, :],
                                      hid_split[:, c % 2, 0, :, :].bitcast(F32), ALU.subtract
                                      ).then_inc(sem("hid_split_ready"), 1)

                gate(n0, 0, 0, 0)
                with dve.Fori(0, FF_STEPS // 2) as i:
                    for j in range(2):
                        n = n0 + 2 + 3 * j
                        for s in range(3):
                            for o in range(2):
                                split_lo(n + s, o, s < 2, 12 * i)
                            if s == 0:
                                combine(n - 1 - (j > 0), j, 12 * i, 2 * i)
                        gate(n, 1 + j, 12 * i, 2 * i)
                split_lo_slot(n0 + 32, columns=False)
                combine(n0 + 30, FF_STEPS - 1, 0, 0)
                if after_slot is not None:
                    split_lo_slot(after_slot)
                wait_done(dve, n0 + 32)
                update(0.5, after)

            split_lo_slot(FIRST["ffn0"])
            update(None, ("ffn0", gains("ffn_norm1", 0)))
            ffn(0, after_slot=FIRST["pw1"])

            dve.wait_ge(sem("h_updated"), 4 * 1)
            split_lo_slot(FIRST["pw1"] + 1)
            normed("conv_in", x_in, h[:, :, :], gains("mix_norm", 0))
            x_lo("pw1")
            dve.wait_ge(sem("rows_turned"), 1)
            step(dve.tensor_copy(vec_b[:, :], ps[:, 5, 0:N_ROWS_B]))
            step(dve.tensor_copy(vec_a[:, ROWS_FIRST:N_ROWS_A], ps[:, 5, N_ROWS_B + ROWS_FIRST:N_ROWS_B + N_ROWS_A]))
            dve.tensor_copy(w_dw[:, :, :].rearrange("p k w -> p (k w)"), ps[:, 6, 0:KD * CONV_W]
                            ).then_inc(sem("vectors_ready"), 1)
            dve.wait_ge(sem("masks_in"), 16)
            step(dve.tensor_copy(mask[:, :, :], mask_in))
            settle()
            step(dve.memset(conv_in[:, :, 0:PAD], 0.0))
            split_lo_slot(FIRST["pw1"] + 2)
            split_lo_slot(FIRST["pw1"] + 3)
            tap_done = {}

            def glu(pair):
                dve.wait_ge(sem("glu_sig_ready"), pair + 1)
                dve.tensor_tensor(conv_in[:, 2 * pair:2 * pair + 2, PAD:PAD + T],
                                  ps[:, (2 * pair) % 4, :].rearrange("p (a t) -> p a t", t=T),
                                  glu_sig[:, pair % 2, :].rearrange("p (a t) -> p a t", t=T), ALU.mult
                                  ).then_inc(sem("glu_ready"), 1)

            def taps(pair, first, last):
                if first == 0:
                    dve.wait_ge(sem("vectors_ready"), 1)
                    dve.wait_ge(sem("glu_ready"), pair + 1)
                    settle()
                for w in range(first, last):
                    for j in (2 * pair, 2 * pair + 1):
                        u = conv_in[:, j, w:w + T]
                        if w == 0:
                            step(dve.tensor_scalar(conv_acc[:, j, :], u, w_dw[:, j, 0:1], None, ALU.mult))
                            tap_done[j] = steps[0]
                        else:
                            dve.wait_ge(sem("dve_step"), tap_done[j])
                            ins = dve.scalar_tensor_tensor(conv_acc[:, j, :], u, w_dw[:, j, w:w + 1],
                                                           conv_acc[:, j, :], ALU.mult, ALU.add)
                            if w < CONV_W - 1:
                                step(ins)
                                tap_done[j] = steps[0]
                            else:
                                ins.then_inc(sem("conv_done"), 1)

            glu(0)
            taps(0, 0, 4)
            split_lo_slot(FIRST["pw1"] + 4)
            taps(0, 4, 8)
            split_lo_slot(FIRST["pw1"] + 5)
            glu(1)
            taps(0, 8, 12)
            split_lo_slot(FIRST["pw1"] + 6)
            taps(0, 12, 16)
            split_lo_slot(FIRST["pw1"] + 7)
            glu(2)
            taps(0, 16, CONV_W)
            glu(3)
            taps(1, 0, CONV_W)
            taps(2, 0, CONV_W)
            split_lo_slot(FIRST["pw2"])
            split_lo_slot(FIRST["pw2"] + 1)
            normed("conv_out", x_in, conv_acc, gains("conv_norm"))
            x_lo("pw2")
            split_lo_slot(FIRST["pw2"] + 2)
            split_lo_slot(FIRST["pw2"] + 3)
            r = ROWS_B["hg_lb_logits_2"]
            lg = vec_b[:, r:r + 16].rearrange("p (d l h) -> p l d h", d=2, l=2)
            a, b, m = (lb_tmp[:, i] for i in range(3))
            step(dve.tensor_tensor(m, lg[:, 0], lg[:, 1], ALU.max))
            settle()
            step(dve.tensor_tensor(a, lg[:, 0], m, ALU.subtract))
            dve.tensor_tensor(b, lg[:, 1], m, ALU.subtract).then_inc(sem("floor_logits"), 1)
            dve.wait_ge(sem("floor_exp"), 1)
            step(dve.tensor_tensor(m, a, b, ALU.add))
            settle()
            step(dve.reciprocal(m, m))
            settle()
            step(dve.tensor_tensor(floor[:, 0], a, m, ALU.mult))
            settle()
            step(dve.tensor_scalar(floor[:, 1], floor[:, 0], -1.0, 1.0, ALU.mult, ALU.add))
            dve.wait_ge(sem("mod_turned"), 12)
            bias = vec_b[:, ROWS_B["b_mod_2"]:ROWS_B["b_mod_2"] + 48].unsqueeze(2).to_broadcast([P, 48, 2])
            step(dve.tensor_tensor(mod[:, :, :], ps[:, 4, T:T + 96].rearrange("p (f c) -> p f c", c=2), bias, ALU.add))
            settle()
            for i, (first, c, g) in enumerate(((KD, 0, "norm1_g_2"), (KD, 1, "norm1_g_2"), (4 * KD, 0, "norm2_g_2"))):
                ins = dve.scalar_tensor_tensor(gain_mod[:, i, :], mod[:, first:first + KD, c], 1.0,
                                               vec_b[:, ROWS_B[g]:ROWS_B[g] + KD], ALU.add, ALU.mult)
                ins.then_inc(sem("mod_ready"), 1)
            dve.wait_ge(sem("mod_ready"), 3)
            dve.wait_ge(sem("mod_ready"), 3)
            dve.wait_ge(sem("ctx_copied"), 1)
            normed("context", xn[:, :, 0:T], xn[:, :, 0:T], gain_mod[:, 1, :], region=T)
            split_lo_slot(FIRST["ffn1"])
            wait_done(dve, FIRST["pw2"] + 3)
            update(1.0, ("ffn1", gains("ffn_norm2", 0)))
            ffn(1, after_slot=FIRST["ffn2"], after=("ffn2", gains("ffn_norm1", 1)))
            ffn(2)

            dve.wait_ge(sem("positions_in"), 16)
            step(dve.tensor_copy(pos_f, pos_i[:, :]))
            settle()
            step(dve.tensor_scalar(ang, pos_f, const("inv_freq"), None, ALU.mult))
            settle()
            step(dve.tensor_scalar(turns, ang, 1.0 / TWO_PI, ROUND_MAGIC, ALU.mult, ALU.add))
            settle()
            step(dve.tensor_scalar(turns, turns, ROUND_MAGIC, None, ALU.subtract))
            for part in (PI_A, PI_B, PI_C):
                settle()
                step(dve.scalar_tensor_tensor(ang, turns, -part, ang, ALU.mult, ALU.add))
            settle()
            step(dve.tensor_scalar(turns, ang, TWO_PI / 4, -TWO_PI, ALU.is_gt, ALU.mult))
            settle()
            step(dve.scalar_tensor_tensor(turns, ang, TWO_PI / 4, turns, ALU.add, ALU.add))
            settle()
            step(dve.tensor_scalar(turns, turns, PI_LIMIT, -PI_LIMIT, ALU.min, ALU.max))
            dve.tensor_scalar(ang, ang, PI_LIMIT, -PI_LIMIT, ALU.min, ALU.max).then_inc(sem("angles_ready"), 1)
            dve.wait_ge(sem("h_updated"), 4 * 4)
            normed("mla", x_in, h[:, :, :], gains("mix_norm", 1))
            latent_ps = banks(0, 3).rearrange("p (k t) -> p k t", t=T)
            r = ROWS_A["mla_q_norm"]
            normed("mla_q", latent_n[:, 0:4, :], latent_ps[:, 0:4, :], vec_a[:, r:r + 4])
            normed("mla_kv", latent_n[:, 4:6, :], latent_ps[:, 4:6, :], vec_a[:, r + 4:r + 6], region=T)
            dve.wait_ge(sem("trig_ready"), 2)
            dve.wait_ge(sem("uq_taken"), 4)
            for a in range(5):
                last = dve.tensor_tensor(rope_a[:, a, :], rope_in[:, a, :], cos_t, ALU.mult)
            step(last)
            dve.wait_ge(sem("rope_turned"), 1)
            turned = banks(5, 3)[:, 0:5 * T].rearrange("p (a t) -> p a t", t=T)
            step(dve.tensor_tensor(rope_b, turned, sin_t.unsqueeze(1).to_broadcast([P, 5, T]), ALU.mult))
            settle()
            dve.tensor_tensor(rope_a, rope_a, rope_b, ALU.add).then_inc(sem("rope_ready"), 1)

            def mla_max(hd):
                dve.wait_ge(sem("mla_scores"), hd + 1)
                for t in range(TT):
                    a, b = (0, P) if t == 0 else (P, 3 * P)
                    step(dve.tensor_reduce(mla_stat[:, 2, hd, t:t + 1], ps[:, hd % 2, a:b], AX_X, ALU.max))
                settle()
                dve.tensor_scalar(mla_stat[:, 0, hd, :], mla_stat[:, 2, hd, :], -MLA_SCALE, None, ALU.mult
                                  ).then_inc(sem("mla_max"), 1)

            def mla_norm(hd):
                dve.wait_ge(sem("mla_exp"), 2 * hd + 2)
                step(dve.reciprocal(mla_stat[:, 3, hd, :], mla_stat[:, 1, hd, :]))
                settle()
                for t in range(TT):
                    a, b = (0, P) if t == 0 else (P, 3 * P)
                    last = dve.tensor_scalar(mla_p[:, hd % 2, a:b], mla_p[:, hd % 2, a:b], mla_stat[:, 3, hd, t:t + 1],
                                             None, ALU.mult)
                last.then_inc(sem("mla_p"), 1)

            def mla_take(hd):
                dve.wait_ge(sem("mla_out"), hd + 1)
                dve.tensor_copy(o_mla[:, hd, :], ps[:, 4 + hd % 2, 0:T]).then_inc(sem("mla_out_taken"), 1)

            for i in range(MLA_HEADS + 2):
                if i < MLA_HEADS:
                    mla_max(i)
                if i < MLA_HEADS:
                    mla_norm(i)
                if i >= 2:
                    mla_take(i - 2)
            update(1.0, ("ffn3", gains("ffn_norm2", 1)), FIRST["mla_o"])
            split_lo_slot(FIRST["ffn3"])
            ffn(3)

            dve.wait_ge(sem("h_updated"), 4 * 6)
            dve.wait_ge(sem("rstd_ready"), NORM["final1"])
            for k in range(KD):
                ins = dve.scalar_tensor_tensor(h[:, k, :], h[:, k, :], gains("final_norm")[:, k:k + 1], rstd[:, 0:T],
                                               ALU.mult, ALU.mult)
                if k % 2 == 1:
                    ins.then_inc(sem("h_normed"), 1)
            dve.wait_ge(sem("h_normed"), 4)
            normed("tokens", x_in, h[:, :, :], gain_mod[:, 0, :])

            step(dve.memset(pre_x[:, :, :, 0:1], 0.0))
            step(dve.memset(pre_c[:, :, :, 0:1], 0.0))
            for dr, (key, log) in enumerate(((key_f, log_f), (key_b, log_b))):
                dve.wait_ge(sem("proj_taken"), 4 + 2 * dr)
                for hd in range(HG_HEADS):
                    step(dve.tensor_scalar(key[:, hd, :], key[:, hd, :], floor[:, 1, dr, hd:hd + 1], None, ALU.mult))
            for dr, log in enumerate((log_f, log_b)):
                for hd in range(HG_HEADS):
                    dve.wait_ge(sem("forget_ready"), HG_HEADS * dr + hd + 1)
                    step(dve.tensor_tensor_scan(pre_c[:, dr, hd, 1:T + 1], ones, log[:, hd, 0:T], 0.0, ALU.mult, ALU.add))
                    step(dve.tensor_tensor_scan(pre_x[:, dr, hd, 1:T + 1], ones, log[:, hd, T:2 * T], 0.0, ALU.mult, ALU.add))
            settle()

            def halves(a, h_):
                v = a.rearrange("p h (n two w) -> p h n two w", two=2, w=h_)
                return v[:, :, :, 0, :], v[:, :, :, 1, :]

            half_of = LEVELS + [P]

            def decay_args(r_):
                h_ = half_of[r_]
                n = T // (2 * h_)
                for dr in range(2):
                    run = pre_x[:, dr, :, 1 - dr:1 - dr + T]
                    left, right = halves(run, h_)
                    d_left, d_right = halves(decay[:, r_ % 2, dr], h_)
                    mid = pre_x[:, dr, :, 0:T].rearrange("p h (n two w) -> p h n two w", two=2, w=h_)[:, :, :, 1, 0:1]
                    mid = mid.to_broadcast([P, HG_HEADS, n, h_])
                    dve.tensor_tensor(d_left, mid, left, ALU.subtract)
                    last = dve.tensor_tensor(d_right, right, mid, ALU.subtract)
                last.then_inc(sem("decay_ready"), 1)

            def decayed(r_):
                if r_ >= 2:
                    dve.wait_ge(sem("round_scores"), r_ - 1)
                q_out, k_out = q_lvl[:, r_ % 2], k_lvl[:, r_ % 2]
                if r_ == ROUND_DIAG:
                    dve.tensor_tensor(k_out, key_f[:, :, T:2 * T], key_b[:, :, T:2 * T], ALU.add
                                      ).then_inc(sem("round_ready"), 1)
                    return
                dve.wait_ge(sem("decay_exp"), r_ + 1)
                h_ = half_of[r_]
                q_l, q_r = halves(q_out, h_)
                k_l, k_r = halves(k_out, h_)
                src_l, src_r = halves(hg_q, h_)
                kf_l, _ = halves(key_f[:, :, T:2 * T], h_)
                _, kb_r = halves(key_b[:, :, T:2 * T], h_)
                f_l, f_r = halves(decay[:, r_ % 2, 0], h_)
                b_l, b_r = halves(decay[:, r_ % 2, 1], h_)
                dve.tensor_tensor(q_r, src_r, f_r, ALU.mult)
                dve.tensor_tensor(q_l, src_l, b_l, ALU.mult)
                dve.tensor_tensor(k_l, kf_l, f_l, ALU.mult)
                dve.tensor_tensor(k_r, kb_r, b_r, ALU.mult).then_inc(sem("round_ready"), 1)

            def take_scores(r_):
                dve.wait_ge(sem("round_scores"), r_ + 1)
                for s in range(TT):
                    t = 1 - s if r_ == ROUND_WIDE else s
                    o = hg_p[:, s, :, t * P:t * P + P]
                    data = ps[:, 6 + s, :].rearrange("p (h t) -> p h t", h=HG_HEADS)
                    if r_ == ROUND_WIDE:
                        last = dve.tensor_copy(o, data)
                    else:
                        m_ = mask[:, r_ if r_ < ROUND_WIDE else len(LEVELS), :].unsqueeze(1).to_broadcast([P, HG_HEADS, P])
                        last = dve.copy_predicated(o, m_, data)
                last.then_inc(sem("round_taken"), 1)

            dve.wait_ge(sem("ctx_turned"), 1)
            step(dve.memset(tok[:, :, :].rearrange("p t d -> p (t d)"), 0.0))
            decay_args(0)
            decay_args(1)
            for r_ in range(ROUNDS):
                decayed(r_)
                if r_ + 2 < ROUNDS - 1:
                    dve.wait_ge(sem("round_ready"), r_ + 1)
                    decay_args(r_ + 2)
                if r_ >= 1:
                    if r_ == 1:
                        settle()
                    take_scores(r_ - 1)
            take_scores(ROUNDS - 1)
            wait_done(dve, FIRST["w_in"] + 12)
            dve.tensor_tensor(q_dec[:, 1], pre_x[:, 1, :, T:T + 1].to_broadcast([P, HG_HEADS, T]), pre_x[:, 1, :, 0:T],
                              ALU.subtract)
            dve.tensor_tensor(key_dec[:, 0], pre_c[:, 0, :, T:T + 1].to_broadcast([P, HG_HEADS, T]), pre_c[:, 0, :, 1:T + 1],
                              ALU.subtract).then_inc(sem("end_ready"), 1)
            dve.wait_ge(sem("key_dec_exp"), 2)
            dve.tensor_tensor(key_dec[:, 0], key_dec[:, 0], key_f[:, :, 0:T], ALU.mult)
            dve.tensor_tensor(key_dec[:, 1], key_dec[:, 1], key_b[:, :, 0:T], ALU.mult).then_inc(sem("key_dec_ready"), 1)
            dve.wait_ge(sem("q_dec_exp"), 2)
            for dr in range(2):
                last = dve.tensor_tensor(q_dec[:, dr], q_dec[:, dr], hg_q, ALU.mult)
            last.then_inc(sem("q_dec_ready"), 1)
            dve.wait_ge(sem("hg_rstd"), 1)
            step(dve.tensor_tensor(o_sq, o_hg, hg_gate, ALU.mult))
            settle()
            r = ROWS_B["hg_norm_g_2"]
            for hd in range(HG_HEADS):
                last = dve.scalar_tensor_tensor(o_hg[:, hd, :], ps[:, hd // 2, (hd % 2) * T:(hd % 2) * T + T],
                                                vec_b[:, r + hd:r + hd + 1], o_sq[:, hd, :], ALU.mult, ALU.mult)
            last.then_inc(sem("hg_normed"), 1)

            dve.wait_ge(sem("att_rstd"), 1)
            dve.wait_ge(sem("gains_in"), 64)
            qf, kf = att_qr.rearrange("p a t -> p (a t)"), att_kr.rearrange("p a t -> p (a t)")
            dve.wait_ge(sem("key_dec_ready"), 1)
            dve.scalar_tensor_tensor(qf, att_q.rearrange("p a t -> p (a t)"), qk_gain[:, 0:1], att_rinv[:, 0:4 * T],
                                     ALU.mult, ALU.mult)
            dve.scalar_tensor_tensor(kf, att_k.rearrange("p a t -> p (a t)"), qk_gain[:, 1:2], att_rinv[:, 4 * T:8 * T],
                                     ALU.mult, ALU.mult).then_inc(sem("att_n_ready"), 1)
            dve.wait_ge(sem("att_turned"), 1)
            cos_q = const("axial_cos").unsqueeze(1).to_broadcast([P, 4, T])
            sin_q = const("axial_sin").unsqueeze(1).to_broadcast([P, 4, T])
            cos_k = const("axial_cos").unsqueeze(1).to_broadcast([P, ATT_KV, T])
            sin_k = const("axial_sin").unsqueeze(1).to_broadcast([P, ATT_KV, T])
            rot = att_rot.rearrange("p (a t) -> p a t", t=T)
            sq = att_sq.rearrange("p (a t) -> p a t", t=T)
            dve.wait_ge(sem("att_n_ready"), 1)
            step(dve.tensor_tensor(rot[:, 0:4, :], att_qr, cos_q, ALU.mult))
            step(dve.tensor_tensor(rot[:, 4:6, :], att_kr[:, :, T:2 * T], cos_k, ALU.mult))
            step(dve.tensor_tensor(sq[:, 0:4, :], banks(4, 2).rearrange("p (a t) -> p a t", t=T), sin_q, ALU.mult))
            step(dve.tensor_tensor(sq[:, 4:6, :], banks(6, 1).rearrange("p (a t) -> p a t", t=T), sin_k, ALU.mult))
            settle()
            dve.tensor_tensor(att_qr, rot[:, 0:4, :], sq[:, 0:4, :], ALU.add)
            dve.tensor_tensor(att_kr[:, :, T:2 * T], rot[:, 4:6, :], sq[:, 4:6, :], ALU.add).then_inc(sem("att_ready"), 1)

            def att_max(u):
                dve.wait_ge(sem("att_scores"), u + 1)
                step(dve.tensor_reduce(att_stat[:, 2, u:u + 1], ps[:, u % 2, :], AX_X, ALU.max))
                settle()
                dve.tensor_scalar(att_stat[:, 0, u:u + 1], att_stat[:, 2, u:u + 1], -ATT_SCALE, None, ALU.mult
                                  ).then_inc(sem("att_max"), 1)

            def att_norm(u):
                dve.wait_ge(sem("att_exp"), u + 1)
                step(dve.reciprocal(att_stat[:, 3, u:u + 1], att_stat[:, 1, u:u + 1]))
                settle()
                dve.tensor_scalar(att_p[:, u % 2, :], att_p[:, u % 2, :], att_stat[:, 3, u:u + 1], None, ALU.mult
                                  ).then_inc(sem("att_p"), 1)

            for u in range(ATT_HEADS * TT):
                att_max(u)
                att_norm(u)

            for br, gate in ((0, gate_a), (1, gate_b)):
                for j in range(2):
                    wait_done(dve, FIRST["branch"] + 2 * br + j)
                    o = (merged if br == 0 else gate_b)[:, 4 * j:4 * j + 4, :]
                    dve.tensor_tensor(o, banks(2 * j, 2).rearrange("p (a t) -> p a t", t=T), gate[:, 4 * j:4 * j + 4, :],
                                      ALU.mult).then_inc(sem("branch_taken"), 1)
            dve.wait_ge(sem("branch_taken"), 4)
            dve.tensor_tensor(merged, merged, gate_b, ALU.add).then_inc(sem("merged_ready"), 1)
            for k in range(KD):
                if k % 2 == 0:
                    wait_done(dve, FIRST["w_out"] + k // 2)
                last = dve.scalar_tensor_tensor(h[:, k, :], ps[:, 4 + k // 2, (k % 2) * T:(k % 2) * T + T],
                                                mod[:, 2 * KD + k, 0:1], h[:, k, :], ALU.mult, ALU.add)
                if k % 2 == 1:
                    last.then_inc(sem("h_updated"), 1)

            dve.wait_ge(sem("h_updated"), 4 * 7)
            normed("experts", x_in, h[:, :, :], gain_mod[:, 2, :])
            dve.wait_ge(sem("router_scores"), 1)
            scores = ps[:, 1, 0:TT * EXPERTS].rearrange("p (t e) -> p t e", t=TT)
            step(dve.tensor_reduce(small[:, 8:10], scores, AX_X, ALU.max))
            settle()
            dve.tensor_tensor(aff_e, scores, small[:, 8:10].unsqueeze(2).to_broadcast([P, TT, EXPERTS]), ALU.subtract
                              ).then_inc(sem("logits_ready"), 1)
            dve.wait_ge(sem("aff_exp"), 1)
            step(dve.tensor_reduce(small[:, 10:12], aff_e, AX_X, ALU.add))
            settle()
            step(dve.reciprocal(small[:, 12:14], small[:, 10:12]))
            settle()
            dve.tensor_tensor(aff, aff_e, small[:, 12:14].unsqueeze(2).to_broadcast([P, TT, EXPERTS]), ALU.mult
                              ).then_inc(sem("aff_ready"), 1)
            dve.wait_ge(sem("aff_turned"), 1)
            E16 = slice(0, EXPERTS)
            step(dve.tensor_copy(aff_t[E16, :], ps[E16, 0, 0:T]))
            src, other = aff_t, (work_a, work_b)
            for i in range(CAP // 8):
                settle()
                step(dve.max(top8[E16, :], src[E16, :]))
                settle()
                dst = other[i % 2]
                step(dve.match_replace(dst[E16, :], top8[E16, :], src[E16, :], -1.0))
                src = dst
            settle()
            step(dve.tensor_scalar(chosen[E16, :], src[E16, :], 0.0, None, ALU.is_lt))
            settle()
            step(dve.tensor_tensor_scan(slot_t[E16, :], ones[E16, :], chosen[E16, :], 0.0, ALU.mult, ALU.add))
            settle()
            dve.tensor_tensor(slot_t[E16, :], slot_t[E16, :], chosen[E16, :], ALU.mult).then_inc(sem("slots_chosen"), 1)
            dve.wait_ge(sem("slots_turned"), 1)
            step(dve.tensor_copy(slot_tok.rearrange("p t e -> p (t e)"), ps[:, 1, 0:TT * EXPERTS]))
            settle()
            iota = const("iota").unsqueeze(1).to_broadcast([P, EXPERTS, CAP])
            for t in range(TT):
                step(dve.tensor_tensor(picks[:, t, 0:EXPERTS, :], iota,
                                       slot_tok[:, t, :].unsqueeze(2).to_broadcast([P, EXPERTS, CAP]), ALU.is_equal))
            settle()
            for t in range(TT):
                last = dve.tensor_tensor(picks[:, TT + t, 0:EXPERTS, :], picks[:, t, 0:EXPERTS, :],
                                         aff[:, t, :].unsqueeze(2).to_broadcast([P, EXPERTS, CAP]), ALU.mult)
            last.then_inc(sem("pick_ready"), 1)

            with dve.Fori(0, EXPERTS) as e:
                dve.wait_ge(sem("half_g_ready"), e + 1)
                dve.tensor_tensor(gate_sum[0:64, :], ps[0:64, 4, :], half_g[0:64, :], ALU.add
                                  ).then_inc(sem("gate_sum_ready"), 1)
                dve.wait_ge(sem("half_u_ready"), e + 1)
                dve.tensor_tensor(up_sum[0:64, :], ps[0:64, 5, :], half_u[0:64, :], ALU.add).then_inc(sem("up_sum_ready"), 1)
                dve.wait_ge(sem("up_sum_ready"), e + 1)
                dve.wait_ge(sem("gate_act_ready"), e + 1)
                dve.tensor_tensor(hid_e[0:64, :], gate_act[0:64, :], up_sum[0:64, :], ALU.mult).then_inc(sem("hid_ready"), 1)
                dve.wait_ge(sem("half_y_ready"), e + 1)
                dve.tensor_tensor(y_e[0:64, :], ps[0:64, 6, :], half_y[0:64, :], ALU.add).then_inc(sem("y_ready"), 1)
            dve.wait_ge(sem("spread_free"), EXPERTS)
            for k in range(KD):
                last = dve.scalar_tensor_tensor(h[:, k, :], ps[:, k // 2, (k % 2) * T:(k % 2) * T + T],
                                                mod[:, 5 * KD + k, 0:1], h[:, k, :], ALU.mult, ALU.add)
                if k % 2 == 1:
                    last.then_inc(sem("h_updated"), 1)
            dve.wait_ge(sem("h_updated"), 4 * 8)
            r = ROWS_B["final_norm_g_2"]
            normed("final2", x_in, h[:, :, :], vec_b[:, r:r + KD])


_INS = ['x', 'positions', 'ffn_norm1', 'ffn1_w1', 'ffn1_w3', 'ffn1_w2', 'mix_norm', 'ffn_norm2', 'ffn2_w1', 'ffn2_w3',
        'ffn2_w2', 'conv_w_pw1', 'conv_w_dw', 'conv_norm', 'conv_w_pw2', 'mla_w_a', 'mla_q_norm', 'mla_kv_norm',
        'mla_w_uq', 'mla_w_ukv', 'mla_w_o', 'final_norm', 'c_2', 'ctx_2', 'c_ctx_2', 'w_mod_2', 'b_mod_2', 'norm1_g_2',
        'norm2_g_2', 'w_in_2', 'hg_lb_logits_2', 'hg_norm_g_2', 'q_norm_g_2', 'k_norm_g_2', 'w_branch_a_2',
        'w_branch_b_2', 'w_out_2', 'w_router_2', 'w_exp_gate_2', 'w_exp_up_2', 'w_exp_down_2', 'final_norm_g_2']
_OUT = (1, T, D)


def kernel(**inputs):
    import concourse.bacc as bacc
    from concourse.bass_utils import run_bass_kernel_spmd

    nc = bacc.Bacc("TRN2", target_bir_lowering=False, num_devices=1)
    arrays = {f"in_{name}": np.ascontiguousarray(inputs[name]) for name in _INS}
    arrays["in_constants"], arrays["in_masks"] = CONSTANTS, MASKS
    args = [nc.dram_tensor(name, a.shape, mybir.dt.from_np(a.dtype), kind="ExternalInput").ap()
            for name, a in arrays.items()]
    args.append(nc.dram_tensor("out_0", _OUT, F32, kind="ExternalOutput").ap())
    build(nc, *args)
    r = run_bass_kernel_spmd(nc, [arrays], core_ids=[0])
    return r.results[0]["out_0"]
```

```python
from contextlib import ExitStack

import numpy as np
import concourse.bass as bass
from concourse import mybir

F32 = mybir.dt.float32
F32R = mybir.dt.float32r
I32 = mybir.dt.int32
U8 = mybir.dt.uint8
BF16 = mybir.dt.bfloat16
ALU = mybir.AluOpType
ACT = mybir.ActivationFunctionType
AX_X = mybir.AxisListType.X

P = 128
D = 1024
KD = D // P
T = 256
TT = T // P
FF = 2816
EPS = 1e-6

SLOTS = 6
SLOT = 2048
FF_CHUNK = 256
FF_STEPS = FF // FF_CHUNK

CONV_W = 31
MLA_HEADS, NOPE, ROPE, VH = 8, 128, 64, 128
Q_LORA, KV_LORA = 512, 256
MLA_SCALE = (NOPE + ROPE) ** -0.5
MASKED = -1e30
CHUNK = 64

N_MOD = 6
HG_HEADS = 4
ATT_HEADS, ATT_HD, ATT_KV = 8, 64, 2
ATT_SCALE = ATT_HD ** -0.5
EXPERTS, CAP, EFF = 16, 32, 1024
LEVELS = [64, 32, 16, 8, 4, 2, 1]
ROUND_WIDE, ROUND_DIAG = len(LEVELS), len(LEVELS) + 1
ROUNDS = len(LEVELS) + 2

STREAM = [("ffn0", 33), ("pw1", 8), ("mod_conv", 12), ("pw2", 4), ("ffn1", 33), ("ffn2", 33),
          ("mod_mla", 2), ("mla_a", 4), ("mod_latent", 2), ("uq", 4), ("ukv", 2), ("mod_rope", 2), ("mla_o", 4),
          ("ffn3", 33), ("mod_final", 2), ("mod_tokens", 4), ("w_in", 21), ("branch", 4), ("w_out", 4), ("experts", 12 * EXPERTS)]
FIRST = {}
_at = 0
for _name, _n in STREAM:
    FIRST[_name] = _at
    _at += _n

SPLIT = ("ffn0", "pw1", "pw2", "ffn1", "ffn2", "ffn3")
HALF_BUFS = 4
HALF = {}
for _name, _n in STREAM:
    if _name in SPLIT:
        for _s in range(_n):
            HALF[FIRST[_name] + _s] = 2 * len(HALF)
X_PIECES = {"ffn0": 4, "pw1": 4, "pw2": 4, "ffn1": 4, "ffn2": 4, "ffn3": 4}
X_BEFORE = {name: sum(list(X_PIECES.values())[:i]) for i, name in enumerate(X_PIECES)}
NORMS = ("ffn0", "conv_in", "context", "conv_out", "ffn1", "ffn2", "mla", "mla_q", "mla_kv", "ffn3", "final1", "tokens",
         "experts", "final2")
NORM = {name: i + 1 for i, name in enumerate(NORMS)}
SQ_PIECES = {name: 4 if name in ("conv_out", "mla", "final1", "tokens", "experts", "final2") else 1 for name in NORMS}
SQ_BEFORE = {name: sum(SQ_PIECES[m] for m in NORMS[:i]) for i, name in enumerate(NORMS)}
NORMED = ("mla_q", "mla_kv")
XN = {name: i + 1 for i, name in enumerate(NORMED)}
NORM_PIECES = {"conv_out": 0, "context": 4, "mla": 8, "tokens": 12, "experts": 16, "final2": 20}
SHIFTED = {"context": 0, "tokens": 4, "experts": 8}
UPDATES = {0: 0, 1: 2, 2: 3, 3: 5}

MOD_CHUNKS, MOD_EARLY = 12, 6
MOD_SLOT = [FIRST["mod_conv"] + 2 * _c for _c in range(MOD_EARLY)] + \
           [FIRST["mod_mla"], FIRST["mod_latent"], FIRST["mod_rope"], FIRST["mod_final"],
            FIRST["mod_tokens"], FIRST["mod_tokens"] + 2]

ROWS_FIRST = 32
ROWS_A = {"ffn_norm1": 0, "mix_norm": 16, "ffn_norm2": 32, "conv_norm": 48, "mla_q_norm": 56, "mla_kv_norm": 60,
          "final_norm": 62}
N_ROWS_A = 70
ROWS_B = {"c_2": 0, "c_ctx_2": 8, "b_mod_2": 16, "norm1_g_2": 64, "norm2_g_2": 72, "hg_lb_logits_2": 80,
          "hg_norm_g_2": 96, "final_norm_g_2": 100}
N_ROWS_B = 108

CONST = {}


def constant_table():
    p = np.arange(P)
    parts = {
        "ident": np.eye(P),
        "ones": np.ones((P, T)),
        "headsum": (p[:, None] // ATT_HD == p[None, :] // ATT_HD),
    }

    def rotation(half):
        m = np.zeros((P, P))
        for col in range(P):
            if col % (2 * half) < half:
                m[col + half, col] = -1.0
            else:
                m[col - half, col] = 1.0
        return m

    parts["rope_rot"] = rotation(ROPE // 2)
    parts["axial_rot"] = rotation(ATT_HD // 4)
    rows = np.repeat(np.arange(T // 64, dtype=np.float32), 64)
    cols = np.tile(np.arange(64, dtype=np.float32), T // 64)
    axis_dim = ATT_HD // 2
    freq = (np.float64(10000.0) ** (-np.arange(0, axis_dim, 2) / axis_dim)).astype(np.float32)
    d = p % ATT_HD
    ang = np.where((d // axis_dim == 0)[:, None], rows[None, :], cols[None, :]).astype(np.float32)
    ang = (ang * freq[d % (axis_dim // 2)][:, None]).astype(np.float32)
    parts["axial_cos"] = np.cos(ang.astype(np.float64))
    parts["axial_sin"] = np.sin(ang.astype(np.float64))
    parts["iota"] = np.tile(np.arange(1, CAP + 1), (P, 1))
    parts["cond_sel"] = (p[:, None] % 32 == np.arange(2)[None, :])
    parts["mask_rows"] = np.tile(p < CHUNK, (P, 1))
    parts["mask_cols"] = np.tile(np.where(p < CHUNK, 0.0, MASKED), (P, 1))
    parts["inv_freq"] = (np.float64(10000.0) ** (-2.0 * (p % (ROPE // 2)) / ROPE))[:, None]
    at = 0
    for name, a in parts.items():
        CONST[name] = (at, at + a.shape[1])
        at += a.shape[1]
    return np.concatenate([np.asarray(a, np.float64).astype(np.float32) for a in parts.values()], axis=1)


def level_masks():
    s, t = np.arange(P)[:, None], np.arange(P)[None, :]
    m = [(s // (2 * h) == t // (2 * h)) & (s // h != t // h) for h in LEVELS] + [s == t]
    return np.ascontiguousarray(np.stack(m, axis=1).astype(np.int32))


CONSTANTS = constant_table()
MASKS = level_masks()
TWO_PI = 2.0 * np.pi
PI_A = 6.28125
PI_B = float(np.float32(np.round((TWO_PI - PI_A) * 2.0 ** 20) / 2.0 ** 20))
PI_C = float(np.float32(TWO_PI - PI_A - PI_B))
ROUND_MAGIC = 1.5 * 2.0 ** 23
PI_LIMIT = 3.1415925


def build(nc, x, positions, ffn_norm1, ffn1_w1, ffn1_w3, ffn1_w2, mix_norm, ffn_norm2, ffn2_w1, ffn2_w3, ffn2_w2,
          conv_w_pw1, conv_w_dw, conv_norm, conv_w_pw2, mla_w_a, mla_q_norm, mla_kv_norm, mla_w_uq, mla_w_ukv,
          mla_w_o, final_norm, c_2, ctx_2, c_ctx_2, w_mod_2, b_mod_2, norm1_g_2, norm2_g_2, w_in_2,
          hg_lb_logits_2, hg_norm_g_2, q_norm_g_2, k_norm_g_2, w_branch_a_2, w_branch_b_2, w_out_2, w_router_2,
          w_exp_gate_2, w_exp_up_2, w_exp_down_2, final_norm_g_2, constants, masks, out):
    vectors_a = {"ffn_norm1": ffn_norm1, "mix_norm": mix_norm, "ffn_norm2": ffn_norm2, "conv_norm": conv_norm,
                 "mla_q_norm": mla_q_norm, "mla_kv_norm": mla_kv_norm, "final_norm": final_norm}
    vectors_b = {"c_2": c_2, "c_ctx_2": c_ctx_2, "b_mod_2": b_mod_2, "norm1_g_2": norm1_g_2, "norm2_g_2": norm2_g_2,
                 "hg_lb_logits_2": hg_lb_logits_2, "hg_norm_g_2": hg_norm_g_2, "final_norm_g_2": final_norm_g_2}

    def as_rows(a):
        names = " ".join("abc"[:len(a.shape)])
        flat = a if len(a.shape) == 1 else a.rearrange(f"{names} -> ({names})")
        return flat.rearrange("(r f) -> r f", f=P)

    with ExitStack() as ctx:
        def sb(name, shape, dt=F32):
            return ctx.enter_context(nc.sbuf_tensor(name, shape, dt))

        sems = {}

        def sem(name):
            if name not in sems:
                sems[name] = ctx.enter_context(nc.semaphore(name))
            return sems[name]

        ps = ctx.enter_context(nc.psum_tensor("banks", [P, 8, 512], F32))

        def banks(first, n):
            return ps[:, first:first + n, :].rearrange("p b c -> p (b c)")

        ring = sb("ring", [P, SLOTS, SLOT])
        h = sb("h", [P, KD, T])
        xn = sb("xn", [P, KD, 2 * T])
        squares = sb("squares", [P, KD, 2 * T])
        std = sb("std", [P, 2 * T])
        rstd = sb("rstd", [P, 2 * T])
        consts = sb("consts", [P, CONSTANTS.shape[1]])
        mask = sb("mask", [P, len(LEVELS) + 1, P], U8)
        vec_a = sb("vec_a", [P, N_ROWS_A])
        vec_b = sb("vec_b", [P, N_ROWS_B])
        qk_gain = sb("qk_gain", [P, 2])
        w_dw = sb("w_dw", [P, KD, CONV_W])
        mod = sb("mod", [P, N_MOD * KD, 2])
        gain_mod = sb("gain_mod", [P, 3, KD])
        tok = sb("tok", [P, TT, D])
        gated = sb("gated", [P, 2, 2 * 512])
        silu_gate = gated[:, 0, :].rearrange("p (a c) -> p a c", a=2)
        hidden = gated[:, 1, :].rearrange("p (a b t) -> p a b t", a=2, b=2)
        small = sb("small", [P, 64])
        router = sb("router", [P, KD, EXPERTS])
        pos_i = sb("pos_i", [P, T], I32)
        zero_w = sb("zero_w", [P, 512], BF16)
        eps_col = sb("eps_col", [P, 1])
        lb_tmp = sb("lb_tmp", [P, 3, 2, HG_HEADS])
        floor = sb("floor", [P, 2, 2, HG_HEADS])
        mla_stat = sb("mla_stat", [P, 4, MLA_HEADS, TT])
        att_stat = sb("att_stat", [P, 4, ATT_HEADS * TT])
        ARENA = 22100
        arena_at = -(-nc.sbuf_base // 32) * 32
        arena = sb("arena", [P, ARENA])
        LOW = (ARENA - HALF_BUFS * SLOT - 2 * KD * T - 8 * T) // 8 * 8

        def split_tensor(name, shape, first):
            return nc.alloc_sbuf_tensor_at(name, shape, F32R, offset=arena_at + 4 * first)

        w_split = split_tensor("w_split", [P, HALF_BUFS, 2, SLOT // 2], LOW)
        x_split = split_tensor("x_split", [P, 2, KD, T], LOW + HALF_BUFS * SLOT)
        hid_split = split_tensor("hid_split", [P, 2, 2, 2, T], LOW + HALF_BUFS * SLOT + 2 * KD * T)

        def const(name, rows=P):
            a, b = CONST[name]
            return consts[0:rows, a:b]

        ident, ones = const("ident"), const("ones")

        class Region:
            def __init__(self):
                self.at = 0

            def take(self, *shape, rows=P):
                n = int(np.prod(shape))
                view = arena[0:rows, self.at:self.at + n]
                self.at += n
                assert self.at <= ARENA, self.at
                names = [f"d{i}" for i in range(len(shape))]
                if len(shape) > 1:
                    sizes = dict(zip(names, shape))
                    view = view.rearrange(f"p ({' '.join(names)}) -> p {' '.join(names)}", **sizes)
                return view

        r0 = Region()
        rows_a, rows_b, rows_dw = r0.take(P, rows=N_ROWS_A), r0.take(P, rows=N_ROWS_B), r0.take(D, rows=CONV_W)
        mask_in = r0.take(len(LEVELS) + 1, P).bitcast(I32)
        r1 = Region()
        PAD = CONV_W - 1
        conv_in, conv_acc, glu_sig = r1.take(KD, PAD + T), r1.take(KD, T), r1.take(2, 2 * T)
        cond_pad, mod_rows = r1.take(KD, 32), r1.take(2, 512)
        POOL_TILES, PE_TILES = (0, 4), (5, 7)
        DIAGS = 16
        TAPS = [(j, w) for j in PE_TILES for w in range(CONV_W)]
        TAP_STEPS = (0, 12, 24, 34, 44, 54, len(TAPS))
        tap_product = squares[:, :, T:2 * T]
        POOL_STEPS = (0, 6, 12, 18, 25, CONV_W, CONV_W)
        diag = arena[:, ARENA - 16 * P:ARENA].rearrange("p (q c) -> p q c", c=P)
        cond_late = tok[:, 1, 0:KD * 32].rearrange("p (k c) -> p k c", k=KD)
        mod_rows_late = tok[:, 0, :].rearrange("p (r c) -> p r c", r=2)
        assert max(r0.at, r1.at) <= LOW
        r2 = Region()
        latent, latent_n = r2.take(6, T), r2.take(6, T)
        q_nope, k_nope = r2.take(MLA_HEADS, T), r2.take(MLA_HEADS, T)
        rope_in, o_mla = r2.take(5, T), r2.take(MLA_HEADS, T)
        rope_a, rope_b, v_tok = r2.take(5, T), r2.take(5, T), r2.take(TT, MLA_HEADS, VH)
        mla_p, mla_pt = r2.take(2, 384), r2.take(2, 3, P)
        cos_t, sin_t, ang, turns, pos_f = (r2.take(T) for _ in range(5))
        r3 = Region()
        hg_q = r3.take(HG_HEADS, T)
        key_f, key_b = r3.take(HG_HEADS, 2 * T), r3.take(HG_HEADS, 2 * T)
        log_f, log_b = r3.take(HG_HEADS, 2 * T), r3.take(HG_HEADS, 2 * T)
        hg_v = r3.take(4, 512)
        att_q, att_k = r3.take(4, T), r3.take(ATT_KV, 2 * T)
        att_v = r3.take(4, P)
        gate_a, gate_b = r3.take(KD, T), r3.take(KD, T)
        pre_x, pre_c = r3.take(2, HG_HEADS, T + 1), r3.take(2, HG_HEADS, T + 1)
        hg_gate = gated[:, 0, :].rearrange("p (a t) -> p a t", t=T)
        state0 = gated[:, 1, :].rearrange("p (d h v) -> p d h v", d=2, h=HG_HEADS)
        decay = squares[:, :, :].rearrange("p k t -> p (k t)").rearrange("p (r d h t) -> p r d h t", r=2, d=2, h=HG_HEADS)
        q_lvl = log_f.rearrange("p a t -> p (a t)").rearrange("p (r h t) -> p r h t", r=2, h=HG_HEADS)
        k_lvl = log_b.rearrange("p a t -> p (a t)").rearrange("p (r h t) -> p r h t", r=2, h=HG_HEADS)
        hg_p = tok[:, :, :].rearrange("p s (h t) -> p s h t", h=HG_HEADS)
        key_dec = xn[:, :, 0:T].rearrange("p (d h) t -> p d h t", d=2)
        key_dec_t = decay[:, 1].rearrange("p d h t -> p (d h t)").rearrange("p (d s c) -> p d s c", d=2, s=TT)
        q_dec = decay[:, 0]
        o_sq = decay[:, 1, 0]
        o_hg = decay[:, 1, 1]
        att_rot = q_lvl.rearrange("p r h t -> p (r h t)")
        att_sq = k_lvl.rearrange("p r h t -> p (r h t)")
        att_qr = key_f.rearrange("p a t -> p (a t)")[:, 0:4 * T].rearrange("p (a t) -> p a t", t=T)
        att_kr = key_f.rearrange("p a t -> p (a t)")[:, 4 * T:8 * T].rearrange("p (a t) -> p a t", t=2 * T)
        att_p = key_b.rearrange("p a t -> p (a t)")[:, 0:1024].rearrange("p (r k) -> p r k", r=2)
        att_pt = key_b.rearrange("p a t -> p (a t)")[:, 1024:2048].rearrange("p (r k q) -> p r k q", r=2, k=4)
        att_rinv = pre_c.rearrange("p d h t -> p (d h t)")[:, 0:2048]
        o_att = hg_q
        merged = xn[:, :, 0:T]
        r4 = Region()
        x_exp = xn
        FIRST_EXPERTS = 4
        picks = r4.take(2 * TT, EXPERTS, CAP)
        pick_cur, x_cur, spread_cur = r4.take(TT, CAP), r4.take(KD, CAP), r4.take(T)
        half_g, half_u, half_y, gate_act = r4.take(512), r4.take(512), r4.take(512), r4.take(512)
        gate_sum, up_sum, hid_e, y_e = r4.take(512), r4.take(512), r4.take(512), r4.take(512)
        hid_t = r4.take(KD, CAP)
        aff, aff_e = r4.take(TT, EXPERTS), r4.take(TT, EXPERTS)
        aff_t, work_a, work_b, chosen, slot_t = (r4.take(T) for _ in range(5))
        slot_tok = r4.take(TT, EXPERTS)
        top8 = r4.take(8)
        AHEAD = SLOTS
        ahead = r4.take(AHEAD, SLOT)
        squares_flat = squares[:, :, :].rearrange("p k t -> p (k t)")
        extra = [gated[:, :, :].rearrange("p a c -> p (a c)"), squares_flat[:, 0:SLOT], squares_flat[:, SLOT:2 * SLOT]]
        EXTRA = len(extra)
        BESIDE = AHEAD + EXTRA
        assert r4.at <= ARENA

        slot_full = [sem(f"slot_full_{i}") for i in range(SLOTS)]
        slot_free = sem("slot_free")
        half_done = sem("half_done")

        def wait_free(sp, n, more=0):
            if n >= SLOTS:
                sp.wait_ge(slot_free, n - SLOTS + 1 + more)

        def wait_full(pe, n, more=0):
            pe.wait_ge(slot_full[n % SLOTS], 16 * (n // SLOTS + 1) + more)

        def wait_done(eng, n, more=0):
            if n in HALF:
                eng.wait_ge(half_done, HALF[n] + 2 + more)
            else:
                eng.wait_ge(slot_free, n + 1 + more)

        def slot(n):
            return ring[:, n % SLOTS, :]

        def half_slot(n, o, columns):
            if columns:
                return slot(n).rearrange("p (k c) -> p k c", k=KD)[:, :, o * P:o * P + P]
            return slot(n)[:, o * D:o * D + D].rearrange("p (k c) -> p k c", k=KD)

        def half_part(n, o, part):
            return w_split[:, (HALF[n] + o) % HALF_BUFS, part, :].rearrange("p (k c) -> p k c", k=KD)

        w_ffn = [(ffn1_w1[0], ffn1_w3[0], ffn1_w2[0]), (ffn2_w1[0], ffn2_w3[0], ffn2_w2[0]),
                 (ffn1_w1[1], ffn1_w3[1], ffn1_w2[1]), (ffn2_w1[1], ffn2_w3[1], ffn2_w2[1])]

        PROJ = [("q", 0), ("q", 1), ("ff", 2), ("ff", 3), ("fb", 4), ("fb", 5), ("i", 6), ("i", 7), ("g", 8), ("g", 9),
                ("aq", 10), ("aq", 11), ("ak", 12), ("av", 12)] + [("ga", 13 + i) for i in range(4)] + \
               [("gb", 17 + i) for i in range(4)]
        ROUND_AT = 8
        PAIRS = 3
        LATER = 4
        EARLY = len(PROJ) - LATER
        LATER_BANK = (4, 2, 3, 7)
        LATER_UNIT = 3

        block = ctx.enter_context(nc.Block())

        @block.sync
        def _(sp):
            def load(n, src, view, more=0):
                wait_free(sp, n, more)
                sp.dma_start(view, src).then_inc(slot_full[n % SLOTS], 16)

            def cols(n, w, first, width, k_tiles):
                load(n, w.rearrange("(k p) c -> p k c", p=P)[:, :, first:first + width],
                     slot(n)[:, 0:k_tiles * width].rearrange("p (k c) -> p k c", k=k_tiles))

            sp.dma_start(consts[:, :], constants).then_inc(sem("consts_in"), 16)
            sp.dma_start(tok[:, :, :], x[0].rearrange("(t p) d -> p t d", p=P)).then_inc(sem("x_in"), 16)
            def rows_in(names):
                for name, rows, row, a in names:
                    src = as_rows(a)
                    sp.dma_start(rows[row:row + src.shape[0], :], src
                                 ).then_inc(sem("first_gains_in" if row < ROWS_FIRST and rows is rows_a else "rows_in"), 16)

            vectors = [(name, rows_a, row, vectors_a[name]) for name, row in ROWS_A.items()] + \
                      [(name, rows_b, row, vectors_b[name]) for name, row in ROWS_B.items()]
            rows_in(vectors[:2])

            def small_inputs():
                rows_in(vectors[2:])
                sp.dma_start(rows_dw, conv_w_dw[0]).then_inc(sem("rows_in"), 16)
                for j, g in enumerate((q_norm_g_2, k_norm_g_2)):
                    for half in range(2):
                        sp.dma_start(qk_gain[64 * half:64 * half + 64, j:j + 1], g.rearrange("a d -> d a")
                                     ).then_inc(sem("gains_in"), 16)
                sp.dma_start(mask_in, masks).then_inc(sem("masks_in"), 16)
                sp.dma_start(router[:, :, :], w_router_2[0].rearrange("(k p) e -> p k e", p=P)).then_inc(sem("router_in"), 16)
                sp.dma_start(pos_i[:, :], positions.partition_broadcast(P)).then_inc(sem("positions_in"), 16)
                sp.wait_ge(sem("x_turned"), 4)
                sp.dma_start(tok[:, :, :], ctx_2[0].rearrange("(t p) d -> p t d", p=P)).then_inc(sem("ctx_in"), 16)

            def ffn(f):
                n0 = FIRST[f"ffn{f}"]
                w1, w3, w2 = w_ffn[f]

                def up(n, w, c, more):
                    wait_free(sp, n, more)
                    src = w.rearrange("(k p) (s c) -> s p k c", p=P, c=FF_CHUNK)[bass.ds(c, 1)]
                    sp.dma_start(slot(n).rearrange("p (k c) -> p k c", k=KD),
                                 src.rearrange("o p k c -> p (o k) c")).then_inc(slot_full[n % SLOTS], 16)

                def down(n, c, more):
                    wait_free(sp, n, more)
                    src = w2.rearrange("(s k p) c -> s p k c", p=P, k=2)[bass.ds(c, 1)]
                    sp.dma_start(slot(n).rearrange("p (k c) -> p k c", k=2),
                                 src.rearrange("o p k c -> p (o k) c")).then_inc(slot_full[n % SLOTS], 16)

                up(n0, w1, 0, 0)
                up(n0 + 1, w3, 0, 0)
                if f == 0:
                    small_inputs()
                first = 2 if f == 0 else 0
                for c in range(first):
                    n = n0 + 2 + 3 * c
                    up(n, w1, c + 1, 0)
                    up(n + 1, w3, c + 1, 0)
                    down(n + 2, c, 0)
                with sp.Fori(0, (FF_STEPS - 1 - first) // 2) as i:
                    for j in range(first, first + 2):
                        n = n0 + 2 + 3 * j
                        up(n, w1, 2 * i + (1 + j), 6 * i)
                        up(n + 1, w3, 2 * i + (1 + j), 6 * i)
                        down(n + 2, 2 * i + j, 6 * i)
                down(n0 + 32, FF_STEPS - 1, 0)

            ffn(0)
            for j in range(KD):
                cols(FIRST["pw1"] + j, conv_w_pw1[0], D * (j % 2) + 256 * (j // 2), 256, KD)
            def mod_chunk(c):
                for half in range(2):
                    n = MOD_SLOT[c] + half
                    load(n, w_mod_2[0].rearrange("(k p) c -> p k c", p=P)[:, 4 * half:4 * half + 4, 512 * c:512 * c + 512],
                         slot(n).rearrange("p (k c) -> p k c", k=4))

            for c in range(MOD_EARLY):
                mod_chunk(c)
            for j in range(4):
                cols(FIRST["pw2"] + j, conv_w_pw2[0], 256 * j, 256, KD)
            ffn(1)
            ffn(2)
            mod_chunk(6)
            for j in range(4):
                cols(FIRST["mla_a"] + j, mla_w_a[0], 256 * j, 256 if j < 3 else ROPE, KD)
            mod_chunk(7)
            for j in range(4):
                cols(FIRST["uq"] + j, mla_w_uq[0].rearrange("c h d -> c (h d)"), 384 * j, 384, 4)
            for j in range(2):
                cols(FIRST["ukv"] + j, mla_w_ukv[0].rearrange("c h d -> c (h d)"), 1024 * j, 1024, 2)
            mod_chunk(8)
            for j in range(4):
                cols(FIRST["mla_o"] + j, mla_w_o[0], 256 * j, 256, KD)
            ffn(3)
            for c in (9, 10, 11):
                mod_chunk(c)
            for j in range(21):
                cols(FIRST["w_in"] + j, w_in_2[0], 256 * j, 256, KD)
            for j in range(2):
                cols(FIRST["branch"] + j, w_branch_a_2[0], 512 * j, 512, 4)
            for j in range(2):
                cols(FIRST["branch"] + 2 + j, w_branch_b_2[0], 512 * j, 512, 4)
            for j in range(4):
                cols(FIRST["w_out"] + j, w_out_2[0], 256 * j, 256, KD)
            exp_tiles = [w[0].rearrange("e (j k p) c -> j e p k c", p=P, k=2)[j]
                         for w in (w_exp_gate_2, w_exp_up_2, w_exp_down_2) for j in range(4)]
            def expert_slot(s, e, more=None):
                n = FIRST["experts"] + 12 * e + s - (BESIDE if e > 0 else 0)
                view = slot(n).rearrange("p (k c) -> p k c", k=2)
                src = exp_tiles[s][e] if more is None else exp_tiles[s][e:][bass.ds(more, 1)].rearrange("o p k c -> p (o k) c")
                sp.dma_start(view, src).then_inc(slot_full[n % SLOTS], 16)

            for s in range(SLOTS):
                wait_free(sp, FIRST["experts"] + s)
                expert_slot(s, 0)
            sp.wait_ge(sem("merged_ready"), 2)
            for i in range(AHEAD):
                sp.dma_start(ahead[:, i, :].rearrange("p (k c) -> p k c", k=2), exp_tiles[SLOTS + i][0]
                             ).then_inc(sem(f"ahead_{i}"), 16)
            for s in range(EXTRA):
                if s == 1:
                    sp.wait_ge(sem("sumsq_ready"), NORM["experts"])
                sp.wait_ge(sem(f"ahead_{s}"), 16)
                sp.dma_start(extra[s].rearrange("p (k c) -> p k c", k=2), exp_tiles[s][1]).then_inc(sem(f"ahead_{s}"), 16)
            for s in range(SLOTS):
                sp.wait_ge(slot_free, FIRST["experts"] + s + 1)
                expert_slot(EXTRA + s, 1)
            LAST = EXTRA + SLOTS
            with sp.Fori(0, EXPERTS - 2) as i:
                for m in range(LAST, LAST + 12):
                    e, s = 1 + m // 12, m % 12
                    wait_free(sp, FIRST["experts"] + 12 * e + s, 12 * i)
                    expert_slot(s, e, i)
            for s in range(LAST, 12):
                wait_free(sp, FIRST["experts"] + 12 * (EXPERTS - 1) + s)
                expert_slot(s, EXPERTS - 1)
            for i in range(2 * TT):
                g, t = i // TT, i % TT
                sp.wait_ge(sem("rows_out"), i + 1)
                sp.dma_start(out[0].rearrange("(t p) d -> t p d", p=P)[t][:, 512 * g:512 * g + 512],
                             tok[:, t, 512 * g:512 * g + 512]).then_inc(sem("stored"), 16)
            sp.wait_ge(sem("stored"), 16 * 2 * TT)

        @block.tensor
        def _(pe):
            mm = pe.matmul

            def done(ins):
                ins.then_inc(slot_free, 1)

            def wait_split(n, o, more_slots=0):
                if o == 0:
                    pe.wait_ge(sem("half_split"), HALF[n] // 2 + 1 + more_slots)
                else:
                    pe.wait_ge(slot_free, n + 1 + more_slots)

            def mm3(out_, n, o, k, moving, start, stop, **kw):
                hi, lo = half_part(n, o, 0)[:, k, :], half_part(n, o, 1)[:, k, :]
                mm(out_, hi, moving(0), start=start, stop=False, **kw)
                mm(out_, hi, moving(1), start=False, stop=False, **kw)
                return mm(out_, lo, moving(0), start=False, stop=stop, **kw)

            def wait_x(name, pieces=None):
                pe.wait_ge(sem("x_split_ready"), X_BEFORE[name] + (pieces or X_PIECES[name]))

            pe.wait_ge(sem("consts_in"), 16)
            pe.wait_ge(sem("x_in"), 16)
            for k in range(KD):
                for t in range(TT):
                    last = pe.transpose(ps[:, 2 + k // 2, (k % 2) * T + t * P:(k % 2) * T + t * P + P],
                                        tok[:, t, k * P:k * P + P], ident)
                if k % 2 == 1:
                    last.then_inc(sem("x_turned"), 1)
            pe.wait_ge(sem("first_gains_in"), 32)
            pe.transpose(ps[:, 0, 0:ROWS_FIRST], rows_a[0:ROWS_FIRST, :], ident[0:ROWS_FIRST, 0:ROWS_FIRST]
                         ).then_inc(sem("first_gains_turned"), 1)

            def sum_squares(m, k_tiles, n, bank, first=0):
                per = k_tiles // SQ_PIECES[m]
                for i in range(k_tiles):
                    if i % per == 0:
                        pe.wait_ge(sem("squares_ready"), SQ_BEFORE[m] + i // per + 1)
                    last = mm(ps[:, bank, 0:n], ones[:, 0:P], squares[:, first + i, 0:n],
                              start=(i == 0), stop=(i == k_tiles - 1))
                last.then_inc(sem("sumsq_ready"), 1)

            x_in = xn[:, :, T:2 * T]

            def ffn(f):
                n0 = FIRST[f"ffn{f}"]
                steps = FF_STEPS * f

                def up(n, bank, more, first=False):
                    for o in range(2):
                        wait_split(n, o, more)
                        for k in range(KD):
                            if first and o == 0 and k % 2 == 0:
                                wait_x(f"ffn{f}", k // 2 + 1)
                            last = mm3(ps[:, bank, o * T:o * T + T], n, o, k, lambda part: x_split[:, part, k, :],
                                       start=(k == 0), stop=(k == KD - 1))
                        last.then_inc(half_done, 1)

                def down(n, c, more_slot, more, final=False):
                    pe.wait_ge(sem("hid_split_ready"), steps + c + 1 + more)
                    for o in range(2):
                        wait_split(n, o, more_slot)
                        for d in range(KD):
                            last = mm3(ps[:, d // 2, (d % 2) * T:(d % 2) * T + T], n, o, d,
                                       lambda part: hid_split[:, c % 2, part, o, :],
                                       start=False, stop=False, skip_group_check=True)
                            if final and o == 1 and d in (1, 3, 5):
                                last.then_inc(sem("ffn_out"), 1)
                        last.then_inc(half_done, 1)

                up(n0, 4, 0, first=True)
                sum_squares(f"ffn{f}", KD, T, 7)
                if f > 0:
                    pe.wait_ge(sem("h_updated"), 4 * UPDATES[f])
                for b in range(4):
                    mm(banks(b, 1), zero_w[:, 0:P], zero_w[:, :], start=True, stop=False, skip_group_check=True)
                up(n0 + 1, 6, 0)
                pe.wait_ge(sem("std_ready"), NORM[f"ffn{f}"])
                with pe.Fori(0, FF_STEPS // 2) as i:
                    for j in range(2):
                        n = n0 + 2 + 3 * j
                        b = 4 + (1 + j) % 2
                        up(n, b, 6 * i)
                        up(n + 1, b + 2, 6 * i)
                        down(n + 2, j, 6 * i, 2 * i)
                down(n0 + 32, FF_STEPS - 1, 0, 0, final=True)

            def split_product(n, bank, first=None):
                for o in range(2):
                    wait_split(n, o)
                    for k in range(KD):
                        if first is not None and o == 0 and k % 2 == 0:
                            wait_x(first, k // 2 + 1)
                        last = mm3(ps[:, bank, o * T:o * T + T], n, o, k, lambda part: x_split[:, part, k, :],
                                   start=(k == 0), stop=(k == KD - 1))
                    last.then_inc(half_done, 1)

            def square_product(name, n_slots, src, bank0=0, k_tiles=KD, half_cols=256, halves=None):
                for j in range(n_slots):
                    n = FIRST[name] + j
                    wait_full(pe, n)
                    per = half_cols // P
                    for o in range(per):
                        tile = j * per + o
                        for k in range(k_tiles):
                            if halves is not None and tile == 0 and k % 4 == 0:
                                pe.wait_ge(sem(halves), k // 4 + 1)
                            last = mm(ps[:, bank0 + tile // 2, (tile % 2) * T:(tile % 2) * T + T],
                                      slot(n)[:, k * half_cols + o * P:k * half_cols + o * P + P], src[:, k, :],
                                      start=(k == 0), stop=(k == k_tiles - 1))
                    done(last)

            pe.wait_ge(sem("gains_ready"), 1)
            ffn(0)

            for j in range(KD):
                n = FIRST["pw1"] + j
                if j >= 4 and j % 2 == 0:
                    pe.wait_ge(sem("glu_ready"), j // 2 - 1)
                split_product(n, j % 4, first="pw1" if j == 0 else None)
                if j == 0:
                    sum_squares("conv_in", KD, T, 4)
                    pe.wait_ge(sem("rows_in"), 16 * (len(ROWS_A) - 2 + len(ROWS_B) + 1))
                    pe.transpose(ps[:, 5, 0:N_ROWS_B], rows_b, ident[0:N_ROWS_B, 0:N_ROWS_B])
                    pe.transpose(ps[:, 5, N_ROWS_B:N_ROWS_B + N_ROWS_A], rows_a, ident[0:N_ROWS_A, 0:N_ROWS_A])
                    for k in range(KD):
                        last = pe.transpose(ps[:, 6, k * CONV_W:(k + 1) * CONV_W], rows_dw[:, k * P:k * P + P],
                                            ident[0:CONV_W, 0:CONV_W])
                    last.then_inc(sem("rows_turned"), 1)

            def mod_product(c, cond, bank):
                for half in range(2):
                    n = MOD_SLOT[c] + half
                    wait_full(pe, n)
                    for j in range(4):
                        last = mm(ps[32 * j:32 * j + 32, bank, :], cond[:, 4 * half + j, :],
                                  slot(n)[:, 512 * j:512 * j + 512], start=(half == 0), stop=(half == 1))
                    done(last)

            def turn_mod(c, rows, bank, column):
                pe.wait_ge(sem("mod_copied"), c + 1)
                for b in range(4):
                    last = mm(ps[:, bank, column + 2 * b:column + 2 * b + 2], rows[:, c % 2, P * b:P * b + P],
                              const("cond_sel"), start=True, stop=True)
                last.then_inc(sem("mod_turned"), 1)

            def tap(q):
                j, w = TAPS[q]
                pe.wait_ge(sem("diag_ready"), q + 1)
                if w == 0:
                    pe.wait_ge(sem("glu_ready"), j // 2 + 1)
                c = PE_TILES.index(j) * T
                mm(ps[:, 7, c:c + T], diag[:, q % DIAGS, :], conv_in[:, j, w:w + T], start=(w == 0),
                   stop=(w == CONV_W - 1)).then_inc(sem("diag_used"), 1)

            pe.wait_ge(sem("cond_ready"), 1)
            for c in range(MOD_EARLY):
                if c >= 2:
                    pe.wait_ge(sem("mod_copied"), c - 1)
                mod_product(c, cond_pad, 5 + c % 2)
                if c >= 1:
                    turn_mod(c - 1, mod_rows, 4, T + 8 * (c - 1))
                for q in range(TAP_STEPS[c], TAP_STEPS[c + 1]):
                    tap(q)
                if c == 2:
                    pe.wait_ge(sem("ctx_in"), 16)
                    pe.wait_ge(sem("glu_ready"), KD // 2)
                    for k in range(KD):
                        for t in range(TT):
                            last = pe.transpose(ps[:, k // 2, (k % 2) * T + t * P:(k % 2) * T + t * P + P],
                                                tok[:, t, k * P:k * P + P], ident)
                    last.then_inc(sem("ctx_turned"), 1)
                if c == 3:
                    sum_squares("context", KD, T, 0)
            turn_mod(MOD_EARLY - 1, mod_rows, 4, T + 8 * (MOD_EARLY - 1))

            sum_squares("conv_out", KD, T, 4)
            for j in range(4):
                split_product(FIRST["pw2"] + j, j, first="pw2" if j == 0 else None)

            pe.wait_ge(sem("mod_ready"), 2)
            ffn(1)
            ffn(2)

            sum_squares("mla", KD, T, 4)
            mod_product(6, cond_late, 5)
            turn_mod(6, mod_rows_late, 7, 0)
            for j in range(4):
                n = FIRST["mla_a"] + j
                wait_full(pe, n)
                for o in range(2):
                    for k in range(KD):
                        if j == 0 and o == 0 and k % 2 == 0:
                            pe.wait_ge(sem("piece_normed"), NORM_PIECES["mla"] + k // 2 + 1)
                        if j < 3:
                            last = mm(ps[:, j, o * T:o * T + T], slot(n)[:, k * 256 + o * P:k * 256 + o * P + P],
                                      x_in[:, k, :], start=(k == 0), stop=(k == KD - 1))
                        else:
                            last = mm(ps[64 * o:64 * o + 64, j, 0:T], slot(n)[:, k * ROPE:k * ROPE + ROPE],
                                      x_in[:, k, :], start=(k == 0), stop=(k == KD - 1))
                done(last)
            sum_squares("mla_q", 4, T, 4)
            pe.wait_ge(sem("mod_taken"), 1)
            sum_squares("mla_kv", 2, T, 7, 4)
            mod_product(7, cond_late, 5)
            turn_mod(7, mod_rows_late, 6, 0)
            pe.wait_ge(sem("xn_ready"), XN["mla_q"])
            pe.wait_ge(sem("mod_taken"), 2)
            for j in range(4):
                n = FIRST["uq"] + j
                wait_full(pe, n)
                if j >= 2:
                    pe.wait_ge(sem("uq_taken"), j - 1)
                b = 5 if j % 2 == 0 else 0
                for o in range(2):
                    for k in range(4):
                        mm(ps[:, b, o * T:o * T + T], slot(n)[:, k * 384 + 192 * o:k * 384 + 192 * o + P],
                           latent_n[:, k, :], start=(k == 0), stop=(k == 3))
                for k in range(4):
                    for o in range(2):
                        c = k * 384 + 192 * o + NOPE
                        last = mm(ps[64 * o:64 * o + 64, b + 1, 0:T], slot(n)[:, c:c + ROPE], latent_n[:, k, :],
                                  start=(k == 0), stop=(k == 3))
                done(last)
            pe.wait_ge(sem("uq_taken"), 4)
            pe.wait_ge(sem("xn_ready"), XN["mla_kv"])
            for j in range(2):
                n = FIRST["ukv"] + j
                wait_full(pe, n)
                if j == 1:
                    pe.wait_ge(sem("ukv_taken"), 1)
                for o in range(4):
                    for k in range(2):
                        mm(ps[:, o // 2, (o % 2) * T:(o % 2) * T + T], slot(n)[:, k * D + 256 * o:k * D + 256 * o + P],
                           latent_n[:, 4 + k, :], start=(k == 0), stop=(k == 1))
                for t in range(TT):
                    for k in range(2):
                        w = slot(n)[:, k * D:(k + 1) * D].rearrange("p (o c) -> p o c", o=4)[:, :, NOPE:NOPE + VH]
                        last = mm(ps[:, 2 + t, :], latent_n[:, 4 + k, t * P:t * P + P], w, start=(k == 0), stop=(k == 1))
                done(last)
            flat = rope_in.rearrange("p a t -> p (a t)")
            for c, (a, b) in enumerate(((0, 512), (512, 1024), (1024, 1280))):
                last = mm(ps[:, 5 + c, 0:b - a], const("rope_rot"), flat[:, a:b], start=True, stop=True)
            last.then_inc(sem("rope_turned"), 1)
            pe.wait_ge(sem("ukv_taken"), 2)
            mod_product(8, cond_late, 0)
            turn_mod(8, mod_rows_late, 1, 0)
            pe.wait_ge(sem("rope_ready"), 1)
            pe.wait_ge(sem("mod_taken"), 3)

            def mla_scores(hd):
                if hd >= 2:
                    pe.wait_ge(sem("mla_exp"), 2 * (hd - 1))
                base = 64 * (hd % 2)
                for t in range(TT):
                    o = ps[:, hd % 2, P * t:P * t + P * (t + 1)]
                    keys = P * (t + 1)
                    mm(o, q_nope[:, hd, t * P:t * P + P], k_nope[:, hd, 0:keys], start=True, stop=False)
                    mm(o, rope_a[base:base + 64, hd // 2, t * P:t * P + P], rope_a[base:base + 64, 4, 0:keys],
                       start=False, stop=False)
                    last = mm(ps[:, hd % 2, 2 * t * P:2 * t * P + P],
                              const("mask_rows", 1), const("mask_cols", 1), start=False, stop=True)
                last.then_inc(sem("mla_scores"), 1)

            def mla_turn(hd):
                pe.wait_ge(sem("mla_p"), hd + 1)
                if hd >= 2:
                    pe.wait_ge(sem("mla_pt"), hd - 1)
                for b in range(3):
                    last = pe.transpose(ps[:, 2 + hd % 2, b * P:b * P + P], mla_p[:, hd % 2, b * P:b * P + P], ident)
                last.then_inc(sem("mla_turned"), 1)

            def mla_values(hd):
                pe.wait_ge(sem("mla_pt"), hd + 1)
                if hd >= 2:
                    pe.wait_ge(sem("mla_out_taken"), hd - 1)
                mm(ps[:, 4 + hd % 2, 0:T], v_tok[:, 0, hd, :],
                   mla_pt[:, hd % 2, 0:2, :].rearrange("p b q -> p (b q)"), start=True, stop=False)
                last = mm(ps[:, 4 + hd % 2, P:T], v_tok[:, 1, hd, :], mla_pt[:, hd % 2, 2, :], start=False, stop=True)
                last.then_inc(sem("mla_out"), 1)

            for i in range(MLA_HEADS + 2):
                if i < MLA_HEADS:
                    mla_scores(i)
                if 1 <= i <= MLA_HEADS:
                    mla_turn(i - 1)
                if i >= 2:
                    mla_values(i - 2)
            pe.wait_ge(sem("mla_out_taken"), MLA_HEADS)
            square_product("mla_o", 4, o_mla)

            ffn(3)

            sum_squares("final1", KD, T, 4)
            mod_product(9, cond_late, 5)
            sum_squares("tokens", KD, T, 6)
            turn_mod(9, mod_rows_late, 2, 0)
            mod_product(10, cond_late, 1)
            mod_product(11, cond_late, 7)
            turn_mod(10, mod_rows_late, 3, 0)
            pe.wait_ge(sem("modulated"), SHIFTED["tokens"])
            pe.wait_ge(sem("mod_taken"), 5)

            def hg_round(r):
                pe.wait_ge(sem("round_ready"), r + 1)
                if r >= 1:
                    pe.wait_ge(sem("round_taken"), r)
                for s in range(TT):
                    t = 1 - s if r == ROUND_WIDE else s
                    for hd in range(HG_HEADS):
                        q = hg_q if r == ROUND_DIAG else q_lvl[:, r % 2]
                        last = mm(ps[:, 6 + s, hd * P:hd * P + P], k_lvl[:, r % 2, hd, s * P:s * P + P],
                                  q[:, hd, t * P:t * P + P], start=True, stop=True)
                last.then_inc(sem("round_scores"), 1)

            def project(step):
                name, s = PROJ[step]
                n = FIRST["w_in"] + s
                b = 2 * (step % PAIRS) if step < EARLY else LATER_BANK[step - EARLY]
                wait_full(pe, n)
                if PAIRS <= step < EARLY:
                    pe.wait_ge(sem("proj_taken"), step - PAIRS + 1)
                if name in ("ff", "fb"):
                    for o in range(2):
                        for k in range(KD):
                            last = mm(ps[:, b + o, :], slot(n)[:, k * 256 + o * P:k * 256 + o * P + P], xn[:, k, :],
                                      start=(k == 0), stop=(k == KD - 1))
                elif name == "i":
                    for t in range(4):
                        for k in range(KD):
                            last = mm(ps[:, b + t // 2, (t % 2) * T:(t % 2) * T + T], xn[:, k, t * P:t * P + P],
                                      slot(n)[:, k * 256:k * 256 + 256], start=(k == 0), stop=(k == KD - 1))
                elif name == "ak":
                    for o in range(ATT_KV):
                        for k in range(KD):
                            for half in range(2):
                                c = k * 256 + o * ATT_HD
                                last = mm(ps[64 * half:64 * half + 64, b + o, :], slot(n)[:, c:c + ATT_HD], xn[:, k, :],
                                          start=(k == 0), stop=(k == KD - 1))
                elif name == "av":
                    for t in range(4):
                        for k in range(KD):
                            last = mm(ps[:, b, t * P:t * P + P], xn[:, k, t * P:t * P + P],
                                      slot(n)[:, k * 256 + P:k * 256 + 256], start=(k == 0), stop=(k == KD - 1))
                else:
                    for o in range(2):
                        for k in range(KD):
                            if step == 0 and o == 0 and k % 2 == 0:
                                pe.wait_ge(sem("modulated"), SHIFTED["tokens"] + k // 2 + 1)
                            last = mm(ps[:, b, o * T:o * T + T], slot(n)[:, k * 256 + o * P:k * 256 + o * P + P],
                                      x_in[:, k, :], start=(k == 0), stop=(k == KD - 1))
                if name == "ak":
                    last.then_inc(sem("ak_product"), 1)
                else:
                    done(last)

            for step in range(EARLY):
                project(step)
                if step == 0:
                    turn_mod(11, mod_rows_late, 6, 0)
                if step == ROUND_AT - 1:
                    pe.wait_ge(sem("mod_taken"), 6)
                if step >= ROUND_AT and step - ROUND_AT < ROUNDS:
                    hg_round(step - ROUND_AT)

            pe.wait_ge(sem("proj_taken"), EARLY)
            project(EARLY)
            pe.wait_ge(sem("key_dec_ready"), 1)
            for dr in range(2):
                for s in range(TT):
                    for hd in range(HG_HEADS):
                        last = pe.transpose(ps[:, 2 * dr + s, hd * P:hd * P + P], key_dec[:, dr, hd, s * P:s * P + P], ident)
            last.then_inc(sem("key_dec_turned"), 1)
            pe.wait_ge(sem("proj_taken"), EARLY + 1)
            pe.wait_ge(sem("key_dec_t_ready"), 1)
            for dr in range(2):
                for hd in range(HG_HEADS):
                    for s in range(TT):
                        last = mm(ps[:, 4 + dr, hd * P:hd * P + P], key_dec_t[:, dr, s, hd * P:hd * P + P],
                                  hg_v[:, s, hd * P:hd * P + P], start=(s == 0), stop=(s == TT - 1))
            last.then_inc(sem("state_product"), 1)
            pe.wait_ge(sem("state_ready"), 1)
            pe.wait_ge(sem("round_taken"), ROUNDS)
            pe.wait_ge(sem("q_dec_ready"), 1)
            for hd in range(HG_HEADS):
                o = ps[:, hd // 2, (hd % 2) * T:(hd % 2) * T + T]
                for s in range(TT):
                    mm(o, hg_v[:, TT + s, hd * P:hd * P + P], hg_p[:, s, hd, :], start=(s == 0), stop=False)
                for dr in range(2):
                    last = mm(o, state0[:, dr, hd, :], q_dec[:, dr, hd, :], start=False, stop=(dr == 1))
            last.then_inc(sem("hg_out"), 1)
            pe.wait_ge(sem("hg_sq_ready"), 1)
            for c in range(2):
                last = mm(ps[:, 2 + c, :], ones[:, 0:P], o_sq[:, 2 * c:2 * c + 2, :].rearrange("p a t -> p (a t)"),
                          start=True, stop=True)
            last.then_inc(sem("hg_sumsq"), 1)

            pe.wait_ge(sem("att_sq_ready"), 1)
            for c in range(2):
                mm(ps[:, 4 + c, :], const("headsum"), att_sq[:, 512 * c:512 * c + 512], start=True, stop=True)
            pe.wait_ge(sem("round_taken"), ROUNDS)
            for c in range(2):
                last = mm(ps[:, 6 + c, :], const("headsum"), att_sq[:, 1024 + 512 * c:1536 + 512 * c], start=True, stop=True)
            last.then_inc(sem("att_sumsq"), 1)
            pe.wait_ge(sem("hg_log"), 1)
            project(EARLY + 1)
            pe.wait_ge(sem("att_n_ready"), 1)
            qf = att_qr.rearrange("p a t -> p (a t)")
            for c in range(2):
                mm(ps[:, 4 + c, :], const("axial_rot"), qf[:, 512 * c:512 * c + 512], start=True, stop=True)
            for o in range(ATT_KV):
                last = mm(ps[:, 6, o * T:o * T + T], const("axial_rot"), att_kr[:, o, T:2 * T], start=True, stop=True)
            last.then_inc(sem("att_turned"), 1)
            project(EARLY + 2)
            pe.wait_ge(sem("att_ready"), 1)
            pe.wait_ge(sem("hg_normed"), 1)
            pe.wait_ge(sem("proj_taken"), EARLY + 3)
            units = [(hd, t) for hd in range(ATT_HEADS) for t in range(TT)]

            def att_scores(u):
                hd, t = units[u]
                base = 64 * (hd % 2)
                if u >= 2:
                    pe.wait_ge(sem("att_exp"), u - 1)
                mm(ps[:, u % 2, :], att_qr[base:base + 64, hd // 2, t * P:t * P + P], att_kr[base:base + 64, hd // 4, :],
                   start=True, stop=True).then_inc(sem("att_scores"), 1)

            def att_turn(u):
                pe.wait_ge(sem("att_p"), u + 1)
                if u >= 2:
                    pe.wait_ge(sem("att_pt"), u - 1)
                for b in range(4):
                    last = pe.transpose(ps[:, 2 + u % 2, b * P:b * P + P], att_p[:, u % 2, b * P:b * P + P], ident)
                last.then_inc(sem("att_p_turned"), 1)

            def att_values(u):
                hd, t = units[u]
                base = 64 * (hd % 2)
                pe.wait_ge(sem("att_pt"), u + 1)
                pair = hd // 2
                for b in range(4):
                    last = mm(ps[base:base + 64, 4 + pair // 2, (pair % 2) * T + t * P:(pair % 2) * T + t * P + P],
                              att_v[:, b, (hd // 4) * ATT_HD:(hd // 4) * ATT_HD + ATT_HD], att_pt[:, u % 2, b, :],
                              start=(b == 0), stop=(b == 3))
                last.then_inc(sem("att_out"), 1)

            for i in range(len(units) + 2):
                if i < len(units):
                    att_scores(i)
                if i == LATER_UNIT:
                    project(EARLY + 3)
                if 1 <= i <= len(units):
                    att_turn(i - 1)
                if i >= 2:
                    att_values(i - 2)

            pe.wait_ge(sem("att_exp"), len(units))
            pe.wait_ge(sem("att_pt"), len(units))
            for br, src in ((0, o_hg), (1, o_att)):
                if br == 1:
                    pe.wait_ge(sem("o_att_ready"), 1)
                for j in range(2):
                    n = FIRST["branch"] + 2 * br + j
                    wait_full(pe, n)
                    if br == 1:
                        pe.wait_ge(sem("branch_taken"), j + 1)
                    for o in range(4):
                        for k in range(4):
                            last = mm(ps[:, 2 * j + o // 2, (o % 2) * T:(o % 2) * T + T],
                                      slot(n)[:, k * 512 + o * P:k * 512 + o * P + P], src[:, k, :],
                                      start=(k == 0), stop=(k == 3))
                    done(last)
            square_product("w_out", 4, merged, bank0=4, halves="merged_ready")

            sum_squares("experts", KD, T, 0)
            pe.wait_ge(sem("router_in"), 16)
            for t in range(TT):
                for k in range(KD):
                    if t == 0 and k % 2 == 0:
                        pe.wait_ge(sem("modulated"), SHIFTED["experts"] + k // 2 + 1)
                    last = mm(ps[:, 1, t * EXPERTS:(t + 1) * EXPERTS], x_in[:, k, t * P:t * P + P], router[:, k, :],
                              start=(k == 0), stop=(k == KD - 1))
            last.then_inc(sem("router_scores"), 1)
            def rows(k):
                for t in range(TT):
                    last = pe.transpose(ps[:, 4 + 2 * t + k // 4, (k % 4) * P:(k % 4) * P + P],
                                        x_in[:, k, t * P:t * P + P], ident)
                return last

            for k in range(2):
                rows(k)
            pe.wait_ge(sem("aff_ready"), 1)
            for t in range(TT):
                last = pe.transpose(ps[0:EXPERTS, 0, t * P:t * P + P], aff[:, t, :], ident)
            last.then_inc(sem("aff_turned"), 1)
            for k in range(2, KD):
                last = rows(k)
            last.then_inc(sem("rows_back"), 1)
            for b in (2, 3):
                mm(banks(b, 1), zero_w[:, 0:P], zero_w[:, :], start=True, stop=False, skip_group_check=True)
            pe.wait_ge(sem("slots_chosen"), 1)
            for t in range(TT):
                last = pe.transpose(ps[:, 1, t * EXPERTS:(t + 1) * EXPERTS], slot_t[0:EXPERTS, t * P:t * P + P],
                                    ident[0:EXPERTS, 0:EXPERTS])
            last.then_inc(sem("slots_turned"), 1)
            pe.wait_ge(sem("pick_ready"), 1)
            pe.wait_ge(sem("rows_copied"), 1)
            for b in (0, 1):
                mm(banks(b, 1), zero_w[:, 0:P], zero_w[:, :], start=True, stop=False, skip_group_check=True)

            def gather(k, bank, column, first, n):
                o = ps[:, bank, column:column + n * CAP]
                for t in range(TT):
                    last = mm(o, tok[:, t, k * P:k * P + P], picks[:, t, first:first + n, :], start=(t == 0),
                              stop=(t == TT - 1))
                return last

            def spread(more, e):
                pe.wait_ge(sem("pick_cur_ready"), more + (e + 1))
                for t in range(TT):
                    for g in (0, 32):
                        last = mm(ps[g:g + 32, 7, T + t * P:T + t * P + P], pick_cur[:, t, :], ident, start=True, stop=True)
                last.then_inc(sem("spread_turned"), 1)

            def expert(more, e, take, early=False, gathers=False, final=False):
                def product(m, j, src):
                    w = take(4 * m + j)
                    for k in range(2):
                        for half in range(2):
                            g = 32 * (2 * k + half)
                            last = mm(ps[g:g + 32, 4 + m, :], src[:, 2 * j + k, :],
                                      w[:, k * D + 512 * half:k * D + 512 * half + 512],
                                      start=(j == 0), stop=(j == 3))
                    done(last)

                pe.wait_ge(sem("x_cur_ready"), more + (e + 1))
                pe.wait_ge(sem("x_exp_taken"), 2 if early else 2 + KD)
                for m in range(2):
                    for j in range(4):
                        product(m, j, x_cur)
                pe.wait_ge(sem("hid_ready"), more + (e + 1))
                pe.wait_ge(sem("spread_cur_ready"), more + (e + 1))
                for c in range(4):
                    last = mm(ps[:, 7, 64 * c:64 * c + 64], hid_e[0:64, P * c:P * c + P], ident[0:64, 0:64],
                              start=True, stop=True)
                last.then_inc(sem("hid_turned"), 1)
                pe.wait_ge(sem("hid_t_ready"), more + (e + 1))
                for j in range(4):
                    if j == 2 and not final:
                        spread(more, e + 1)
                        if gathers:
                            gather_others()
                    product(2, j, hid_t)
                pe.wait_ge(sem("y_ready"), more + (e + 1))
                for d in range(KD):
                    half = d // 4
                    last = mm(ps[:, d // 2, (d % 2) * T:(d % 2) * T + T],
                              y_e[32 * half:32 * half + 32, (d % 4) * P:(d % 4) * P + P],
                              spread_cur[32 * half:32 * half + 32, :], start=False, stop=False, skip_group_check=True)
                    if final and d % 2 == 1:
                        last.then_inc(sem("moe_out"), 1)
                if not final:
                    last.then_inc(sem("spread_free"), 1)

            def take_first(s):
                if s < SLOTS:
                    wait_full(pe, FIRST["experts"] + s)
                    return slot(FIRST["experts"] + s)
                pe.wait_ge(sem(f"ahead_{s - SLOTS}"), 16)
                return ahead[:, s - SLOTS, :]

            def gather_others():
                for k in range(KD):
                    if k >= 2:
                        pe.wait_ge(sem("x_exp_taken"), 2 + k - 1)
                    gather(k, 4 + k % 2, 0, FIRST_EXPERTS, EXPERTS - FIRST_EXPERTS).then_inc(sem("x_exp_product"), 1)

            for k in range(KD):
                last = gather(k, 4 + k // 4, (k % 4) * P, 0, FIRST_EXPERTS)
                if k % 4 == 3:
                    last.then_inc(sem("x_exp_product"), 1)
            spread(0, 0)
            expert(0, 0, take_first, early=True)

            def take_later(s, more, e):
                if e == 1 and s < EXTRA:
                    pe.wait_ge(sem(f"ahead_{s}"), 32)
                    return extra[s]
                n = FIRST["experts"] + 12 * e + s - BESIDE
                wait_full(pe, n, more * 32)
                return slot(n)

            expert(0, 1, lambda s: take_later(s, 0, 1), early=True, gathers=True)
            with pe.Fori(0, EXPERTS - 3) as i:
                expert(i, 2, lambda s: take_later(s, i, 2))
            expert(0, EXPERTS - 1, lambda s: take_later(s, 0, EXPERTS - 1), final=True)

            sum_squares("final2", KD, T, 4)
            for g in range(2):
                pe.wait_ge(sem("piece_normed"), NORM_PIECES["final2"] + 2 * g + 2)
                for t in range(TT):
                    for k in range(4 * g, 4 * g + 4):
                        last = pe.transpose(ps[:, 2 * t + g, (k % 4) * P:(k % 4) * P + P], x_in[:, k, t * P:t * P + P], ident)
                    last.then_inc(sem("out_turned"), 1)

        @block.scalar
        def _(act):
            fn = act.activation

            for piece in range(4):
                act.wait_ge(sem("x_turned"), piece + 1)
                fn(h[:, 2 * piece:2 * piece + 2, :].rearrange("p k t -> p (k t)"), ps[:, 2 + piece, :], ACT.Copy
                   ).then_inc(sem("h_loaded"), 1)
            act.wait_ge(sem("gains_ready"), 1)

            def square(src, first, n):
                k_tiles = src.shape[1]
                fn(squares[:, first:first + k_tiles, 0:n], src, ACT.Square).then_inc(sem("squares_ready"), 1)

            def square_pieces(count, before):
                for piece in range(4):
                    act.wait_ge(sem(count), before + piece + 1)
                    square(h[:, 2 * piece:2 * piece + 2, :], 2 * piece, T)

            def root(m, bank, dim, region=0, n=T):
                act.wait_ge(sem("sumsq_ready"), NORM[m])
                fn(std[:, region:region + n], ps[:, bank, 0:n], ACT.Sqrt, bias=eps_col[:, 0:1],
                   scale=1.0 / dim).then_inc(sem("std_ready"), 1)

            x_in = xn[:, :, T:2 * T]

            def split_hi(n, o, columns=True, more_halves=0, more_full=0):
                q = HALF[n] + o
                if q >= HALF_BUFS:
                    act.wait_ge(half_done, q - HALF_BUFS + 1 + more_halves)
                if o == 0:
                    wait_full(act, n, more_full)
                fn(half_part(n, o, 0), half_slot(n, o, columns), ACT.Copy).then_inc(sem("half_hi"), 1)

            def split_hi_slot(n, columns=True):
                for o in range(2):
                    split_hi(n, o, columns)

            def start_products(n0, gain, updates, norm, bank):
                if n0 != FIRST["ffn1"]:
                    split_hi_slot(n0)
                if n0 - 1 in HALF:
                    wait_done(act, n0 - 1 if n0 - 1 == FIRST["pw2"] + 3 else n0 - 2)
                for k in range(KD):
                    if k % 2 == 0 and updates > 0:
                        act.wait_ge(sem("h_updated"), 4 * (updates - 1) + k // 2 + 1)
                    ins = fn(x_split[:, 0, k, :], h[:, k, :], ACT.Copy, scale=gain[:, k:k + 1])
                    if k % 2 == 1:
                        ins.then_inc(sem("x_hi"), 1)
                split_hi(n0 + 1, 0)
                square(h[:, :, :], 0, T)
                split_hi(n0 + 1, 1)
                root(norm, bank, D)

            def ffn(f, gain):
                n0 = FIRST[f"ffn{f}"]
                steps = FF_STEPS * f
                start_products(n0, gain, UPDATES[f], f"ffn{f}", 7)

                def gate(c, more):
                    act.wait_ge(sem("gate_scaled"), steps + c + 1 + more)
                    fn(silu_gate[:, c % 2, :], silu_gate[:, c % 2, :], ACT.Silu).then_inc(sem("silu_ready"), 1)

                def hidden_hi(c, more):
                    act.wait_ge(sem("hidden_ready"), steps + c + 1 + more)
                    fn(hid_split[:, c % 2, 0, :, :], hidden[:, c % 2, :, :], ACT.Copy).then_inc(sem("hid_hi"), 1)

                gate(0, 0)
                with act.Fori(0, FF_STEPS // 2) as i:
                    for j in range(2):
                        n = n0 + 2 + 3 * j
                        for s in range(3):
                            for o in range(2):
                                split_hi(n + s, o, s < 2, 12 * i, 16 * i)
                            if s == 0:
                                hidden_hi(j, 2 * i)
                        gate(1 + j, 2 * i)
                split_hi_slot(n0 + 32, columns=False)
                hidden_hi(FF_STEPS - 1, 0)

            def gains(name, layer):
                return vec_a[:, ROWS_A[name] + KD * layer:ROWS_A[name] + KD * layer + KD]

            def shift(m, c, half, row=0):
                for k in range(KD):
                    if k % 2 == 0:
                        act.wait_ge(sem("piece_normed"), NORM_PIECES[m] + k // 2 + 1)
                    o = xn[:, k, half * T:half * T + T]
                    ins = fn(o, o, ACT.Identity, bias=mod[:, row + k, c:c + 1])
                    if k % 2 == 1:
                        ins.then_inc(sem("modulated"), 1)

            act.wait_ge(sem("h_loaded"), 4)
            ffn(0, gains("ffn_norm1", 0))

            start_products(FIRST["pw1"], gains("mix_norm", 0), 1, "conv_in", 4)
            act.wait_ge(sem("vectors_ready"), 1)
            fn(cond_pad[:, :, 0:2], vec_b[:, 0:2 * KD].rearrange("p (c k) -> p k c", c=2), ACT.Silu
               ).then_inc(sem("cond_ready"), 1)
            def products(tile, first, last):
                j = POOL_TILES[tile]
                if first == 0:
                    act.wait_ge(sem("glu_ready"), j // 2 + 1)
                for w in range(first, last):
                    added = tile * (CONV_W - 1) + w - KD
                    if w > KD:
                        act.wait_ge(sem("tap_added"), added)
                    elif w >= 1 and tile > 0:
                        act.wait_ge(sem("tap_added"), CONV_W - 1 - (CONV_W - 1 - w) % KD)
                    fn(conv_acc[:, j, :] if w == 0 else tap_product[:, w % KD, :], conv_in[:, j, w:w + T], ACT.Copy,
                       scale=w_dw[:, j, w:w + 1]).then_inc(sem("tap_product_ready"), 1)

            def diagonals(first, last):
                for q in range(first, last):
                    j, w = TAPS[q]
                    if q >= DIAGS:
                        act.wait_ge(sem("diag_used"), q - DIAGS + 1)
                    fn(diag[:, q % DIAGS, :], ident, ACT.Copy, scale=w_dw[:, j, w:w + 1]).then_inc(sem("diag_ready"), 1)

            for i in range(KD // 2):
                if i >= 2:
                    diagonals(DIAGS // 2 * (i - 2), DIAGS // 2 * (i - 1))
                if i < KD // 2 - 1:
                    split_hi_slot(FIRST["pw1"] + 2 * i + 2)
                    split_hi_slot(FIRST["pw1"] + 2 * i + 3)
                if i >= 1:
                    products(0, 8 * (i - 1), 8 * i)
                act.wait_ge(sem("glu_gate_scaled"), i + 1)
                fn(glu_sig[:, i % 2, :], glu_sig[:, i % 2, :], ACT.Sigmoid).then_inc(sem("glu_sig_ready"), 1)
            products(0, 24, CONV_W)

            def mod_copy(c, rows, bank):
                wait_done(act, MOD_SLOT[c] + 1)
                if c >= 2:
                    act.wait_ge(sem("mod_turned"), c - 1)
                fn(rows[:, c % 2, :], ps[:, bank, :], ACT.Copy).then_inc(sem("mod_copied"), 1)

            for c in range(MOD_EARLY):
                mod_copy(c, mod_rows, 5 + c % 2)
                diagonals(min(TAP_STEPS[c] + DIAGS, len(TAPS)), min(TAP_STEPS[c + 1] + DIAGS, len(TAPS)))
                products(1, POOL_STEPS[c], POOL_STEPS[c + 1])
                if c == 2:
                    act.wait_ge(sem("ctx_turned"), 1)
                    fn(xn[:, :, 0:T], banks(0, 4).rearrange("p (k t) -> p k t", t=T), ACT.Copy).then_inc(sem("ctx_copied"), 1)
                    square(banks(0, 4).rearrange("p (k t) -> p k t", t=T), 0, T)
                if c == MOD_EARLY - 1:
                    root("context", 0, D, region=T)
                    act.wait_ge(sem("tap_added"), CONV_W - 1)
                    act.wait_ge(sem("conv_done"), 1)
                    square(conv_acc[:, 0:2, :], 0, T)
                if c == MOD_EARLY - 2:
                    split_hi_slot(FIRST["pw2"])
                    split_hi_slot(FIRST["pw2"] + 1)
            act.wait_ge(sem("diag_used"), len(TAPS))
            fn(conv_acc[:, 5:8:2, :], ps[:, 7, :].rearrange("p (a t) -> p a t", t=T), ACT.Copy
               ).then_inc(sem("taps_copied"), 1)
            act.wait_ge(sem("conv_done"), 3)
            square(conv_acc[:, 2:4, :], 2, T)
            act.wait_ge(sem("taps_copied"), 1)
            square(conv_acc[:, 5:8:2, :], 4, T)
            act.wait_ge(sem("conv_done"), 4)
            act.wait_ge(sem("tap_added"), 2 * (CONV_W - 1))
            square(conv_acc[:, 4:8:2, :], 6, T)
            root("conv_out", 4, D)
            for g in range(4):
                act.wait_ge(sem("piece_normed"), NORM_PIECES["conv_out"] + g + 1)
                x_g = x_in[:, 2 * g:2 * g + 2, :]
                fn(x_split[:, 0, 2 * g:2 * g + 2, :], x_g, ACT.Silu)
                fn(x_g, x_g, ACT.Silu).then_inc(sem("x_hi"), 1)
            split_hi_slot(FIRST["pw2"] + 2)
            split_hi_slot(FIRST["pw2"] + 3)
            act.wait_ge(sem("floor_logits"), 1)
            fn(lb_tmp[:, 0:2], lb_tmp[:, 0:2], ACT.Exp).then_inc(sem("floor_exp"), 1)
            split_hi_slot(FIRST["ffn1"])
            shift("context", 1, 0)
            fn(cond_late, cond_pad, ACT.Copy).then_inc(sem("cond_kept"), 1)
            ffn(1, gains("ffn_norm2", 0))
            ffn(2, gains("ffn_norm1", 1))

            square_pieces("h_updated", 4 * 3)
            root("mla", 4, D)
            mod_copy(6, mod_rows_late, 5)
            act.wait_ge(sem("angles_ready"), 1)
            fn(sin_t, ang, ACT.Sin).then_inc(sem("trig_ready"), 1)
            fn(cos_t, turns, ACT.Sin).then_inc(sem("trig_ready"), 1)
            wait_done(act, FIRST["mla_a"] + 1)
            square(banks(0, 2).rearrange("p (k t) -> p k t", t=T), 0, T)
            wait_done(act, FIRST["mla_a"] + 2)
            square(banks(2, 1).rearrange("p (k t) -> p k t", t=T), 4, T)
            wait_done(act, FIRST["mla_a"] + 3)
            fn(rope_in[:, 4, :], ps[:, 3, 0:T], ACT.Copy)
            root("mla_q", 4, Q_LORA)
            root("mla_kv", 7, KV_LORA, region=T)
            mod_copy(7, mod_rows_late, 5)
            for j in range(4):
                b = 5 if j % 2 == 0 else 0
                wait_done(act, FIRST["uq"] + j)
                fn(q_nope[:, 2 * j:2 * j + 2, :].rearrange("p a t -> p (a t)"), ps[:, b, :], ACT.Copy)
                fn(rope_in[:, j, :], ps[:, b + 1, 0:T], ACT.Copy).then_inc(sem("uq_taken"), 1)
            for j in range(2):
                wait_done(act, FIRST["ukv"] + j)
                fn(k_nope[:, 4 * j:4 * j + 4, :].rearrange("p a t -> p (a t)"), banks(0, 2), ACT.Copy)
                fn(v_tok[:, :, 4 * j:4 * j + 4, :].rearrange("p s a v -> p s (a v)"), ps[:, 2:4, :], ACT.Copy
                   ).then_inc(sem("ukv_taken"), 1)
            mod_copy(8, mod_rows_late, 0)

            def mla_exp(hd):
                act.wait_ge(sem("mla_max"), hd + 1)
                if hd >= 2:
                    act.wait_ge(sem("mla_turned"), hd - 1)
                for t in range(TT):
                    a, b = (0, P) if t == 0 else (P, 3 * P)
                    fn(mla_p[:, hd % 2, a:b], ps[:, hd % 2, a:b], ACT.Exp, bias=mla_stat[:, 0, hd, t:t + 1],
                       scale=MLA_SCALE, accum_out=mla_stat[:, 1, hd, t:t + 1]).then_inc(sem("mla_exp"), 1)

            def mla_copy(hd):
                act.wait_ge(sem("mla_turned"), hd + 1)
                if hd >= 2:
                    act.wait_ge(sem("mla_out"), hd - 1)
                fn(mla_pt[:, hd % 2, :, :].rearrange("p b q -> p (b q)"), ps[:, 2 + hd % 2, 0:3 * P], ACT.Copy
                   ).then_inc(sem("mla_pt"), 1)

            for i in range(MLA_HEADS + 1):
                if i < MLA_HEADS:
                    mla_exp(i)
                if i >= 1:
                    mla_copy(i - 1)
            act.wait_ge(sem("mla_out"), MLA_HEADS)
            ffn(3, gains("ffn_norm2", 1))

            square_pieces("h_updated", 4 * 5)
            root("final1", 4, D)
            square_pieces("h_normed", 0)
            mod_copy(9, mod_rows_late, 5)
            root("tokens", 6, D)
            mod_copy(10, mod_rows_late, 1)
            shift("tokens", 0, 1)
            mod_copy(11, mod_rows_late, 7)

            def decay_exp(r):
                act.wait_ge(sem("decay_ready"), r + 1)
                d = decay[:, r % 2].rearrange("p d h t -> p (d h t)")
                fn(d, d, ACT.Exp).then_inc(sem("decay_exp"), 1)

            def taken(step):
                name, s = PROJ[step]
                b = 2 * (step % PAIRS) if step < EARLY else LATER_BANK[step - EARLY]
                if name == "ak":
                    act.wait_ge(sem("ak_product"), 1)
                else:
                    wait_done(act, FIRST["w_in"] + s)
                one, two = ps[:, b, :], ps[:, b:min(b + 2, 8), :]
                i = s % 2 if s < 12 else 0
                if name == "q":
                    last = fn(hg_q[:, 2 * s:2 * s + 2, :].rearrange("p a t -> p (a t)"), one, ACT.Copy)
                elif name in ("ff", "fb"):
                    key, log = (key_f, log_f) if name == "ff" else (key_b, log_b)
                    fn(key[:, 2 * i:2 * i + 2, :], two, ACT.Sigmoid, scale=-1.0)
                    last = fn(log[:, 2 * i:2 * i + 2, :], two, ACT.Sigmoid)
                elif name == "i":
                    last = fn(hg_v[:, :, 256 * i:256 * i + 256].rearrange("p (b t) c -> p b t c", b=2),
                              two.rearrange("p b (t c) -> p b t c", c=256), ACT.Copy)
                elif name == "g":
                    last = fn(hg_gate[:, 2 * i:2 * i + 2, :].rearrange("p a t -> p (a t)"), one, ACT.Silu)
                elif name == "aq":
                    last = fn(att_q[:, 2 * i:2 * i + 2, :].rearrange("p a t -> p (a t)"), one, ACT.Copy)
                elif name == "ak":
                    last = fn(att_k, two, ACT.Copy)
                elif name == "av":
                    last = fn(att_v.rearrange("p b c -> p (b c)"), one, ACT.Copy)
                else:
                    g, i = (gate_a, s - 13) if name == "ga" else (gate_b, s - 17)
                    last = fn(g[:, 2 * i:2 * i + 2, :].rearrange("p a t -> p (a t)"), one, ACT.Sigmoid)
                last.then_inc(sem("proj_taken"), 1)

            for step in range(EARLY):
                taken(step)
                if step == 5:
                    act.wait_ge(sem("proj_taken"), 6)
                    for dr, log in ((0, log_f), (1, log_b)):
                        for hd in range(HG_HEADS):
                            fn(log[:, hd, :], log[:, hd, :], ACT.Ln, bias=floor[:, 0, dr, hd:hd + 1],
                               scale=floor[:, 1, dr, hd:hd + 1]).then_inc(sem("forget_ready"), 1)
                if step >= ROUND_AT - 2 and step - (ROUND_AT - 2) < ROUNDS - 1:
                    decay_exp(step - (ROUND_AT - 2))

            act.wait_ge(sem("round_ready"), ROUND_WIDE)
            fn(q_dec[:, 0], pre_x[:, 0, :, 1:T + 1], ACT.Exp).then_inc(sem("q_dec_exp"), 1)
            act.wait_ge(sem("end_ready"), 1)
            fn(q_dec[:, 1], q_dec[:, 1], ACT.Exp).then_inc(sem("q_dec_exp"), 1)
            fn(key_dec[:, 0], key_dec[:, 0], ACT.Exp).then_inc(sem("key_dec_exp"), 1)
            fn(key_dec[:, 1], pre_c[:, 1, :, 0:T], ACT.Exp).then_inc(sem("key_dec_exp"), 1)
            taken(EARLY)
            act.wait_ge(sem("key_dec_turned"), 1)
            fn(key_dec_t.rearrange("p d s c -> p (d s c)"), banks(0, 4), ACT.Copy).then_inc(sem("key_dec_t_ready"), 1)
            act.wait_ge(sem("state_product"), 1)
            fn(state0.rearrange("p d h v -> p (d h v)"), banks(4, 2), ACT.Copy).then_inc(sem("state_ready"), 1)
            act.wait_ge(sem("round_scores"), ROUNDS)
            fn(att_sq[:, 0:4 * T], att_q.rearrange("p a t -> p (a t)"), ACT.Square)
            fn(att_sq[:, 4 * T:8 * T], att_k.rearrange("p a t -> p (a t)"), ACT.Square).then_inc(sem("att_sq_ready"), 1)
            act.wait_ge(sem("hg_out"), 1)
            act.wait_ge(sem("round_ready"), ROUNDS)
            fn(o_sq.rearrange("p a t -> p (a t)"), banks(0, 2), ACT.Square).then_inc(sem("hg_sq_ready"), 1)
            act.wait_ge(sem("hg_sumsq"), 1)
            o_flat = o_hg.rearrange("p a t -> p (a t)")
            fn(o_flat, banks(2, 2), ACT.Ln, bias=eps_col[:, 0:1], scale=1.0 / P).then_inc(sem("hg_log"), 1)
            act.wait_ge(sem("hg_log"), 1)
            fn(o_flat, o_flat, ACT.Exp, scale=-0.5).then_inc(sem("hg_rstd"), 1)
            act.wait_ge(sem("att_sumsq"), 1)
            fn(att_rinv, banks(4, 4), ACT.Ln, bias=eps_col[:, 0:1], scale=1.0 / ATT_HD).then_inc(sem("att_log"), 1)
            act.wait_ge(sem("att_log"), 1)
            fn(att_rinv, att_rinv, ACT.Exp, scale=-0.5).then_inc(sem("att_rstd"), 1)

            taken(EARLY + 1)
            taken(EARLY + 2)

            n_units = ATT_HEADS * TT

            def att_exp(u):
                act.wait_ge(sem("att_max"), u + 1)
                if u >= 2:
                    act.wait_ge(sem("att_p_turned"), u - 1)
                fn(att_p[:, u % 2, :], ps[:, u % 2, :], ACT.Exp, bias=att_stat[:, 0, u:u + 1], scale=ATT_SCALE,
                   accum_out=att_stat[:, 1, u:u + 1]).then_inc(sem("att_exp"), 1)

            def att_copy(u):
                act.wait_ge(sem("att_p_turned"), u + 1)
                if u >= 2:
                    act.wait_ge(sem("att_out"), u - 1)
                fn(att_pt[:, u % 2, :, :].rearrange("p k q -> p (k q)"), ps[:, 2 + u % 2, :], ACT.Copy
                   ).then_inc(sem("att_pt"), 1)

            for i in range(n_units + 1):
                if i < n_units:
                    att_exp(i)
                if i == LATER_UNIT + 1:
                    taken(EARLY + 3)
                if i >= 1:
                    att_copy(i - 1)
            act.wait_ge(sem("att_out"), n_units)
            fn(o_att.rearrange("p a t -> p (a t)"), banks(4, 2), ACT.Copy).then_inc(sem("o_att_ready"), 1)

            square_pieces("h_updated", 4 * 6)
            root("experts", 0, D)
            shift("experts", 0, 1, 3 * KD)
            act.wait_ge(sem("logits_ready"), 1)
            fn(aff_e.rearrange("p t e -> p (t e)"), aff_e.rearrange("p t e -> p (t e)"), ACT.Exp).then_inc(sem("aff_exp"), 1)
            act.wait_ge(sem("rows_back"), 1)
            fn(tok[:, :, :].rearrange("p t d -> p (t d)"), banks(4, 4), ACT.Copy).then_inc(sem("rows_copied"), 1)
            def pick_of(more, e):
                fn(pick_cur, picks[:, TT:2 * TT, e:, :][:, :, bass.ds(more, 1), :].rearrange("p k o c -> p k (o c)"),
                   ACT.Copy).then_inc(sem("pick_cur_ready"), 1)

            def rows_of(more, e):
                fn(x_cur, x_exp[:, :, e * CAP:][:, :, bass.ds(more * CAP, CAP)], ACT.Copy).then_inc(sem("x_cur_ready"), 1)

            def spread_of(more, e):
                act.wait_ge(sem("spread_turned"), more + (e + 1))
                fn(spread_cur[0:64, :], ps[0:64, 7, T:2 * T], ACT.Copy).then_inc(sem("spread_cur_ready"), 1)

            def expert(more, gathers=False, final=False):
                n = FIRST["experts"]
                wait_done(act, n + 3, more * 12)
                fn(half_g[0:64, :], ps[64:128, 4, :], ACT.Copy).then_inc(sem("half_g_ready"), 1)
                act.wait_ge(sem("gate_sum_ready"), more + 1)
                fn(gate_act[0:64, :], gate_sum[0:64, :], ACT.Silu).then_inc(sem("gate_act_ready"), 1)
                wait_done(act, n + 7, more * 12)
                fn(half_u[0:64, :], ps[64:128, 5, :], ACT.Copy).then_inc(sem("half_u_ready"), 1)
                if not final:
                    pick_of(more, 1)
                act.wait_ge(sem("hid_turned"), more + 1)
                fn(hid_t.rearrange("p (h c) s -> p h c s", h=2),
                   ps[:, 7, 0:256].rearrange("p (c h s) -> p h c s", c=4, h=2), ACT.Copy).then_inc(sem("hid_t_ready"), 1)
                if gathers:
                    for k in range(KD):
                        act.wait_ge(sem("x_exp_product"), 2 + k + 1)
                        fn(x_exp[:, k, FIRST_EXPERTS * CAP:], ps[:, 4 + k % 2, 0:(EXPERTS - FIRST_EXPERTS) * CAP], ACT.Copy
                           ).then_inc(sem("x_exp_taken"), 1)
                    act.wait_ge(sem("x_exp_taken"), 2 + KD)
                if not final:
                    rows_of(more, 1)
                wait_done(act, n + 11, more * 12)
                fn(half_y[0:64, :], ps[64:128, 6, :], ACT.Copy).then_inc(sem("half_y_ready"), 1)
                if not final:
                    act.wait_ge(sem("spread_free"), more + 1)
                    spread_of(more, 1)

            act.wait_ge(sem("pick_ready"), 2)
            pick_of(0, 0)
            for b in range(2):
                act.wait_ge(sem("x_exp_product"), b + 1)
                fn(x_exp[:, 4 * b:4 * b + 4, 0:FIRST_EXPERTS * CAP],
                   ps[:, 4 + b, :].rearrange("p (k c) -> p k c", k=4)[:, :, 0:FIRST_EXPERTS * CAP], ACT.Copy
                   ).then_inc(sem("x_exp_taken"), 1)
            act.wait_ge(sem("x_exp_taken"), 2)
            rows_of(0, 0)
            spread_of(0, 0)
            expert(0)
            expert(1, gathers=True)
            with act.Fori(2, EXPERTS - 1) as e:
                expert(e)
            expert(EXPERTS - 1, final=True)

            square_pieces("h_updated", 4 * 7)
            root("final2", 4, D)
            for i in range(2 * TT):
                g, t = i // TT, i % TT
                act.wait_ge(sem("out_turned"), i + 1)
                fn(tok[:, t, 512 * g:512 * g + 512], ps[:, 2 * t + g, :], ACT.Copy).then_inc(sem("rows_out"), 1)

        @block.gpsimd
        def _(pool):
            def taps(tile, between):
                j = POOL_TILES[tile]
                acc = conv_acc[:, j, :]
                for w in range(1, CONV_W):
                    pool.wait_ge(sem("tap_product_ready"), tile * CONV_W + w + 1)
                    if w > 1:
                        pool.wait_ge(sem("tap_added"), tile * (CONV_W - 1) + w - 1)
                    pool.tensor_tensor(acc, acc, tap_product[:, w % KD, :], ALU.add).then_inc(sem("tap_added"), 1)
                    if w in between:
                        scale_gate(between[w])

            def scale_gate(i):
                pool.wait_ge(sem("glu_sig_ready"), i + 1)
                sig = glu_sig[:, i % 2, :].rearrange("p (a t) -> p a t", t=T)
                pool.tensor_tensor(sig, sig, rstd[:, 0:T].unsqueeze(1).to_broadcast([P, 2, T]), ALU.mult
                                   ).then_inc(sem("glu_gate_ready"), 1)

            pool.wait_ge(sem("vectors_ready"), 1)
            scale_gate(0)
            taps(0, {6: 1, 14: 2, 22: 3})
            taps(1, {})
        @block.vector
        def _(dve):
            steps = [0]

            def step(ins):
                ins.then_inc(sem("dve_step"), 1)
                steps[0] += 1

            def settle():
                dve.wait_ge(sem("dve_step"), steps[0])

            x_in = xn[:, :, T:2 * T]

            dve.memset(cond_pad, 0.0).then_inc(sem("pad_cleared"), 1)
            step(dve.memset(zero_w[:, :], 0.0))
            dve.memset(eps_col[:, :], EPS).then_inc(sem("eps_set"), 1)
            dve.wait_ge(sem("first_gains_turned"), 1)
            dve.tensor_copy(vec_a[:, 0:ROWS_FIRST], ps[:, 0, 0:ROWS_FIRST]).then_inc(sem("gains_ready"), 1)

            def root(m, region=0):
                dve.wait_ge(sem("std_ready"), NORM[m])
                dve.reciprocal(rstd[:, region:region + T], std[:, region:region + T]).then_inc(sem("rstd_ready"), 1)
                dve.wait_ge(sem("rstd_ready"), NORM[m])

            def normed(m, dst, src, gain, region=0, rooted=False):
                if not rooted:
                    root(m, region)
                k_tiles = dst.shape[1]
                for k in range(k_tiles):
                    last = dve.scalar_tensor_tensor(dst[:, k, :], src[:, k, :], gain[:, k:k + 1],
                                                    rstd[:, region:region + T], ALU.mult, ALU.mult)
                    if m in NORM_PIECES and k % 2 == 1:
                        last.then_inc(sem("piece_normed"), 1)
                if m not in NORM_PIECES:
                    last.then_inc(sem("xn_ready"), 1)

            def x_lo(name):
                for g in range(4):
                    dve.wait_ge(sem("x_hi"), X_BEFORE[name] + g + 1)
                    hi, lo = (x_split[:, part, 2 * g:2 * g + 2, :] for part in range(2))
                    dve.tensor_tensor(lo, x_in[:, 2 * g:2 * g + 2, :], hi.bitcast(F32), ALU.subtract
                                      ).then_inc(sem("x_split_ready"), 1)

            def split_lo(n, o, columns=True, more_halves=0):
                dve.wait_ge(sem("half_hi"), HALF[n] + o + 1 + more_halves)
                if o == 1 and n >= 1 and n - 1 not in HALF:
                    dve.wait_ge(slot_free, n)
                ins = dve.tensor_tensor(half_part(n, o, 1), half_slot(n, o, columns), half_part(n, o, 0).bitcast(F32),
                                        ALU.subtract)
                ins.then_inc(sem("half_split") if o == 0 else slot_free, 1)

            def split_lo_slot(n, columns=True):
                for o in range(2):
                    split_lo(n, o, columns)

            def gains(name, layer=0):
                return vec_a[:, ROWS_A[name] + KD * layer:ROWS_A[name] + KD * layer + KD]

            def update(factor, after, slots=None, f=None, los_last=False):
                def lo(piece):
                    dve.wait_ge(sem("x_hi"), X_BEFORE[after[0]] + piece + 1)
                    for k in (2 * piece, 2 * piece + 1):
                        ins = dve.scalar_tensor_tensor(x_split[:, 1, k, :], h[:, k, :], after[1][:, k:k + 1],
                                                       x_split[:, 0, k, :].bitcast(F32), ALU.mult, ALU.subtract)
                    ins.then_inc(sem("x_split_ready"), 1)

                for piece in range(4):
                    if factor is not None:
                        if slots is not None:
                            wait_done(dve, slots + piece)
                        elif piece < 3:
                            dve.wait_ge(sem("ffn_out"), 3 * f + piece + 1)
                        else:
                            wait_done(dve, FIRST[f"ffn{f}"] + 32)
                        hp = h[:, 2 * piece:2 * piece + 2, :].rearrange("p k t -> p (k t)")
                        dve.scalar_tensor_tensor(hp, ps[:, piece, :], factor, hp, ALU.mult, ALU.add
                                                 ).then_inc(sem("h_updated"), 1)
                    if after is not None and piece >= 1 and not los_last:
                        lo(piece - 1)
                if after is not None:
                    for piece in range(0 if los_last else 3, 4):
                        lo(piece)

            def ffn(f, after_slot=None, after=None):
                n0 = FIRST[f"ffn{f}"]
                done = FF_STEPS * f
                split_lo_slot(n0 + 1)
                root(f"ffn{f}")
                scale = rstd[:, 0:T].unsqueeze(1).to_broadcast([P, 2, T])

                def scaled(c, dst, bank):
                    return dve.tensor_tensor(dst, ps[:, bank + c % 2, :].rearrange("p (k t) -> p k t", t=T), scale, ALU.mult)

                def gate(n, c, more_halves, more):
                    wait_done(dve, n, more_halves)
                    scaled(c, silu_gate[:, c % 2, :].rearrange("p (k t) -> p k t", t=T), 4
                           ).then_inc(sem("gate_scaled"), 1)

                def combine(n, c, more_halves, more):
                    wait_done(dve, n, more_halves)
                    scaled(c, hidden[:, c % 2, :, :], 6).then_inc(sem("up_scaled"), 1)
                    dve.wait_ge(sem("up_scaled"), done + c + 1 + more)
                    dve.wait_ge(sem("silu_ready"), done + c + 1 + more)
                    flat = hidden[:, c % 2, :, :].rearrange("p k t -> p (k t)")
                    dve.tensor_tensor(flat, silu_gate[:, c % 2, :], flat, ALU.mult).then_inc(sem("hidden_ready"), 1)
                    dve.wait_ge(sem("hid_hi"), done + c + 1 + more)
                    dve.tensor_tensor(hid_split[:, c % 2, 1, :, :], hidden[:, c % 2, :, :],
                                      hid_split[:, c % 2, 0, :, :].bitcast(F32), ALU.subtract
                                      ).then_inc(sem("hid_split_ready"), 1)

                gate(n0, 0, 0, 0)
                with dve.Fori(0, FF_STEPS // 2) as i:
                    for j in range(2):
                        n = n0 + 2 + 3 * j
                        for s in range(3):
                            for o in range(2):
                                split_lo(n + s, o, s < 2, 12 * i)
                            if s == 0:
                                combine(n - 1 - (j > 0), j, 12 * i, 2 * i)
                        gate(n, 1 + j, 12 * i, 2 * i)
                split_lo_slot(n0 + 32, columns=False)
                combine(n0 + 30, FF_STEPS - 1, 0, 0)
                if after_slot is not None:
                    split_lo_slot(after_slot)
                update(0.5, after, f=f)

            split_lo_slot(FIRST["ffn0"])
            update(None, ("ffn0", gains("ffn_norm1", 0)))
            ffn(0, after_slot=FIRST["pw1"], after=("pw1", gains("mix_norm", 0)))

            dve.wait_ge(sem("h_updated"), 4 * 1)
            split_lo_slot(FIRST["pw1"] + 1)
            root("conv_in")
            dve.wait_ge(sem("rows_turned"), 1)
            step(dve.tensor_copy(vec_b[:, :], ps[:, 5, 0:N_ROWS_B]))
            step(dve.tensor_copy(vec_a[:, ROWS_FIRST:N_ROWS_A], ps[:, 5, N_ROWS_B + ROWS_FIRST:N_ROWS_B + N_ROWS_A]))
            dve.tensor_copy(w_dw[:, :, :].rearrange("p k w -> p (k w)"), ps[:, 6, 0:KD * CONV_W]
                            ).then_inc(sem("vectors_ready"), 1)
            dve.wait_ge(sem("masks_in"), 16)
            step(dve.tensor_copy(mask[:, :, :], mask_in))
            settle()
            step(dve.memset(conv_in[:, :, 0:PAD], 0.0))
            split_lo_slot(FIRST["pw1"] + 2)
            split_lo_slot(FIRST["pw1"] + 3)
            tap_done = {}

            def glu(pair):
                dve.wait_ge(sem("glu_gate_ready"), pair + 1)
                dve.tensor_tensor(conv_in[:, 2 * pair:2 * pair + 2, PAD:PAD + T],
                                  ps[:, (2 * pair) % 4, :].rearrange("p (a t) -> p a t", t=T),
                                  glu_sig[:, pair % 2, :].rearrange("p (a t) -> p a t", t=T), ALU.mult
                                  ).then_inc(sem("glu_ready"), 1)

            def glu_gate(pair):
                wait_done(dve, FIRST["pw1"] + 2 * pair + 1)
                dve.tensor_tensor(glu_sig[:, pair % 2, :].rearrange("p (a t) -> p a t", t=T),
                                  ps[:, (2 * pair + 1) % 4, :].rearrange("p (a t) -> p a t", t=T),
                                  rstd[:, 0:T].unsqueeze(1).to_broadcast([P, 2, T]), ALU.mult
                                  ).then_inc(sem("glu_gate_scaled"), 1)

            def taps(*runs):
                for i in range(max(last - first for j, first, last in runs)):
                    for j, first, last in runs:
                        w = first + i
                        if w >= last:
                            continue
                        u, acc = conv_in[:, j, w:w + T], conv_acc[:, j, :]
                        if w == 0:
                            dve.wait_ge(sem("vectors_ready"), 1)
                            dve.wait_ge(sem("glu_ready"), j // 2 + 1)
                            settle()
                            step(dve.tensor_scalar(acc, u, w_dw[:, j, 0:1], None, ALU.mult))
                            tap_done[j] = steps[0]
                            continue
                        dve.wait_ge(sem("dve_step"), tap_done[j])
                        ins = dve.scalar_tensor_tensor(acc, u, w_dw[:, j, w:w + 1], acc, ALU.mult, ALU.add)
                        if w < CONV_W - 1:
                            step(ins)
                            tap_done[j] = steps[0]
                        else:
                            ins.then_inc(sem("conv_done"), 1)

            glu_gate(0)
            split_lo_slot(FIRST["pw1"] + 4)
            glu(0)
            taps((1, 0, 8))
            split_lo_slot(FIRST["pw1"] + 5)
            glu_gate(1)
            taps((1, 8, 16))
            glu(1)
            split_lo_slot(FIRST["pw1"] + 6)
            taps((1, 16, 20), (2, 0, 4))
            split_lo_slot(FIRST["pw1"] + 7)
            glu_gate(2)
            taps((1, 20, 24), (2, 4, 8))
            glu(2)
            taps((1, 24, 30), (2, 8, 14))
            glu_gate(3)
            taps((1, 30, CONV_W), (2, 14, 20), (3, 0, 6))
            glu(3)
            taps((2, 20, CONV_W), (3, 6, 17), (6, 0, 11))
            taps((3, 17, CONV_W), (6, 11, 25))
            taps((6, 25, CONV_W))
            root("context", T)
            split_lo_slot(FIRST["pw2"])
            normed("conv_out", x_in, conv_acc, gains("conv_norm"))
            x_lo("pw2")
            split_lo_slot(FIRST["pw2"] + 1)
            split_lo_slot(FIRST["pw2"] + 2)
            split_lo_slot(FIRST["pw2"] + 3)
            r = ROWS_B["hg_lb_logits_2"]
            lg = vec_b[:, r:r + 16].rearrange("p (d l h) -> p l d h", d=2, l=2)
            a, b, m = (lb_tmp[:, i] for i in range(3))
            step(dve.tensor_tensor(m, lg[:, 0], lg[:, 1], ALU.max))
            settle()
            step(dve.tensor_tensor(a, lg[:, 0], m, ALU.subtract))
            dve.tensor_tensor(b, lg[:, 1], m, ALU.subtract).then_inc(sem("floor_logits"), 1)
            dve.wait_ge(sem("floor_exp"), 1)
            step(dve.tensor_tensor(m, a, b, ALU.add))
            settle()
            step(dve.reciprocal(m, m))
            settle()
            step(dve.tensor_tensor(floor[:, 0], a, m, ALU.mult))
            settle()
            step(dve.tensor_scalar(floor[:, 1], floor[:, 0], -1.0, 1.0, ALU.mult, ALU.add))
            def mod_take(first, n, bank, column):
                dve.wait_ge(sem("mod_turned"), first + n)
                row = ROWS_B["b_mod_2"] + 4 * first
                return dve.tensor_tensor(mod[:, 4 * first:4 * (first + n), :],
                                         ps[:, bank, column:column + 8 * n].rearrange("p (f c) -> p f c", c=2),
                                         vec_b[:, row:row + 4 * n].unsqueeze(2).to_broadcast([P, 4 * n, 2]), ALU.add)

            def mod_gain(i, first, c, g):
                return dve.scalar_tensor_tensor(gain_mod[:, i, :], mod[:, first:first + KD, c], 1.0,
                                                vec_b[:, ROWS_B[g]:ROWS_B[g] + KD], ALU.add, ALU.mult)

            step(mod_take(0, MOD_EARLY, 4, T))
            settle()
            for c in range(2):
                mod_gain(c, KD, c, "norm1_g_2").then_inc(sem("mod_ready"), 1)
            dve.wait_ge(sem("mod_ready"), 2)
            dve.wait_ge(sem("ctx_copied"), 1)
            normed("context", xn[:, :, 0:T], xn[:, :, 0:T], gain_mod[:, 1, :], region=T, rooted=True)
            split_lo_slot(FIRST["ffn1"])
            update(1.0, ("ffn1", gains("ffn_norm2", 0)), FIRST["pw2"], los_last=True)
            ffn(1, after_slot=FIRST["ffn2"], after=("ffn2", gains("ffn_norm1", 1)))
            ffn(2)

            dve.wait_ge(sem("positions_in"), 16)
            step(dve.tensor_copy(pos_f, pos_i[:, :]))
            settle()
            step(dve.tensor_scalar(ang, pos_f, const("inv_freq"), None, ALU.mult))
            settle()
            step(dve.tensor_scalar(turns, ang, 1.0 / TWO_PI, ROUND_MAGIC, ALU.mult, ALU.add))
            settle()
            step(dve.tensor_scalar(turns, turns, ROUND_MAGIC, None, ALU.subtract))
            for part in (PI_A, PI_B, PI_C):
                settle()
                step(dve.scalar_tensor_tensor(ang, turns, -part, ang, ALU.mult, ALU.add))
            settle()
            step(dve.tensor_scalar(turns, ang, TWO_PI / 4, -TWO_PI, ALU.is_gt, ALU.mult))
            settle()
            step(dve.scalar_tensor_tensor(turns, ang, TWO_PI / 4, turns, ALU.add, ALU.add))
            settle()
            step(dve.tensor_scalar(turns, turns, PI_LIMIT, -PI_LIMIT, ALU.min, ALU.max))
            dve.tensor_scalar(ang, ang, PI_LIMIT, -PI_LIMIT, ALU.min, ALU.max).then_inc(sem("angles_ready"), 1)
            dve.wait_ge(sem("h_updated"), 4 * 4)
            normed("mla", x_in, h[:, :, :], gains("mix_norm", 1))
            mod_take(6, 1, 7, 0).then_inc(sem("mod_taken"), 1)
            latent_ps = banks(0, 3).rearrange("p (k t) -> p k t", t=T)
            r = ROWS_A["mla_q_norm"]
            normed("mla_q", latent_n[:, 0:4, :], latent_ps[:, 0:4, :], vec_a[:, r:r + 4])
            mod_take(7, 1, 6, 0).then_inc(sem("mod_taken"), 1)
            normed("mla_kv", latent_n[:, 4:6, :], latent_ps[:, 4:6, :], vec_a[:, r + 4:r + 6], region=T)
            dve.wait_ge(sem("trig_ready"), 2)
            dve.wait_ge(sem("uq_taken"), 4)
            for a in range(5):
                last = dve.tensor_tensor(rope_a[:, a, :], rope_in[:, a, :], cos_t, ALU.mult)
            step(last)
            dve.wait_ge(sem("rope_turned"), 1)
            turned = banks(5, 3)[:, 0:5 * T].rearrange("p (a t) -> p a t", t=T)
            step(dve.tensor_tensor(rope_b, turned, sin_t.unsqueeze(1).to_broadcast([P, 5, T]), ALU.mult))
            settle()
            dve.tensor_tensor(rope_a, rope_a, rope_b, ALU.add).then_inc(sem("rope_ready"), 1)
            mod_take(8, 1, 1, 0).then_inc(sem("mod_taken"), 1)

            def mla_max(hd):
                dve.wait_ge(sem("mla_scores"), hd + 1)
                for t in range(TT):
                    a, b = (0, P) if t == 0 else (P, 3 * P)
                    step(dve.tensor_reduce(mla_stat[:, 2, hd, t:t + 1], ps[:, hd % 2, a:b], AX_X, ALU.max))
                settle()
                dve.tensor_scalar(mla_stat[:, 0, hd, :], mla_stat[:, 2, hd, :], -MLA_SCALE, None, ALU.mult
                                  ).then_inc(sem("mla_max"), 1)

            def mla_norm(hd):
                dve.wait_ge(sem("mla_exp"), 2 * hd + 2)
                step(dve.reciprocal(mla_stat[:, 3, hd, :], mla_stat[:, 1, hd, :]))
                settle()
                for t in range(TT):
                    a, b = (0, P) if t == 0 else (P, 3 * P)
                    last = dve.tensor_scalar(mla_p[:, hd % 2, a:b], mla_p[:, hd % 2, a:b], mla_stat[:, 3, hd, t:t + 1],
                                             None, ALU.mult)
                last.then_inc(sem("mla_p"), 1)

            def mla_take(hd):
                dve.wait_ge(sem("mla_out"), hd + 1)
                dve.tensor_copy(o_mla[:, hd, :], ps[:, 4 + hd % 2, 0:T]).then_inc(sem("mla_out_taken"), 1)

            for i in range(MLA_HEADS + 2):
                if i < MLA_HEADS:
                    mla_max(i)
                if i < MLA_HEADS:
                    mla_norm(i)
                if i >= 2:
                    mla_take(i - 2)
            split_lo(FIRST["ffn3"], 0)
            update(1.0, ("ffn3", gains("ffn_norm2", 1)), FIRST["mla_o"])
            split_lo(FIRST["ffn3"], 1)
            ffn(3)

            dve.wait_ge(sem("h_updated"), 4 * 6)
            root("final1")
            for k in range(KD):
                ins = dve.scalar_tensor_tensor(h[:, k, :], h[:, k, :], gains("final_norm")[:, k:k + 1], rstd[:, 0:T],
                                               ALU.mult, ALU.mult)
                if k % 2 == 1:
                    ins.then_inc(sem("h_normed"), 1)
            dve.wait_ge(sem("h_normed"), 4)
            normed("tokens", x_in, h[:, :, :], gain_mod[:, 0, :])
            mod_take(9, 1, 2, 0).then_inc(sem("mod_taken"), 1)
            mod_take(10, 1, 3, 0).then_inc(sem("mod_taken"), 1)
            dve.wait_ge(sem("mod_taken"), 4)
            step(mod_gain(2, 4 * KD, 0, "norm2_g_2"))
            mod_take(11, 1, 6, 0).then_inc(sem("mod_taken"), 1)

            step(dve.memset(pre_x[:, :, :, 0:1], 0.0))
            step(dve.memset(pre_c[:, :, :, 0:1], 0.0))
            for dr, (key, log) in enumerate(((key_f, log_f), (key_b, log_b))):
                dve.wait_ge(sem("proj_taken"), 4 + 2 * dr)
                for hd in range(HG_HEADS):
                    step(dve.tensor_scalar(key[:, hd, :], key[:, hd, :], floor[:, 1, dr, hd:hd + 1], None, ALU.mult))
            for dr, log in enumerate((log_f, log_b)):
                for hd in range(HG_HEADS):
                    dve.wait_ge(sem("forget_ready"), HG_HEADS * dr + hd + 1)
                    step(dve.tensor_tensor_scan(pre_c[:, dr, hd, 1:T + 1], ones, log[:, hd, 0:T], 0.0, ALU.mult, ALU.add))
                    step(dve.tensor_tensor_scan(pre_x[:, dr, hd, 1:T + 1], ones, log[:, hd, T:2 * T], 0.0, ALU.mult, ALU.add))
            settle()

            def halves(a, h_):
                v = a.rearrange("p h (n two w) -> p h n two w", two=2, w=h_)
                return v[:, :, :, 0, :], v[:, :, :, 1, :]

            half_of = LEVELS + [P]

            def decay_args(r_):
                h_ = half_of[r_]
                n = T // (2 * h_)
                for dr in range(2):
                    run = pre_x[:, dr, :, 1 - dr:1 - dr + T]
                    left, right = halves(run, h_)
                    d_left, d_right = halves(decay[:, r_ % 2, dr], h_)
                    mid = pre_x[:, dr, :, 0:T].rearrange("p h (n two w) -> p h n two w", two=2, w=h_)[:, :, :, 1, 0:1]
                    mid = mid.to_broadcast([P, HG_HEADS, n, h_])
                    dve.tensor_tensor(d_left, mid, left, ALU.subtract)
                    last = dve.tensor_tensor(d_right, right, mid, ALU.subtract)
                last.then_inc(sem("decay_ready"), 1)

            def decayed(r_):
                if r_ >= 2:
                    dve.wait_ge(sem("round_scores"), r_ - 1)
                q_out, k_out = q_lvl[:, r_ % 2], k_lvl[:, r_ % 2]
                if r_ == ROUND_DIAG:
                    dve.tensor_tensor(k_out, key_f[:, :, T:2 * T], key_b[:, :, T:2 * T], ALU.add
                                      ).then_inc(sem("round_ready"), 1)
                    return
                dve.wait_ge(sem("decay_exp"), r_ + 1)
                h_ = half_of[r_]
                q_l, q_r = halves(q_out, h_)
                k_l, k_r = halves(k_out, h_)
                src_l, src_r = halves(hg_q, h_)
                kf_l, _ = halves(key_f[:, :, T:2 * T], h_)
                _, kb_r = halves(key_b[:, :, T:2 * T], h_)
                f_l, f_r = halves(decay[:, r_ % 2, 0], h_)
                b_l, b_r = halves(decay[:, r_ % 2, 1], h_)
                dve.tensor_tensor(q_r, src_r, f_r, ALU.mult)
                dve.tensor_tensor(q_l, src_l, b_l, ALU.mult)
                dve.tensor_tensor(k_l, kf_l, f_l, ALU.mult)
                dve.tensor_tensor(k_r, kb_r, b_r, ALU.mult).then_inc(sem("round_ready"), 1)

            def take_scores(r_):
                dve.wait_ge(sem("round_scores"), r_ + 1)
                for s in range(TT):
                    t = 1 - s if r_ == ROUND_WIDE else s
                    o = hg_p[:, s, :, t * P:t * P + P]
                    data = ps[:, 6 + s, :].rearrange("p (h t) -> p h t", h=HG_HEADS)
                    if r_ == ROUND_WIDE:
                        last = dve.tensor_copy(o, data)
                    else:
                        m_ = mask[:, r_ if r_ < ROUND_WIDE else len(LEVELS), :].unsqueeze(1).to_broadcast([P, HG_HEADS, P])
                        last = dve.copy_predicated(o, m_, data)
                last.then_inc(sem("round_taken"), 1)

            dve.wait_ge(sem("mod_turned"), MOD_CHUNKS)
            step(dve.memset(tok[:, :, :].rearrange("p t d -> p (t d)"), 0.0))
            decay_args(0)
            decay_args(1)
            for r_ in range(ROUNDS):
                decayed(r_)
                if r_ + 2 < ROUNDS - 1:
                    dve.wait_ge(sem("round_ready"), r_ + 1)
                    decay_args(r_ + 2)
                if r_ >= 1:
                    if r_ == 1:
                        settle()
                    take_scores(r_ - 1)
            take_scores(ROUNDS - 1)
            wait_done(dve, FIRST["w_in"] + 12)
            dve.tensor_tensor(q_dec[:, 1], pre_x[:, 1, :, T:T + 1].to_broadcast([P, HG_HEADS, T]), pre_x[:, 1, :, 0:T],
                              ALU.subtract)
            dve.tensor_tensor(key_dec[:, 0], pre_c[:, 0, :, T:T + 1].to_broadcast([P, HG_HEADS, T]), pre_c[:, 0, :, 1:T + 1],
                              ALU.subtract).then_inc(sem("end_ready"), 1)
            dve.wait_ge(sem("key_dec_exp"), 2)
            dve.tensor_tensor(key_dec[:, 0], key_dec[:, 0], key_f[:, :, 0:T], ALU.mult)
            dve.tensor_tensor(key_dec[:, 1], key_dec[:, 1], key_b[:, :, 0:T], ALU.mult).then_inc(sem("key_dec_ready"), 1)
            dve.wait_ge(sem("q_dec_exp"), 2)
            for dr in range(2):
                last = dve.tensor_tensor(q_dec[:, dr], q_dec[:, dr], hg_q, ALU.mult)
            last.then_inc(sem("q_dec_ready"), 1)
            dve.wait_ge(sem("hg_rstd"), 1)
            step(dve.tensor_tensor(o_sq, o_hg, hg_gate, ALU.mult))
            settle()
            r = ROWS_B["hg_norm_g_2"]
            for hd in range(HG_HEADS):
                last = dve.scalar_tensor_tensor(o_hg[:, hd, :], ps[:, hd // 2, (hd % 2) * T:(hd % 2) * T + T],
                                                vec_b[:, r + hd:r + hd + 1], o_sq[:, hd, :], ALU.mult, ALU.mult)
            last.then_inc(sem("hg_normed"), 1)

            dve.wait_ge(sem("att_rstd"), 1)
            dve.wait_ge(sem("gains_in"), 64)
            qf, kf = att_qr.rearrange("p a t -> p (a t)"), att_kr.rearrange("p a t -> p (a t)")
            dve.wait_ge(sem("key_dec_ready"), 1)
            dve.scalar_tensor_tensor(qf, att_q.rearrange("p a t -> p (a t)"), qk_gain[:, 0:1], att_rinv[:, 0:4 * T],
                                     ALU.mult, ALU.mult)
            dve.scalar_tensor_tensor(kf, att_k.rearrange("p a t -> p (a t)"), qk_gain[:, 1:2], att_rinv[:, 4 * T:8 * T],
                                     ALU.mult, ALU.mult).then_inc(sem("att_n_ready"), 1)
            dve.wait_ge(sem("att_turned"), 1)
            cos_q = const("axial_cos").unsqueeze(1).to_broadcast([P, 4, T])
            sin_q = const("axial_sin").unsqueeze(1).to_broadcast([P, 4, T])
            cos_k = const("axial_cos").unsqueeze(1).to_broadcast([P, ATT_KV, T])
            sin_k = const("axial_sin").unsqueeze(1).to_broadcast([P, ATT_KV, T])
            rot = att_rot.rearrange("p (a t) -> p a t", t=T)
            sq = att_sq.rearrange("p (a t) -> p a t", t=T)
            dve.wait_ge(sem("att_n_ready"), 1)
            step(dve.tensor_tensor(rot[:, 0:4, :], att_qr, cos_q, ALU.mult))
            step(dve.tensor_tensor(rot[:, 4:6, :], att_kr[:, :, T:2 * T], cos_k, ALU.mult))
            step(dve.tensor_tensor(sq[:, 0:4, :], banks(4, 2).rearrange("p (a t) -> p a t", t=T), sin_q, ALU.mult))
            step(dve.tensor_tensor(sq[:, 4:6, :], banks(6, 1).rearrange("p (a t) -> p a t", t=T), sin_k, ALU.mult))
            settle()
            dve.tensor_tensor(att_qr, rot[:, 0:4, :], sq[:, 0:4, :], ALU.add)
            dve.tensor_tensor(att_kr[:, :, T:2 * T], rot[:, 4:6, :], sq[:, 4:6, :], ALU.add).then_inc(sem("att_ready"), 1)

            def att_max(u):
                dve.wait_ge(sem("att_scores"), u + 1)
                step(dve.tensor_reduce(att_stat[:, 2, u:u + 1], ps[:, u % 2, :], AX_X, ALU.max))
                settle()
                dve.tensor_scalar(att_stat[:, 0, u:u + 1], att_stat[:, 2, u:u + 1], -ATT_SCALE, None, ALU.mult
                                  ).then_inc(sem("att_max"), 1)

            def att_norm(u):
                dve.wait_ge(sem("att_exp"), u + 1)
                step(dve.reciprocal(att_stat[:, 3, u:u + 1], att_stat[:, 1, u:u + 1]))
                settle()
                dve.tensor_scalar(att_p[:, u % 2, :], att_p[:, u % 2, :], att_stat[:, 3, u:u + 1], None, ALU.mult
                                  ).then_inc(sem("att_p"), 1)

            for u in range(ATT_HEADS * TT):
                att_max(u)
                att_norm(u)

            for br, gate in ((0, gate_a), (1, gate_b)):
                for j in range(2):
                    wait_done(dve, FIRST["branch"] + 2 * br + j)
                    o = (merged if br == 0 else gate_b)[:, 4 * j:4 * j + 4, :]
                    dve.tensor_tensor(o, banks(2 * j, 2).rearrange("p (a t) -> p a t", t=T), gate[:, 4 * j:4 * j + 4, :],
                                      ALU.mult).then_inc(sem("branch_taken"), 1)
                    if br == 1:
                        dve.wait_ge(sem("branch_taken"), 2 + j + 1)
                        m = merged[:, 4 * j:4 * j + 4, :]
                        dve.tensor_tensor(m, m, o, ALU.add).then_inc(sem("merged_ready"), 1)
            for k in range(KD):
                if k % 2 == 0:
                    wait_done(dve, FIRST["w_out"] + k // 2)
                last = dve.scalar_tensor_tensor(h[:, k, :], ps[:, 4 + k // 2, (k % 2) * T:(k % 2) * T + T],
                                                mod[:, 2 * KD + k, 0:1], h[:, k, :], ALU.mult, ALU.add)
                if k % 2 == 1:
                    last.then_inc(sem("h_updated"), 1)

            dve.wait_ge(sem("h_updated"), 4 * 7)
            normed("experts", x_in, h[:, :, :], gain_mod[:, 2, :])
            dve.wait_ge(sem("router_scores"), 1)
            scores = ps[:, 1, 0:TT * EXPERTS].rearrange("p (t e) -> p t e", t=TT)
            step(dve.tensor_reduce(small[:, 8:10], scores, AX_X, ALU.max))
            settle()
            dve.tensor_tensor(aff_e, scores, small[:, 8:10].unsqueeze(2).to_broadcast([P, TT, EXPERTS]), ALU.subtract
                              ).then_inc(sem("logits_ready"), 1)
            dve.wait_ge(sem("aff_exp"), 1)
            step(dve.tensor_reduce(small[:, 10:12], aff_e, AX_X, ALU.add))
            settle()
            step(dve.reciprocal(small[:, 12:14], small[:, 10:12]))
            settle()
            dve.tensor_tensor(aff, aff_e, small[:, 12:14].unsqueeze(2).to_broadcast([P, TT, EXPERTS]), ALU.mult
                              ).then_inc(sem("aff_ready"), 1)
            dve.wait_ge(sem("aff_turned"), 1)
            E16 = slice(0, EXPERTS)
            step(dve.tensor_copy(aff_t[E16, :], ps[E16, 0, 0:T]))
            src, other = aff_t, (work_a, work_b)
            for i in range(CAP // 8):
                settle()
                step(dve.max(top8[E16, :], src[E16, :]))
                settle()
                dst = other[i % 2]
                step(dve.match_replace(dst[E16, :], top8[E16, :], src[E16, :], -1.0))
                src = dst
            settle()
            step(dve.tensor_scalar(chosen[E16, :], src[E16, :], 0.0, None, ALU.is_lt))
            settle()
            step(dve.tensor_tensor_scan(slot_t[E16, :], ones[E16, :], chosen[E16, :], 0.0, ALU.mult, ALU.add))
            settle()
            dve.tensor_tensor(slot_t[E16, :], slot_t[E16, :], chosen[E16, :], ALU.mult).then_inc(sem("slots_chosen"), 1)
            dve.wait_ge(sem("slots_turned"), 1)
            step(dve.tensor_copy(slot_tok.rearrange("p t e -> p (t e)"), ps[:, 1, 0:TT * EXPERTS]))
            settle()
            iota = const("iota").unsqueeze(1).to_broadcast([P, EXPERTS, CAP])
            for t in range(TT):
                last = dve.tensor_tensor(picks[:, t, 0:EXPERTS, :], iota,
                                         slot_tok[:, t, :].unsqueeze(2).to_broadcast([P, EXPERTS, CAP]), ALU.is_equal)
            last.then_inc(sem("pick_ready"), 1)
            dve.wait_ge(sem("pick_ready"), 1)
            for t in range(TT):
                last = dve.tensor_tensor(picks[:, TT + t, 0:EXPERTS, :], picks[:, t, 0:EXPERTS, :],
                                         aff[:, t, :].unsqueeze(2).to_broadcast([P, EXPERTS, CAP]), ALU.mult)
            last.then_inc(sem("pick_ready"), 1)

            with dve.Fori(0, EXPERTS) as e:
                dve.wait_ge(sem("half_g_ready"), e + 1)
                dve.tensor_tensor(gate_sum[0:64, :], ps[0:64, 4, :], half_g[0:64, :], ALU.add
                                  ).then_inc(sem("gate_sum_ready"), 1)
                dve.wait_ge(sem("half_u_ready"), e + 1)
                dve.tensor_tensor(up_sum[0:64, :], ps[0:64, 5, :], half_u[0:64, :], ALU.add).then_inc(sem("up_sum_ready"), 1)
                dve.wait_ge(sem("up_sum_ready"), e + 1)
                dve.wait_ge(sem("gate_act_ready"), e + 1)
                dve.tensor_tensor(hid_e[0:64, :], gate_act[0:64, :], up_sum[0:64, :], ALU.mult).then_inc(sem("hid_ready"), 1)
                dve.wait_ge(sem("half_y_ready"), e + 1)
                dve.tensor_tensor(y_e[0:64, :], ps[0:64, 6, :], half_y[0:64, :], ALU.add).then_inc(sem("y_ready"), 1)
            for k in range(KD):
                if k % 2 == 0:
                    dve.wait_ge(sem("moe_out"), k // 2 + 1)
                last = dve.scalar_tensor_tensor(h[:, k, :], ps[:, k // 2, (k % 2) * T:(k % 2) * T + T],
                                                mod[:, 5 * KD + k, 0:1], h[:, k, :], ALU.mult, ALU.add)
                if k % 2 == 1:
                    last.then_inc(sem("h_updated"), 1)
            dve.wait_ge(sem("h_updated"), 4 * 8)
            r = ROWS_B["final_norm_g_2"]
            normed("final2", x_in, h[:, :, :], vec_b[:, r:r + KD])


_INS = ['x', 'positions', 'ffn_norm1', 'ffn1_w1', 'ffn1_w3', 'ffn1_w2', 'mix_norm', 'ffn_norm2', 'ffn2_w1', 'ffn2_w3',
        'ffn2_w2', 'conv_w_pw1', 'conv_w_dw', 'conv_norm', 'conv_w_pw2', 'mla_w_a', 'mla_q_norm', 'mla_kv_norm',
        'mla_w_uq', 'mla_w_ukv', 'mla_w_o', 'final_norm', 'c_2', 'ctx_2', 'c_ctx_2', 'w_mod_2', 'b_mod_2', 'norm1_g_2',
        'norm2_g_2', 'w_in_2', 'hg_lb_logits_2', 'hg_norm_g_2', 'q_norm_g_2', 'k_norm_g_2', 'w_branch_a_2',
        'w_branch_b_2', 'w_out_2', 'w_router_2', 'w_exp_gate_2', 'w_exp_up_2', 'w_exp_down_2', 'final_norm_g_2']
_OUT = (1, T, D)


def kernel(**inputs):
    import concourse.bacc as bacc
    from concourse.bass_utils import run_bass_kernel_spmd

    nc = bacc.Bacc("TRN2", target_bir_lowering=False, num_devices=1)
    arrays = {f"in_{name}": np.ascontiguousarray(inputs[name]) for name in _INS}
    arrays["in_constants"], arrays["in_masks"] = CONSTANTS, MASKS
    args = [nc.dram_tensor(name, a.shape, mybir.dt.from_np(a.dtype), kind="ExternalInput").ap()
            for name, a in arrays.items()]
    args.append(nc.dram_tensor("out_0", _OUT, F32, kind="ExternalOutput").ap())
    build(nc, *args)
    r = run_bass_kernel_spmd(nc, [arrays], core_ids=[0])
    return r.results[0]["out_0"]
```
